# Optimizing a Trainium2 kernel written in Bass

```python
import jax, jax.numpy as jnp
from jax import lax
import numpy as np

D_MODEL = 1024
BATCH = 1
SEQ = 1024
DEPTH = 1

HEAD_DIM = 64
FOX_HEADS = 8
DIL_GROUPS = ((128, 1), (512, 4), (2048, 16))
DIL_HEADS_PER_GROUP = 4
N_DIL_GROUPS = len(DIL_GROUPS)
DIL_HEADS = N_DIL_GROUPS * DIL_HEADS_PER_GROUP
QK_HEADS = FOX_HEADS + DIL_HEADS
FOX_WIDTH = FOX_HEADS * HEAD_DIM
DIL_WIDTH = DIL_HEADS * HEAD_DIM
DIL_OUT_WIDTH = DIL_HEADS_PER_GROUP * HEAD_DIM
Q_BLOCK = 128
NUM_BUCKETS = 32
REL_MAX_DISTANCE = 2048
N_GROUPS = 4
EXPERTS_PER_GROUP = 8
N_EXPERTS = N_GROUPS * EXPERTS_PER_GROUP
TOP_K_IN_GROUP = 2
EXPERT_HIDDEN = D_MODEL // 2
MOE_BLOCK = 128
EPS = 1e-6

OFF_FOX_Q = 0
OFF_FOX_K = OFF_FOX_Q + FOX_WIDTH
OFF_FOX_V = OFF_FOX_K + FOX_WIDTH
OFF_FOX_F = OFF_FOX_V + FOX_WIDTH
OFF_DIL_Q = OFF_FOX_F + FOX_HEADS
OFF_DIL_K = OFF_DIL_Q + DIL_WIDTH
OFF_DIL_V = OFF_DIL_K + DIL_WIDTH
OFF_GATE_A = OFF_DIL_V + DIL_WIDTH
OFF_GATE_B = OFF_GATE_A + D_MODEL
N_IN = OFF_GATE_B + D_MODEL

kernel_name = 'hybrid_fox_dilated_hmoe_adaln'

def _rmsnorm(x, g):
    x32 = x.astype(jnp.float32)
    y = x32 * lax.rsqrt(jnp.mean(x32 * x32, axis=-1, keepdims=True) + EPS)
    return y.astype(x.dtype) * g

def _head_rms(t, g):
    t32 = t.astype(jnp.float32)
    y = t32 * lax.rsqrt(jnp.mean(t32 * t32, axis=-1, keepdims=True) + EPS)
    return y.astype(t.dtype) * g

def _t5_bucket(dist):
    max_exact = NUM_BUCKETS // 2
    d = np.maximum(dist, 1).astype(np.float32)
    large = max_exact + (np.log(d / max_exact) / np.log(REL_MAX_DISTANCE / max_exact)
                         * (NUM_BUCKETS - max_exact)).astype(np.int32)
    large = np.minimum(large, NUM_BUCKETS - 1)
    return np.where(dist < max_exact, dist, large).astype(np.int32)

def _forgetting_attention(q, k, v, log_f):
    B, S, H, E = q.shape
    scale = HEAD_DIM ** -0.5
    cum = jnp.cumsum(log_f, axis=1).transpose(0, 2, 1)
    outs = []
    for blk in range(S // Q_BLOCK):
        s0 = blk * Q_BLOCK
        s1 = s0 + Q_BLOCK
        logits = jnp.einsum('bqhe,bkhe->bhqk', q[:, s0:s1], k[:, :s1]).astype(jnp.float32) * scale
        logits = logits + cum[:, :, s0:s1, None] - cum[:, :, None, :s1]
        causal = np.arange(s0, s1)[:, None] >= np.arange(s1)[None, :]
        p = jax.nn.softmax(jnp.where(causal, logits, -jnp.inf), axis=-1)
        outs.append(jnp.einsum('bhqk,bkhe->bqhe', p.astype(v.dtype), v[:, :s1]))
    return jnp.concatenate(outs, axis=1)

def _dilated_group(q, k, v, table, window, dilation):
    B, S, H, E = q.shape
    L = window // dilation
    unit = L * dilation
    S_pad = -(-S // unit) * unit
    N = S_pad // dilation
    nb = N // L
    scale = HEAD_DIM ** -0.5

    def to_blocks(t):
        t = jnp.pad(t, ((0, 0), (0, S_pad - S), (0, 0), (0, 0)))
        t = t.reshape(B, N, dilation, H, E).transpose(0, 2, 1, 3, 4)
        return t.reshape(B, dilation, nb, L, H, E)

    def with_prev(t):
        prev = jnp.pad(t, ((0, 0), (0, 0), (1, 0), (0, 0), (0, 0), (0, 0)))[:, :, :-1]
        return jnp.concatenate([prev, t], axis=3)

    qb = to_blocks(q)
    kk = with_prev(to_blocks(k))
    vv = with_prev(to_blocks(v))
    i = np.arange(L)[:, None]
    j = np.arange(2 * L)[None, :]
    m = L + i - j
    band = (m >= 0) & (m <= L)
    first = band & (j >= L)
    valid = np.where(np.arange(nb)[:, None, None] == 0, first[None], band[None])
    bucket = _t5_bucket(np.clip(m, 0, None) * dilation)
    bias = table[bucket].transpose(2, 0, 1)
    logits = jnp.einsum('bdnqhe,bdnkhe->bdnhqk', qb, kk).astype(jnp.float32) * scale + bias
    logits = jnp.where(valid[None, None, :, None], logits, -jnp.inf)
    lse = jax.nn.logsumexp(logits, axis=-1)
    p = jnp.exp(logits - lse[..., None])
    o = jnp.einsum('bdnhqk,bdnkhe->bdnqhe', p.astype(v.dtype), vv)
    o = o.reshape(B, dilation, N, H, E).transpose(0, 2, 1, 3, 4).reshape(B, S_pad, H, E)[:, :S]
    lse = lse.transpose(0, 1, 2, 4, 3).reshape(B, dilation, N, H).transpose(0, 2, 1, 3).reshape(B, S_pad, H)[:, :S]
    return o, lse

def _mixer(h, rel_bias_table, w_in, b_forget, q_gain, k_gain, w_branch_a, w_branch_b, w_out):
    B, S, D = h.shape
    proj = h @ w_in
    qa = _head_rms(proj[..., OFF_FOX_Q:OFF_FOX_K].reshape(B, S, FOX_HEADS, HEAD_DIM), q_gain[:FOX_HEADS])
    ka = _head_rms(proj[..., OFF_FOX_K:OFF_FOX_V].reshape(B, S, FOX_HEADS, HEAD_DIM), k_gain[:FOX_HEADS])
    va = proj[..., OFF_FOX_V:OFF_FOX_F].reshape(B, S, FOX_HEADS, HEAD_DIM)
    log_f = jax.nn.log_sigmoid((proj[..., OFF_FOX_F:OFF_DIL_Q] + b_forget).astype(jnp.float32))
    ya = _forgetting_attention(qa, ka, va, log_f).reshape(B, S, FOX_WIDTH)
    qd = _head_rms(proj[..., OFF_DIL_Q:OFF_DIL_K].reshape(B, S, DIL_HEADS, HEAD_DIM), q_gain[FOX_HEADS:])
    kd = _head_rms(proj[..., OFF_DIL_K:OFF_DIL_V].reshape(B, S, DIL_HEADS, HEAD_DIM), k_gain[FOX_HEADS:])
    vd = proj[..., OFF_DIL_V:OFF_GATE_A].reshape(B, S, DIL_HEADS, HEAD_DIM)
    outs = []
    lses = []
    for g, (window, dilation) in enumerate(DIL_GROUPS):
        hs = slice(g * DIL_HEADS_PER_GROUP, (g + 1) * DIL_HEADS_PER_GROUP)
        o_g, lse_g = _dilated_group(qd[:, :, hs], kd[:, :, hs], vd[:, :, hs], rel_bias_table[:, hs], window, dilation)
        outs.append(o_g)
        lses.append(lse_g)
    wts = jax.nn.softmax(jnp.stack(lses, axis=0), axis=0)
    yd = jnp.sum(wts[..., None].astype(vd.dtype) * jnp.stack(outs, axis=0), axis=0).reshape(B, S, DIL_OUT_WIDTH)
    gate_a = jax.nn.sigmoid(proj[..., OFF_GATE_A:OFF_GATE_B])
    gate_b = jax.nn.sigmoid(proj[..., OFF_GATE_B:N_IN])
    merged = gate_a * (ya @ w_branch_a) + gate_b * (yd @ w_branch_b)
    return merged @ w_out

def _hier_moe(h, w_rg, b_rg, w_re, b_re, w1, w3, w2):
    B, S, D = h.shape
    T = B * S
    hf = h.reshape(T, D)
    g_logits = (hf @ w_rg + b_rg).astype(jnp.float32)
    g_prob = jax.nn.softmax(g_logits, axis=-1)
    g_idx = jnp.argmax(g_logits, axis=-1).astype(jnp.int32)
    g_w = jnp.take_along_axis(g_prob, g_idx[:, None], axis=1)
    e_logits = (hf @ w_re + b_re).astype(jnp.float32).reshape(T, N_GROUPS, EXPERTS_PER_GROUP)
    e_in = jnp.take_along_axis(e_logits, g_idx[:, None, None], axis=1)[:, 0]
    top_v, top_i = lax.top_k(e_in, TOP_K_IN_GROUP)
    weights = g_w * jax.nn.softmax(top_v, axis=-1)
    expert_ids = (g_idx[:, None] * EXPERTS_PER_GROUP + top_i).astype(jnp.int32)
    A = T * TOP_K_IN_GROUP
    flat_e = expert_ids.reshape(A)
    flat_tok = jnp.repeat(jnp.arange(T, dtype=jnp.int32), TOP_K_IN_GROUP)
    flat_w = weights.reshape(A)
    order = jnp.argsort(flat_e)
    sorted_e = flat_e[order]
    counts = jnp.zeros((N_EXPERTS,), jnp.int32).at[flat_e].add(1)
    starts = jnp.cumsum(counts) - counts
    padded = (counts + MOE_BLOCK - 1) // MOE_BLOCK * MOE_BLOCK
    pends = jnp.cumsum(padded)
    pstarts = pends - padded
    rank = jnp.arange(A, dtype=jnp.int32) - starts[sorted_e]
    dest = pstarts[sorted_e] + rank
    R = A + N_EXPERTS * MOE_BLOCK
    n_blk = R // MOE_BLOCK
    row_tok = jnp.full((R,), T, jnp.int32).at[dest].set(flat_tok[order])
    row_w = jnp.zeros((R,), jnp.float32).at[dest].set(flat_w[order])
    block_e = jnp.minimum(jnp.searchsorted(pends, jnp.arange(n_blk, dtype=jnp.int32) * MOE_BLOCK, side='right'),
                          N_EXPERTS - 1).astype(jnp.int32)
    xpad = jnp.concatenate([hf, jnp.zeros((1, D), hf.dtype)], axis=0)
    xs = xpad[row_tok].reshape(n_blk, MOE_BLOCK, D)

    def expert_block(args):
        xb, e = args
        return (jax.nn.silu(xb @ w1[e]) * (xb @ w3[e])) @ w2[e]

    y = lax.map(expert_block, (xs, block_e)).reshape(R, D)
    y = y * row_w[:, None].astype(y.dtype)
    out = jnp.zeros((T + 1, D), y.dtype).at[row_tok].add(y)[:T]
    return out.reshape(B, S, D)

def setup_inputs(seed: int = 0) -> dict:
    key = jax.random.key(seed)
    ks = jax.random.split(key, 21)

    def nrm(k, shape, scale):
        return jax.random.normal(k, shape, jnp.float32) * scale

    return {
        'x': nrm(ks[0], (BATCH, SEQ, D_MODEL), 1.0),
        'c': nrm(ks[1], (BATCH, D_MODEL), 1.0),
        'rel_bias_table': nrm(ks[2], (NUM_BUCKETS, DIL_HEADS), 0.5),
        'w_ada': nrm(ks[3], (DEPTH, D_MODEL, 6 * D_MODEL), D_MODEL ** -0.5),
        'b_ada': nrm(ks[4], (DEPTH, 6 * D_MODEL), 0.02),
        'norm1_g': 1.0 + nrm(ks[5], (DEPTH, D_MODEL), 0.02),
        'w_in': nrm(ks[6], (DEPTH, D_MODEL, N_IN), D_MODEL ** -0.5),
        'b_forget': 3.0 + nrm(ks[7], (DEPTH, FOX_HEADS), 0.1),
        'q_gain': 1.0 + nrm(ks[8], (DEPTH, QK_HEADS, HEAD_DIM), 0.02),
        'k_gain': 1.0 + nrm(ks[9], (DEPTH, QK_HEADS, HEAD_DIM), 0.02),
        'w_branch_a': nrm(ks[10], (DEPTH, FOX_WIDTH, D_MODEL), FOX_WIDTH ** -0.5),
        'w_branch_b': nrm(ks[11], (DEPTH, DIL_OUT_WIDTH, D_MODEL), DIL_OUT_WIDTH ** -0.5),
        'w_out': nrm(ks[12], (DEPTH, D_MODEL, D_MODEL), D_MODEL ** -0.5),
        'norm2_g': 1.0 + nrm(ks[13], (DEPTH, D_MODEL), 0.02),
        'w_router_group': nrm(ks[14], (DEPTH, D_MODEL, N_GROUPS), D_MODEL ** -0.5),
        'b_router_group': nrm(ks[15], (DEPTH, N_GROUPS), 0.01),
        'w_router_expert': nrm(ks[16], (DEPTH, D_MODEL, N_EXPERTS), D_MODEL ** -0.5),
        'b_router_expert': nrm(ks[17], (DEPTH, N_EXPERTS), 0.01),
        'w1': nrm(ks[18], (DEPTH, N_EXPERTS, D_MODEL, EXPERT_HIDDEN), D_MODEL ** -0.5),
        'w3': nrm(ks[19], (DEPTH, N_EXPERTS, D_MODEL, EXPERT_HIDDEN), D_MODEL ** -0.5),
        'w2': nrm(ks[20], (DEPTH, N_EXPERTS, EXPERT_HIDDEN, D_MODEL), EXPERT_HIDDEN ** -0.5),
    }

def reference(x, c, rel_bias_table, w_ada, b_ada, norm1_g, w_in, b_forget, q_gain, k_gain,
              w_branch_a, w_branch_b, w_out, norm2_g, w_router_group, b_router_group,
              w_router_expert, b_router_expert, w1, w3, w2):
    for l in range(DEPTH):
        mod = jax.nn.silu(c) @ w_ada[l] + b_ada[l]
        sh1, sc1, g1, sh2, sc2, g2 = jnp.split(mod, 6, axis=-1)
        h = _rmsnorm(x, norm1_g[l]) * (1 + sc1[:, None]) + sh1[:, None]
        x = x + g1[:, None] * _mixer(h, rel_bias_table, w_in[l], b_forget[l], q_gain[l], k_gain[l],
                                     w_branch_a[l], w_branch_b[l], w_out[l])
        h = _rmsnorm(x, norm2_g[l]) * (1 + sc2[:, None]) + sh2[:, None]
        x = x + g2[:, None] * _hier_moe(h, w_router_group[l], b_router_group[l], w_router_expert[l],
                                        b_router_expert[l], w1[l], w3[l], w2[l])
    return x


_drawn_inputs = setup_inputs


def setup_inputs(seed=0):
    import zlib

    import numpy as np

    out = dict(_drawn_inputs(seed))
    spreads = {}
    factors = {'norm1_g': 3.046,
     'q_gain': 5.198,
     'k_gain': 4.619,
     'b_router_group': 62.49,
     'b_router_expert': 16.047,
     'norm2_g': 4.147}
    for name, (base, spread) in spreads.items():
        noise = np.random.default_rng([zlib.crc32(name.encode()), seed]).standard_normal(out[name].shape)
        drawn = base * np.exp(spread * noise) if base else spread * noise
        out[name] = __import__('jax').numpy.asarray(drawn.astype(out[name].dtype))
    for name, factor in factors.items():
        out[name] = (out[name] * factor).astype(out[name].dtype)
    return out
```

```python
from contextlib import ExitStack

import concourse.bass as bass
from concourse import mybir
from concourse.alu_op_type import AluOpType as ALU

ACT = mybir.ActivationFunctionType
AX = mybir.AxisListType
F32 = mybir.dt.float32
F32R = mybir.dt.float32r
BF16 = mybir.dt.bfloat16
I32 = mybir.dt.int32
U32 = mybir.dt.uint32

P = 128
T = 1024
D = 1024
KT = D // P
NT = T // P
HALF = 512
E = 64
FOX_HEADS, DIL_HEADS, NG = 8, 12, 3
DILATION = (1, 4, 16)
ORDER_STEP = (1, 4, 8)
FOX_W, DIL_W = FOX_HEADS * E, DIL_HEADS * E
OFF_FQ, OFF_FK, OFF_FV = 0, FOX_W, 2 * FOX_W
OFF_DQ = 3 * FOX_W + FOX_HEADS
OFF_DK, OFF_DV = OFF_DQ + DIL_W, OFF_DQ + 2 * DIL_W
OFF_GA = OFF_DQ + 3 * DIL_W
OFF_GB = OFF_GA + D
N_GROUPS, PER_GROUP = 4, 8
N_EXP = N_GROUPS * PER_GROUP
HID = D // 2
N_ROUTE = N_GROUPS + N_EXP
SLOTS = 128
MAX_BLK = 48
N_OVER = MAX_BLK - N_EXP
UW = E + 2
BIG = 1e30
EXP_AND_LN = 6
N_SMALL = 12
EPS = 1e-6
C_C, C_N1, C_N2, C_BADA, C_QG, C_KG, N_ROWS = 0, 8, 16, 24, 72, 82, 92
K_ID, K_CM, K_BO, K_TI, K_TS, K_ROW = 0, 128, 256, 384, 512, 640
R_PRI4, R_PRI8, R_I32, R_I16, R_BID = 0, 4, 12, 44, 60
K_COLS = K_ROW + R_BID + MAX_BLK


def build(nc, x, c, rel, w_ada, b_ada, n1, w_in, b_f, qg, kg, w_a, w_b, w_out, n2, w_rg, b_rg,
          w_re, b_re, w1, w3, w2, cst, oh, out):
    KB = 1024
    BASE = 16512
    RP, RA, RH, RB, RY, RW, RS, RK = (BASE + v * KB for v in (0, 15, 47, 111, 143, 167, 193, 201))

    ctx = ExitStack()
    with ctx:
        def at(name, shape, dt, offset):
            return nc.alloc_sbuf_tensor_at(name, shape, dt, offset=offset)

        def sems(text):
            return [ctx.enter_context(nc.semaphore(name)) for name in text.split()]

        def dram(name, shape, dt=F32):
            return nc.dram_tensor(name, shape, dt, kind="Internal").ap()

        cursor = [RP]

        def keep(name, cols, dt=F32):
            t = at(name, [P, cols], dt, cursor[0])
            cursor[0] += (cols * (2 if dt == BF16 else 4) + 31) // 32 * 32
            return t

        consts = keep("consts", K_COLS)
        ones = keep("ones", P)
        ident = consts[:, K_ID:K_ID + P]
        block_ones = consts[:, K_BO:K_BO + P]
        tri_incl = consts[:, K_TI:K_TI + P]
        tri_strict = consts[:, K_TS:K_TS + P]
        wide0 = cursor[0]
        gate_row = [at(f"gate_row{i}", [P, D], F32, wide0 + i * 4096) for i in range(2)]
        cum_row = at("cum_row", [P, 2, T], F32, wide0)
        bias01 = at("bias01", [P, 8, 256], F32, wide0)
        bias2 = at("bias2", [P, 4, P], F32, wide0 + 8192)
        assert wide0 + 8192 + 2048 <= RA
        cursor[0] = RK
        col = keep("col", N_ROWS)
        mod = keep("mod", 48)
        scale1 = keep("scale1", KT)
        scale2 = keep("scale2", KT)
        eps_col = keep("eps_col", 1)
        id_bf = keep("id_bf", P, BF16)
        cm_bf = keep("cm_bf", P, BF16)
        silu_c = keep("silu_c", KT)
        silu_t = keep("silu_t", KT)
        qgain = keep("qgain", 10)
        ssq = keep("ssq", NT)
        rstd = keep("rstd", NT)
        nmin = keep("nmin", 4)
        denom = keep("denom", 4)
        rden = keep("rden", 4)
        bfr = keep("bfr", FOX_HEADS)
        brr = keep("brr", N_ROUTE)
        tab = keep("tab", DIL_HEADS)
        wts = keep("wts", 2 * NT)
        dest = keep("dest", 2 * NT, U32)
        sidx = keep("sidx", 2 * NT, U32)
        tok_id = keep("tok_id", NT, I32)
        slot_tok = keep("slot_tok", MAX_BLK, I32)
        blk_exp = keep("blk_exp", MAX_BLK + 2, I32)
        idx_now = keep("idx_now", 1, I32)
        assert cursor[0] <= 229344, cursor[0]

        rows = at("rows", [P, P], F32, RB)
        ohs = at("ohs", [P, NG * 384], F32, RB + 512)
        relrow = at("relrow", [4, NG, 384], F32, RB + 6 * KB)
        ada_w = [at(f"ada_w{i}", [P, KT, 256], F32, RW + i * 8 * KB) for i in range(4)]
        xt = at("xt", [P, NT, D], F32, RA)
        junk = at("junk", [P, D], F32, RB + 16 * KB)
        h_tmp = [at(f"h_tmp{i}", [P, HALF], F32, RB + 20 * KB + i * 2 * KB) for i in range(2)]
        h_hi = at("h_hi", [P, KT, T], F32R, RH)
        h_lo = at("h_lo", [P, KT, T], F32R, RH + 32 * KB)
        VN = 4 * E + FOX_HEADS
        v_raw = at("v_raw", [P, KT, VN], F32, RW)
        v_hi = at("v_hi", [P, KT, VN], F32R, RW + 8448)
        v_lo = at("v_lo", [P, KT, VN], F32R, RW + 2 * 8448)
        qk_raw = [at(f"qk_raw{i}", [P, KT, P], F32, RW + i * 4096) for i in range(2)]
        qk_hi = [at(f"qk_hi{i}", [P, KT, P], F32R, RW + 8448 + i * 8192) for i in range(2)]
        qk_lo = [at(f"qk_lo{i}", [P, KT, P], F32R, RW + 8448 + 4096 + i * 8192) for i in range(2)]
        v_fox = at("v_fox", [P, NT, FOX_W], F32, RA)
        v_dil = at("v_dil", [P, NT, 4 * E], F32, RA)
        rec = [at(f"rec{i}", [P, NT, 2 * UW], F32, RA + 16 * KB + i * 4224) for i in range(2)]
        logits = [at(f"logits{i}", [P, T], F32, RB + i * 4096) for i in range(2)]
        prob = [at(f"prob{i}", [P, T], F32, RB + 8 * KB + i * 4096) for i in range(2)]
        probT = [at(f"probT{i}", [P, NT, P], F32, RB + 16 * KB + i * 4096) for i in range(2)]
        square = at("square", [P, HALF], F32, RB + 24 * KB)
        rs_head = at("rs_head", [P, HALF], F32, RB + 26 * KB)
        y_pair = at("y_pair", [P, NT, P], F32, RB + 28 * KB)
        qT = at("qT", [P, T], F32, RS)
        kT = at("kT", [P, T], F32, RS + 4096)
        fg = [at(f"fg{i}", [P, FOX_HEADS, NT], F32, RA + 25 * KB + i * 256) for i in range(6)]
        cumT = at("cumT", [FOX_HEADS * NT, P], F32, RA + 27 * KB)
        mrec = at("mrec", [P, 4, NG, 4, UW], F32, RB)
        macc = [at(f"macc{i}", [P, 4, 4, E], F32, RB + 13 * KB + i * 4096) for i in range(2)]
        msm = at("msm", [P, 12, 4, 4], F32, RB + 21 * KB)
        y_f = at("y_f", [P, 6, T], F32, RY)
        y_lo = at("y_lo", [P, 6, T], F32R, RY)
        y_hi = at("y_hi", [P, 6, T], F32R, RA)
        merged = at("merged", [P, KT, T], F32, RB)
        g_k = (KT, KT, 6)
        g_raw, g_hi, g_lo = [], [], []
        g_at = RW
        for part, (lst, dt) in {"raw": (g_raw, F32), "hi": (g_hi, F32R), "lo": (g_lo, F32R)}.items():
            for i in range(3):
                lst.append(at(f"g_{part}{i}", [P, g_k[i], P], dt, g_at))
                g_at += g_k[i] * P * 4
        assert g_at <= RK
        g_tmp = [at(f"g_tmp{i}", [P, 2, HALF], F32, RA + 24 * KB + i * 4096) for i in range(2)]
        mod_rows = at("mod_rows", [48, P], F32, RB + 24 * KB)
        m_hi = at("m_hi", [P, KT, T], F32R, RH)
        m_lo = at("m_lo", [P, KT, T], F32R, RH + 32 * KB)
        x2 = at("x2", [P, NT, D], F32, RA)
        OC = 256
        o_raw = [at(f"o_raw{i}", [P, KT, OC], F32, RY + i * 8192) for i in range(3)]
        o_hi = [at(f"o_hi{i}", [P, KT, OC], F32R, RW + i * 16384) for i in range(2)]
        o_lo = [at(f"o_lo{i}", [P, KT, OC], F32R, RW + i * 16384 + 8192) for i in range(2)]
        o_tmp = at("o_tmp", [P, 2, OC], F32, RB + 28 * KB)
        o_junk = at("o_junk", [P, D], F32, RW)
        xn2 = [at(f"xn2_{i}", [P, D], F32, RY + i * 4096) for i in range(4)]
        w_rt = at("w_rt", [P, KT, N_ROUTE], F32, RY + 16 * KB)
        h2T = at("h2T", [P, KT, T], F32, RB)
        e_raw = [at(f"e_raw{i}", [P, 4, HID], F32, RW + i * 8192) for i in range(3)]
        e_hi = [at(f"e_hi{i}", [P, 4, HID], F32R, RH + i * 16384) for i in range(6)]
        e_lo = [at(f"e_lo{i}", [P, 4, HID], F32R, RH + i * 16384 + 8192) for i in range(6)]
        y_e = at("y_e", [P, D], F32, RY)
        xT_f = at("xT_f", [P, KT, P], F32, RY + 4 * KB)
        gate_act = at("gate_act", [P, HID], F32, RY + 8 * KB)
        act_in = at("act_in", [P, HID], F32, RY + 10 * KB)
        xg = at("xg", [P, D], F32, RY + 12 * KB)
        xT_hi = at("xT_hi", [P, KT, P], F32R, RY + 16 * KB)
        xT_lo = at("xT_lo", [P, KT, P], F32R, RY + 20 * KB)
        aT_hi = at("aT_hi", [P, 4, P], F32R, RW + 30 * KB)
        aT_lo = at("aT_lo", [P, 4, P], F32R, RW + 32 * KB)
        y_slot = [at(f"y_slot{i}", [P, D], F32, RH + i * 4096) for i in range(2 * NT)]
        y_sum = [at(f"y_sum{i}", [P, D], F32, RB + i * 4096) for i in range(4)]
        free = [RW + 24 * KB, RY + 20 * KB + 1024]

        def scratch(name, shape, dt=F32, where=0):
            size = 4
            for v in shape:
                size *= v
            t = at(name, [P] + shape, dt, free[where])
            free[where] += (size + 31) // 32 * 32
            return t

        lg = scratch("lg", [NT, N_ROUTE])
        g_max, g_sum, g_w, g_first, m_one, m_two, m_ex, m_r, e_first = (
            scratch(n, [NT], where=1) for n in "g_max g_sum g_w g_first m_one m_two m_ex m_r e_first".split())
        g_ex, g_eq, g_hot = (scratch(n, [NT, N_GROUPS], where=1) for n in "g_ex g_eq g_hot".split())
        e_in, e_eq, hot1, hot2, e_next = (scratch(n, [NT, PER_GROUP], where=0) for n in "e_in e_eq hot1 hot2 e_next".split())
        r_prod, r_mask, rank, r_blk = (scratch(n, [NT, N_EXP]) for n in "r_prod r_mask rank r_blk".split())
        r_int = scratch("r_int", [NT, N_EXP], I32)
        assert free[0] <= RW + 34 * KB
        before = at("before", [P, NT, N_EXP], F32, RY + 19 * KB + 512)
        c_int = at("c_int", [P, N_EXP], I32, free[1])
        over = [at(f"over{i}", [P, N_EXP], F32, free[1] + 128 + 128 * i) for i in range(3)]
        dest_f = at("dest_f", [P, 2 * NT], F32, free[1] + 512)
        sidx_f = at("sidx_f", [P, 2 * NT], F32, free[1] + 576)
        assert free[1] + 640 <= RW
        exp_cmp = at("exp_cmp", [1, N_OVER, N_EXP], F32, RY + 17 * KB + 512)
        exp_of = at("exp_of", [1, N_OVER], F32, RY + 20 * KB + 512)

        bank = ctx.enter_context(nc.psum_tensor("bank", [P, 8, HALF], F32))

        d_rel = dram("d_rel", [DIL_HEADS, P, 384])
        d_cum = dram("d_cum", [FOX_HEADS * NT, P])
        d_rec = dram("d_rec", [NG, T, 4 * UW])
        d_mod = dram("d_mod", [48, P])
        d_xn = dram("d_xn", [T, D])
        d_slot = dram("d_slot", [SLOTS * MAX_BLK, 1], I32)
        d_y = dram("d_y", [MAX_BLK * SLOTS, D])

        (small_ld, pool_set, bf_set, rowsT_pe, col_ok, silu_e, rel_pe, rel_ev, rel_st, bias_ld,
         ada_pe, mod_ok, scl_ok, chain_a, chain_v) = sems(
            "small_ld pool_set bf_set rowsT_pe col_ok silu_e rel_pe rel_ev rel_st bias_ld "
            "ada_pe mod_ok scl_ok chain_a chain_v")
        tile_ld = sems(" ".join(f"tile_ld{t}" for t in range(NT)))
        ada_ld = sems(" ".join(f"ada_ld{i}" for i in range(4)))
        ssq_ok, rstd_ok, xn_ok, xT_pe, xT_act, h_hi_ok, h_lo_ok = sems(
            "ssq_ok rstd_ok xn_ok xT_pe xT_act h_hi_ok h_lo_ok")
        w_ld = sems("w_ld_a w_ld_b")
        w_hi_ok, w_lo_ok, v_pe, v_ev_act, v_ev_dve = sems(
            "w_hi_ok w_lo_ok v_pe v_ev_act v_ev_dve")
        proj_pe, sq_ok, ss_pe, ln_ok, rs_ok, norm_ok = sems("proj_pe sq_ok ss_pe ln_ok rs_ok norm_ok")
        qk_pe, min_ok, exp_ok, turn_pe, pT_act, pT_dve, pv_pe, rden_ok, y_ok, yT_pe, yT_ok = sems(
            "qk_pe min_ok exp_ok turn_pe pT_act pT_dve pv_pe rden_ok y_ok yT_pe yT_ok")
        rec_st = sems("rec_st0 rec_st1")
        fg_ok, fg_act, cum_pe, cum_dve, cumT_pe, cumT_ev, cum_st, cum_ld = sems(
            "fg_ok fg_act cum_pe cum_dve cumT_pe cumT_ev cum_st cum_ld")
        mrec_ld, mrg_d, mrg_e, mrg_y, mrg_pe, mrg_ev = sems("mrec_ld mrg_d mrg_e mrg_y mrg_pe mrg_ev")
        modT_pe, modT_ok, mod_st, gate_ld, y_hi_ok, y_lo_ok = sems("modT_pe modT_ok mod_st gate_ld y_hi_ok y_lo_ok")
        g_ld = sems("g_ld0 g_ld1 g_ld2")
        g_hi_ok, g_lo_ok, gate_pe, gate_e, merged_ok = sems("g_hi_ok g_lo_ok gate_pe gate_e merged_ok")
        x2_ld, m_hi_ok, m_lo_ok, o_hi_ok, o_lo_ok, o_pe, o_done = sems("x2_ld m_hi_ok m_lo_ok o_hi_ok o_lo_ok o_pe o_done")
        o_ld = sems("o_ld0 o_ld1 o_ld2")
        rs2_ok, xn2_ok, h2_pe, h2_act, h2_dve, rt_ld, rt_pe = sems("rs2_ok xn2_ok h2_pe h2_act h2_dve rt_ld rt_pe")
        xn_st = sems("xn_st0 xn_st1 xn_st2 xn_st3")
        r_d, r_a, rank_pe, tok_ok, slot_z, scat, slot_ld, dest_ok = sems("r_d r_a rank_pe tok_ok slot_z scat slot_ld dest_ok")
        e_ld = sems("e_ld0 e_ld1 e_ld2")
        e_hi_ok, e_lo_ok, e_used, xg_ld, xgT_pe, xmod_ok, xT_hi_ok, xT_lo_ok = sems(
            "e_hi_ok e_lo_ok e_used xg_ld xgT_pe xmod_ok xT_hi_ok xT_lo_ok")
        idx_ok, ye_end = sems("idx_ok ye_end")
        slot_y = sems(" ".join(f"slot_y{t}" for t in range(NT)))
        sig_e, silu_v, act_ok, actT_pe, aT_hi_ok, aT_lo_ok, ye_act, ye_dve, ye_st = sems(
            "sig_e silu_v act_ok actT_pe aT_hi_ok aT_lo_ok ye_act ye_dve ye_st")
        f_act, f_dve, f_pool, out_st = sems("f_act f_dve f_pool out_st")
        block = ctx.enter_context(nc.Block())

        jobs = []
        for g in range(NG):
            jobs.append(("v", OFF_DV + g * 4 * E, 4 * E))
            for p in range(2):
                jobs.append(("qk", OFF_DQ + (2 * g + p) * P, OFF_DK + (2 * g + p) * P))
        jobs += [("v", OFF_FV, 4 * E), ("v", OFF_FV + 4 * E, VN)]
        for p in range(FOX_HEADS // 2):
            jobs.append(("qk", OFF_FQ + p * P, OFF_FK + p * P))
        J_FOX = 9
        w_in_v = w_in.rearrange("(k p) n -> p k n", p=P)

        def raw_parts(j):
            kind, a, b = jobs[j]
            if kind == "v":
                return [(v_raw[:, 4 * i:4 * i + 4, 0:b], w_in_v[:, 4 * i:4 * i + 4, a:a + b]) for i in range(2)]
            return [(qk_raw[0][:, :, :], w_in_v[:, :, a:a + P]), (qk_raw[1][:, :, :], w_in_v[:, :, b:b + P])]

        def split_parts(j):
            kind, a, b = jobs[j]
            if kind == "v":
                return [tuple(t[:, 4 * i:4 * i + 4, 0:b] for t in (v_raw, v_hi, v_lo)) for i in range(2)]
            return [(qk_raw[i][:, :, :], qk_hi[i][:, :, :], qk_lo[i][:, :, :]) for i in range(2)]

        def products_done(eng, j):
            if jobs[j][0] == "v":
                eng.wait_ge(v_pe, NT * sum(job[0] == "v" for job in jobs[:j + 1]))
            else:
                eng.wait_ge(proj_pe, 4 * sum(job[0] == "qk" for job in jobs[:j + 1]))

        def act_split(act, j):
            for i, (raw, hi, _) in enumerate(split_parts(j)):
                act.wait_ge(w_ld[i], 16 * (j + 1))
                if j:
                    products_done(act, j - 1)
                nc.scalar.activation(hi, raw, ACT.Copy).then_inc(w_hi_ok, 1)

        def dve_split(dve, j):
            for i, (raw, hi, lo) in enumerate(split_parts(j)):
                dve.wait_ge(w_hi_ok, 2 * j + i + 1)
                nc.vector.tensor_tensor(lo, raw, hi.bitcast(F32), ALU.subtract).then_inc(w_lo_ok, 1)

        PROJ_BANK = (0, 2, 1, 3)

        def tokens_of(view, g, tile):
            if g == 0:
                return view[:, tile * P:(tile + 1) * P]
            if g == 1:
                r, b = tile // 2, tile % 2
                return view[:, r + 512 * b:min(r + 512 * b + 512, T):4]
            return view[:, tile:T:8]

        def placed(view, g, half):
            if g <= 0:
                return view[:, half * HALF:(half + 1) * HALF]
            r = ORDER_STEP[g]
            n = HALF // r
            return view.rearrange("p (r n) -> p n r", r=r)[:, half * n:(half + 1) * n, :]

        def units_of(g):
            out = []
            for q in range(NT):
                for a in range(2):
                    if g < 0:
                        out.append((q, a, 0, (q + 1) * P))
                    elif g == 2 or (g == 0 and q == 0) or (g == 1 and q % 2 == 0):
                        out.append((q, a, q * P, P))
                    else:
                        out.append((q, a, (q - 1) * P, 2 * P))
            return out

        def groups(g):
            n, out = 0, []
            for _, _, _, kw in units_of(g):
                here = []
                for b in range(0, kw // P, 4):
                    here.append((n, list(range(b, min(b + 4, kw // P)))))
                    n += 1
                out.append(here)
            return out, n

        def group_of_pair(jp):
            return jp // 2 if jp < 6 else -1

        gbase = [0]
        for jp in range(10):
            gbase.append(gbase[-1] + groups(group_of_pair(jp))[1])

        def s_at(u, kw):
            if kw <= HALF:
                return bank[:, 2 * (u % 2), 0:kw]
            b = 2 * (u % 2)
            return bank[:, b:b + 2, :].rearrange("p b n -> p (b n)")[:, 0:kw]

        def pe_proj(pe, dst, hi, lo, lhs, half):
            n = 0
            for k in range(KT):
                t = slice(half * HALF, (half + 1) * HALF)
                for w, h in ((hi, h_hi), (hi, h_lo), (lo, h_hi)):
                    mm = nc.tensor.matmul(dst, w[:, k, :], h[:, k, t], start=(n == 0), stop=(n == 3 * KT - 1))
                    n += 1
            return mm

        def pe_values(pe, j, vj, g):
            kind, a, ncol = jobs[j]
            pe.wait_ge(w_lo_ok, 2 * j + 1)
            for t in range(NT):
                m = vj * NT + t
                if t >= 4:
                    pe.wait_ge(v_ev_dve if t % 2 else v_ev_act, (m - 4) // 2 + 1)
                n = 0
                for k in range(KT):
                    if k == 4 and t == 0:
                        pe.wait_ge(w_lo_ok, 2 * j + 2)
                    for w, h in ((v_hi, h_hi), (v_hi, h_lo), (v_lo, h_hi)):
                        mm = nc.tensor.matmul(bank[:, t % 4, 0:ncol], tokens_of(h[:, k, :], max(g, 0), t),
                                              w[:, k, 0:ncol], start=(n == 0), stop=(n == 3 * KT - 1))
                        n += 1
                mm.then_inc(v_pe, 1)

        def ev_values(eng, op, j, vj, which, done):
            kind, a, ncol = jobs[j]
            for t in range(which, NT, 2):
                eng.wait_ge(v_pe, vj * NT + t + 1)
                if j < J_FOX:
                    dst = v_dil[:, t, :]
                else:
                    c0 = (j - J_FOX) * 4 * E
                    dst = v_fox[:, t, c0:c0 + 4 * E]
                last = op(dst, bank[:, t % 4, 0:4 * E])
                if ncol > 4 * E:
                    last = op(fg[0][:, :, t], bank[:, t % 4, 4 * E:VN])
                last.then_inc(done, 1)

        def act_copy(out_, in_):
            return nc.scalar.activation(out_, in_, ACT.Copy)

        def pe_pair(pe, jp, j):
            g = group_of_pair(jp)
            units, (turns, _) = units_of(g), groups(g)
            heads0 = 0 if g >= 0 else 2 * (jp - 6)

            def proj(n):
                i, half = n % 2, n // 2
                pe.wait_ge(w_lo_ok, 2 * j + i + 1)
                mm = pe_proj(pe, bank[:, PROJ_BANK[n], :], qk_hi[i], qk_lo[i], None, half)
                mm.then_inc(proj_pe, 1)

            def sum_squares(n):
                pe.wait_ge(sq_ok, 4 * jp + n + 1)
                if 4 * jp + n:
                    pe.wait_ge(ln_ok, 4 * jp + n)
                nc.tensor.matmul(bank[:, 7, :], block_ones, square[:, :], start=True, stop=True).then_inc(ss_pe, 1)

            def scores(u):
                q, a, k0, kw = units[u]
                pe.wait_ge(norm_ok, 4 * jp + (2 if g <= 0 and q < 4 else 4))
                if u >= 2:
                    pe.wait_ge(min_ok, 16 * jp + u - 1)
                dst = s_at(u, kw)
                h = slice(a * E, (a + 1) * E)
                for c in range(0, kw, HALF):
                    w = min(HALF, kw - c)
                    diag = g < 0 and c <= q * P < c + w
                    mm = nc.tensor.matmul(dst[:, c:c + w], qT[h, q * P:(q + 1) * P], kT[h, k0 + c:k0 + c + w],
                                          start=True, stop=not diag)
                    if diag:
                        mm = nc.tensor.matmul(dst[:, q * P:(q + 1) * P], id_bf[:, :], cm_bf[:, :],
                                              start=False, stop=True)
                mm.then_inc(qk_pe, 1)

            def turn(u):
                pe.wait_ge(exp_ok, 16 * jp + u + 1)
                for n, blocks in turns[u]:
                    G = gbase[jp] + n
                    if G >= 2:
                        pe.wait_ge((pT_act, pT_dve)[G % 2], G // 2)
                    for b in blocks:
                        mm = nc.tensor.transpose(bank[:, 5 + G % 2, (b % 4) * P:(b % 4 + 1) * P],
                                                 prob[u % 2][:, b * P:(b + 1) * P], ident)
                    mm.then_inc(turn_pe, 1)

            def values(u):
                q, a, k0, kw = units[u]
                for n, _ in turns[u]:
                    G = gbase[jp] + n
                    pe.wait_ge((pT_act, pT_dve)[G % 2], G // 2 + 1)
                if u >= 2 or jp:
                    pe.wait_ge(y_ok, 16 * jp + u - 1)
                for b in range(kw // P):
                    if g < 0:
                        v = v_fox[:, b, (heads0 + a) * E:(heads0 + a + 1) * E]
                    else:
                        v = v_dil[:, k0 // P + b, (2 * (jp % 2) + a) * E:(2 * (jp % 2) + a + 1) * E]
                    mm = nc.tensor.matmul(bank[:, (4, 7)[u % 2], 0:E], probT[u % 2][:, b, :], v,
                                          start=(b == 0), stop=(b == kw // P - 1))
                mm.then_inc(pv_pe, 1)

            def turn_y(half):
                pe.wait_ge(y_ok, 16 * jp + (16 if half else 10))
                for q in range(4):
                    mm = nc.tensor.transpose(bank[:, 7, q * P:(q + 1) * P], y_pair[:, 4 * half + q, :], ident)
                mm.then_inc(yT_pe, 1)

            early = g <= 0
            proj(0)
            proj(1)
            if jp:
                pe.wait_ge(y_ok, 16 * jp)
            if jp > 6:
                pe.wait_ge(yT_ok, 2 * (jp - 6))
            sum_squares(0)
            proj(2)
            sum_squares(1)
            proj(3)
            sum_squares(2)
            if not early:
                sum_squares(3)
            scores(0)
            scores(1)
            if early:
                sum_squares(3)
            for u in range(16):
                turn(u)
                if g < 0 and u == 12:
                    pe.wait_ge(yT_ok, 2 * (jp - 6) + 1)
                if u:
                    values(u - 1)
                if g < 0 and u == 10:
                    turn_y(0)
                if u + 2 < 16:
                    scores(u + 2)
            values(15)
            if g < 0:
                turn_y(1)

        def act_pair(act, jp, j):
            g = group_of_pair(jp)
            units, (turns, _) = units_of(g), groups(g)
            early = g <= 0

            def norm(n):
                N = 4 * jp + n
                act.wait_ge(proj_pe, N + 1)
                if N:
                    act.wait_ge(ss_pe, N)
                nc.scalar.activation(square[:, :], bank[:, PROJ_BANK[n], :], ACT.Square).then_inc(sq_ok, 1)

            def root(n):
                N = 4 * jp + n
                act.wait_ge(ss_pe, N + 1)
                if N:
                    act.wait_ge(norm_ok, N)
                nc.scalar.activation(rs_head[:, :], bank[:, 7, :], ACT.Ln, scale=1.0 / E,
                                     bias=eps_col[:, :]).then_inc(ln_ok, 1)
                act.wait_ge(ln_ok, N + 1)
                nc.scalar.activation(rs_head[:, :], rs_head[:, :], ACT.Exp, scale=-0.5).then_inc(rs_ok, 1)

            def exps(u):
                q, a, k0, kw = units[u]
                act.wait_ge(min_ok, 16 * jp + u + 1)
                if u >= 2:
                    act.wait_ge(turn_pe, gbase[jp] + turns[u - 2][-1][0] + 1)
                if g < 0:
                    lo, su = nmin[:, u % 4:u % 4 + 1], denom[:, u % 4:u % 4 + 1]
                    if u >= 4:
                        act.wait_ge(rden_ok, 16 * (jp - 6) + u - 3)
                else:
                    r = rec[jp % 2][:, q, a * UW:(a + 1) * UW]
                    su, lo = r[:, E:E + 1], r[:, E + 1:E + 2]
                nc.scalar.activation(prob[u % 2][:, 0:kw], logits[u % 2][:, 0:kw], ACT.Exp, bias=lo, scale=-1.0,
                                     accum_out=su).then_inc(exp_ok, 1)

            def copies(u):
                for n, blocks in turns[u]:
                    G = gbase[jp] + n
                    if G % 2 == 0:
                        act.wait_ge(turn_pe, G + 1)
                        if u >= 2:
                            act.wait_ge(pv_pe, 16 * jp + u - 1)
                        elif jp:
                            act.wait_ge(pv_pe, 16 * jp)
                        w = len(blocks)
                        nc.scalar.activation(probT[u % 2][:, blocks[0]:blocks[0] + w, :],
                                             bank[:, 5, 0:w * P].rearrange("p (b n) -> p b n", n=P),
                                             ACT.Copy).then_inc(pT_act, 1)

            norm(0)
            root(0)
            norm(1)
            root(1)
            norm(2)
            root(2)
            norm(3)
            root(3)
            exps(0)
            exps(1)
            for u in range(16):
                copies(u)
                if u == 2 and j + 1 < len(jobs):
                    act_split(act, j + 1)
                if g < 0 and u == 11:
                    y_out(act, jp, 0)
                if u + 2 < 16:
                    exps(u + 2)
            if g < 0:
                y_out(act, jp, 1)

        def y_out(act, jp, half):
            act.wait_ge(yT_pe, 2 * (jp - 6) + half + 1)
            nc.scalar.activation(y_f[:, jp - 6, half * HALF:(half + 1) * HALF], bank[:, 7, :],
                                 ACT.Copy).then_inc(yT_ok, 1)

        def dve_pair(dve, jp, j):
            g = group_of_pair(jp)
            units, (turns, _) = units_of(g), groups(g)
            early = g <= 0

            def norm(n):
                i, half = n % 2, n // 2
                dve.wait_ge(rs_ok, 4 * jp + n + 1)
                gain = qgain if i == 0 else col[:, C_KG:C_KG + 10]
                p = jp - 6 if g < 0 else 4 + jp
                src, rr, dst = bank[:, PROJ_BANK[n], :], rs_head[:, :], placed((qT, kT)[i][:, :], g, half)
                if g > 0:
                    src = src.rearrange("p (n r) -> p n r", r=ORDER_STEP[g])
                    rr = rr.rearrange("p (n r) -> p n r", r=ORDER_STEP[g])
                if n == 0 and jp:
                    dve.wait_ge(qk_pe, 16 * jp)
                nc.vector.scalar_tensor_tensor(out=dst, in0=src, scalar=gain[:, p:p + 1], in1=rr,
                                               op0=ALU.mult, op1=ALU.mult).then_inc(norm_ok, 1)

            def minimum(u):
                q, a, k0, kw = units[u]
                dve.wait_ge(qk_pe, 16 * jp + u + 1)
                if u >= 2:
                    dve.wait_ge(exp_ok, 16 * jp + u - 1)
                elif u == 0:
                    if jp:
                        dve.wait_ge(exp_ok, 16 * jp)
                    if g < 0:
                        dve.wait_ge(cum_ld, 16 * (jp - 5))
                    elif jp >= 2:
                        dve.wait_ge(rec_st[jp % 2], 128 * (jp // 2))
                if g < 0:
                    add, lo = cum_row[:, a, 0:kw], nmin[:, u % 4:u % 4 + 1]
                else:
                    h = 2 * (jp % 2) + a
                    add = bias2[:, h, :] if g == 2 else bias01[:, 4 * g + h, 256 - kw:256]
                    lo = rec[jp % 2][:, q, a * UW + E + 1:a * UW + E + 2]
                nc.vector.tensor_tensor_reduce(out=logits[u % 2][:, 0:kw], in0=s_at(u, kw), in1=add,
                                               scale=1.0, scalar=3e38, op0=ALU.add, op1=ALU.min,
                                               accum_out=lo).then_inc(min_ok, 1)

            def copies(u):
                for n, blocks in turns[u]:
                    G = gbase[jp] + n
                    if G % 2:
                        dve.wait_ge(turn_pe, G + 1)
                        if u >= 2:
                            dve.wait_ge(pv_pe, 16 * jp + u - 1)
                        elif jp:
                            dve.wait_ge(pv_pe, 16 * jp)
                        w = len(blocks)
                        nc.vector.tensor_copy(probT[u % 2][:, blocks[0]:blocks[0] + w, :],
                                              bank[:, 6, 0:w * P].rearrange("p (b n) -> p b n", n=P)).then_inc(pT_dve, 1)

            def result(u):
                q, a, _, _ = units[u]
                src = bank[:, (4, 7)[u % 2], 0:E]
                if g < 0:
                    if u == 0 and jp > 6:
                        dve.wait_ge(yT_pe, 2 * (jp - 6))
                    dve.wait_ge(exp_ok, 16 * jp + u + 1)
                    nc.vector.reciprocal(rden[:, u % 4:u % 4 + 1], denom[:, u % 4:u % 4 + 1]).then_inc(rden_ok, 1)
                    dve.wait_ge(pv_pe, 16 * jp + u + 1)
                    dve.wait_ge(rden_ok, 16 * (jp - 6) + u + 1)
                    nc.vector.tensor_scalar(y_pair[:, q, a * E:(a + 1) * E], src, rden[:, u % 4:u % 4 + 1], None,
                                            ALU.mult).then_inc(y_ok, 1)
                else:
                    dve.wait_ge(pv_pe, 16 * jp + u + 1)
                    nc.vector.tensor_copy(rec[jp % 2][:, q, a * UW:a * UW + E], src).then_inc(y_ok, 1)

            norm(0)
            norm(1)
            norm(2)
            if not early:
                norm(3)
            minimum(0)
            minimum(1)
            if early:
                norm(3)
            for u in range(16):
                copies(u)
                if u == 2 and j + 1 < len(jobs):
                    dve_split(dve, j + 1)
                if u:
                    result(u - 1)
                if u + 2 < 16:
                    minimum(u + 2)
            result(15)
        def g_sources(f):
            c = slice(f * P, (f + 1) * P)
            return [(0, g_raw[0][:, :, :], w_in_v[:, :, OFF_GA + f * P:OFF_GA + (f + 1) * P]),
                    (1, g_raw[1][:, :, :], w_in_v[:, :, OFF_GB + f * P:OFF_GB + (f + 1) * P]),
                    (2, g_raw[2][:, 0:4, :], w_a.rearrange("(k p) n -> p k n", p=P)[:, :, c]),
                    (2, g_raw[2][:, 4:6, :], w_b.rearrange("(k p) n -> p k n", p=P)[:, :, c])]

        def g_split_hi(f, i):
            A.wait_ge(g_ld[i], (32 if i == 2 else 16) * (f + 1))
            if f:
                A.wait_ge(gate_pe, 8 * (f - 1) + (8 if i == 2 else 5 + i))
            else:
                A.wait_ge(proj_pe, 40)
            A.activation(g_hi[i][:, :, :], g_raw[i][:, :, :], ACT.Copy).then_inc(g_hi_ok, 1)

        def g_split_lo(f, i):
            V.wait_ge(g_hi_ok, 3 * f + i + 1)
            V.tensor_tensor(g_lo[i][:, :, :], g_raw[i][:, :, :], g_hi[i][:, :, :].bitcast(F32),
                            ALU.subtract).then_inc(g_lo_ok, 1)

        def at_start(b):
            return type(b) is int and b == 0

        def loads_before(step, at):
            n = 2 * step + at // 3 + 1
            return n if at % 3 == 0 or at_start(step) else n - 1

        def chunk_hi(step, i, place=None, first=False):
            place = i if place is None else place
            A.wait_ge(e_ld[place % 3], 16 * loads_before(step, place))
            if not first:
                A.wait_ge(e_used, 6 * (step - 1) + i + 1)
            A.activation(e_hi[i][:, :, :], e_raw[place % 3][:, :, :], ACT.Copy).then_inc(
                e_hi_ok, 3 if first and i == 3 else 1)

        def chunk_lo(step, i, place=None, first=False):
            place = i if place is None else place
            V.wait_ge(e_hi_ok, 6 * step + place + 1)
            V.tensor_tensor(e_lo[i][:, :, :], e_raw[place % 3][:, :, :], e_hi[i][:, :, :].bitcast(F32),
                            ALU.subtract).then_inc(e_lo_ok, 3 if first and i == 3 else 1)

        def chunk_load(sp, step, place, src):
            if not at_start(step) or place == 3:
                sp.wait_ge(e_lo_ok, 6 * step + place - 2)
            sp.dma_start(e_raw[place % 3][:, :, :], src).then_inc(e_ld[place % 3], 16)

        def three(dst, lhs, rhs, first, last):
            for n, (a, b) in enumerate(((0, 0), (0, 1), (1, 0))):
                mm = nc.tensor.matmul(dst, lhs[a], rhs[b], start=first and n == 0, stop=last and n == 2)
            return mm

        def pe_up(e, which, first=False):
            if which == 0:
                nc.tensor.wait_ge(xT_lo_ok, e + 1)
            if not first:
                nc.tensor.wait_ge(act_ok, e)
            for i in range(2):
                c = 2 * which + i
                nc.tensor.wait_ge(e_lo_ok, 6 * e + c + 1)
                for kk in range(4):
                    k = 4 * i + kk
                    mm = three(bank[:, which, :], (xT_hi[:, k, :], xT_lo[:, k, :]),
                               (e_hi[c][:, kk, :], e_lo[c][:, kk, :]), k == 0, k == KT - 1)
                mm.then_inc(e_used, 3 if first and c == 3 else 1)

        def pe_turn_act(b):
            nc.tensor.wait_ge(act_ok, b + 1)
            for k in range(4):
                mm = nc.tensor.transpose(bank[:, 4, k * P:(k + 1) * P], act_in[:, k * P:(k + 1) * P], ident)
            mm.then_inc(actT_pe, 1)

        def pe_turn_x(b):
            nc.tensor.wait_ge(xg_ld, 16 * (b + 1))
            for k in range(KT):
                mm = nc.tensor.transpose(bank[:, 5 + k // 4, k % 4 * P:(k % 4 + 1) * P], xg[:, k * P:(k + 1) * P], ident)
            mm.then_inc(xgT_pe, 1)

        def pe_down(b, place=4):
            nc.tensor.wait_ge(aT_lo_ok, b + 1)
            if not at_start(b):
                nc.tensor.wait_ge(ye_act, b)
                nc.tensor.wait_ge(ye_dve, b)
            for half in range(2):
                c = 4 + half
                nc.tensor.wait_ge(e_lo_ok, 6 * (b + 1) + place + half + 1)
                for k in range(4):
                    mm = three(bank[:, 2 + half, :], (aT_hi[:, k, :], aT_lo[:, k, :]),
                               (e_hi[c][:, k, :], e_lo[c][:, k, :]), k == 0, k == 3)
                mm.then_inc(e_used, 1)

        def act_xmod(b, first=False):
            A.wait_ge(xgT_pe, b + 1)
            if not first:
                A.wait_ge(xT_lo_ok, b)
            for k in range(KT):
                last = A.activation(xT_f[:, k, :], bank[:, 5 + k // 4, k % 4 * P:(k % 4 + 1) * P], ACT.Identity,
                                    scale=scale2[:, k:k + 1], bias=mod[:, 24 + k:25 + k])
            last.then_inc(xmod_ok, 1)

        def act_xT(b, first=False):
            A.wait_ge(xmod_ok, b + 1)
            if not first:
                A.wait_ge(e_used, 6 * (b - 1) + 4)
            A.activation(xT_hi[:, :, :], xT_f[:, :, :], ACT.Copy).then_inc(xT_hi_ok, 1)

        def dve_xT(b):
            V.wait_ge(xT_hi_ok, b + 1)
            V.tensor_tensor(xT_lo[:, :, :], xT_f[:, :, :], xT_hi[:, :, :].bitcast(F32),
                            ALU.subtract).then_inc(xT_lo_ok, 1)

        def act_sig(e, first=False):
            A.wait_ge(e_used, 6 * e + 2)
            if not first:
                A.wait_ge(act_ok, e)
            A.activation(gate_act[:, :], bank[:, 0, :], ACT.Exp, scale=-1.0).then_inc(sig_e, 1)

        def dve_silu(e):
            V.wait_ge(sig_e, e + 1)
            V.tensor_scalar(gate_act[:, :], gate_act[:, :], 1.0, None, ALU.add).then_inc(silu_v, 1)
            V.wait_ge(silu_v, 3 * e + 1)
            V.reciprocal(gate_act[:, :], gate_act[:, :]).then_inc(silu_v, 1)
            V.wait_ge(silu_v, 3 * e + 2)
            V.tensor_tensor(gate_act[:, :], gate_act[:, :], bank[:, 0, :], ALU.mult).then_inc(silu_v, 1)

        def dve_act(e, first=False):
            V.wait_ge(silu_v, 3 * e + 3)
            V.wait_ge(e_used, 6 * e + 4)
            if not first:
                V.wait_ge(actT_pe, e)
            V.tensor_tensor(act_in[:, :], gate_act[:, :], bank[:, 1, :], ALU.mult).then_inc(act_ok, 1)

        def act_aT(b):
            A.wait_ge(actT_pe, b + 1)
            if not at_start(b):
                A.wait_ge(e_used, 6 * b + 6)
            A.activation(aT_hi[:, :, :], bank[:, 4, :].rearrange("p (k n) -> p k n", n=P), ACT.Copy).then_inc(aT_hi_ok, 1)

        def dve_aT(b):
            V.wait_ge(aT_hi_ok, b + 1)
            V.tensor_tensor(aT_lo[:, :, :], bank[:, 4, :].rearrange("p (k n) -> p k n", n=P),
                            aT_hi[:, :, :].bitcast(F32), ALU.subtract).then_inc(aT_lo_ok, 1)

        def act_y(b, place=4):
            if not at_start(b):
                A.wait_ge(ye_st, 16 * b)
            A.wait_ge(e_used, 6 * (b + 1) + place + 1)
            A.activation(y_e[:, 0:HALF], bank[:, 2, :], ACT.Copy).then_inc(ye_act, 1)

        def dve_y(b, place=4):
            if not at_start(b):
                V.wait_ge(ye_st, 16 * b)
            V.wait_ge(e_used, 6 * (b + 1) + place + 2)
            V.tensor_copy(y_e[:, HALF:D], bank[:, 3, :]).then_inc(ye_dve, 1)

        def store_y(b, signal=None):
            row = b * SLOTS
            A.wait_ge(ye_act, b + 1)
            A.wait_ge(ye_dve, b + 1)
            A.dma_start(d_y[bass.ds(row, SLOTS), :], y_e[:, :]).then_inc(signal or ye_st, 16)

        def act_step(e, last=False):
            first = at_start(e)
            if not last:
                chunk_hi(e + 1, 0)
                chunk_hi(e + 1, 1)
            if not first:
                act_aT(e - 1)
            if not last:
                act_xmod(e + 1)
            act_sig(e, first)
            if not last:
                chunk_hi(e + 1, 2)
                act_xT(e + 1)
                chunk_hi(e + 1, 3)
            if not first:
                act_y(e - 1)
            chunk_hi(e + 1, 4, 0 if last else None, first)
            chunk_hi(e + 1, 5, 1 if last else None, first)
            if not first:
                store_y(e - 1)

        def dve_step(e, last=False):
            first = at_start(e)
            if not last:
                chunk_lo(e + 1, 0)
                chunk_lo(e + 1, 1)
            if not first:
                dve_aT(e - 1)
            dve_silu(e)
            if not last:
                chunk_lo(e + 1, 2)
                dve_xT(e + 1)
            dve_act(e, first)
            if not last:
                chunk_lo(e + 1, 3)
            if not first:
                dve_y(e - 1)
            chunk_lo(e + 1, 4, 0 if last else None)
            chunk_lo(e + 1, 5, 1 if last else None)

        def pe_step(e, last=False):
            first = at_start(e)
            pe_up(e, 0, first)
            if not first:
                pe_turn_act(e - 1)
            if not last:
                pe_turn_x(e + 1)
            pe_up(e, 1, first)
            if not first:
                pe_down(e - 1)

        w1_v = w1.rearrange("e (k p) n -> (e k) p n", p=P)
        w3_v = w3.rearrange("e (k p) n -> (e k) p n", p=P)
        w2_v = w2.rearrange("e (k p) n -> (e k) p n", p=P)

        def sp_up(sp, step, expert, places=range(4)):
            for i in places:
                src = (w1_v, w3_v)[i // 2][bass.ds(expert * 8 + 4 * (i % 2), 4), :, :]
                chunk_load(sp, step, i, src.rearrange("k p n -> p k n"))

        def sp_down(sp, step, expert, place=4):
            for half in range(2):
                src = w2_v[bass.ds(expert * 4, 4), :, half * HID:(half + 1) * HID]
                chunk_load(sp, step, place + half, src.rearrange("k p n -> p k n"))

        def pool_index(pool, b, first=False):
            if not first:
                pool.wait_ge(xgT_pe, b)
            pool.tensor_copy(idx_now[:, :], slot_tok[:, bass.ds(b, 1)]).then_inc(idx_ok, 1)
            pool.wait_ge(idx_ok, b + 1)

        def pool_gather(pool):
            pool.indirect_dma_start(xg[:, :], None, d_xn, bass.IndirectOffsetOnAxis(ap=idx_now[:, :], axis=0)).then_inc(xg_ld, 16)

        def bc(ap, axis, shape):
            return ap.unsqueeze(axis).to_broadcast([P] + shape)

        def pick(dst, scores, top, priority, groups):
            link_v(V.tensor_reduce(top[:, :], scores, AX.X, ALU.max))
            link_v(V.tensor_tensor(dst[:, :, :], scores, bc(top[:, :], 2, [NT, groups]), ALU.is_equal))
            link_v(V.tensor_tensor(dst[:, :, :], dst[:, :, :], bc(priority, 1, [NT, groups]), ALU.mult))
            link_v(V.tensor_reduce(e_first[:, :], dst[:, :, :], AX.X, ALU.max))
            link_v(V.tensor_tensor(dst[:, :, :], dst[:, :, :], bc(e_first[:, :], 2, [NT, groups]), ALU.is_equal))

        def dve_route():
            row = lambda at, n: consts[:, K_ROW + at:K_ROW + at + n]
            G, EG = N_GROUPS, PER_GROUP
            V.wait_ge(rt_pe, 1)
            link_v(V.tensor_tensor(lg[:, :, :], bank[:, 4, 0:NT * N_ROUTE].rearrange("p (t n) -> p t n", t=NT),
                                   bc(brr[:, :], 1, [NT, N_ROUTE]), ALU.add))
            gl = lg[:, :, 0:G]
            el = lg[:, :, G:].rearrange("p t (g e) -> p t g e", g=G)
            pick(g_hot, gl, g_max, row(R_PRI4, G), G)
            V.tensor_tensor(g_ex[:, :, :], gl, bc(g_max[:, :], 2, [NT, G]), ALU.subtract).then_inc(r_d, 1)
            pr = r_prod[:, :, :].rearrange("p t (g e) -> p t g e", g=G)
            link_v(V.tensor_tensor(pr, el, bc(g_hot[:, :, :], 3, [NT, G, EG]), ALU.mult))
            link_v(V.tensor_reduce(e_in[:, :, :], r_prod[:, :, :].rearrange("p t (g e) -> p t e g", g=G), AX.X, ALU.add))
            pick(hot1, e_in[:, :, :], m_one, row(R_PRI8, EG), EG)
            link_v(V.tensor_scalar(e_next[:, :, :], hot1[:, :, :], -3e38, None, ALU.mult))
            link_v(V.tensor_tensor(e_next[:, :, :], e_next[:, :, :], e_in[:, :, :], ALU.add))
            pick(hot2, e_next[:, :, :], m_two, row(R_PRI8, EG), EG)
            V.tensor_tensor(m_ex[:, :], m_two[:, :], m_one[:, :], ALU.subtract).then_inc(r_d, 1)
            link_v(V.tensor_tensor(e_eq[:, :, :], hot1[:, :, :], hot2[:, :, :], ALU.add))
            for g in range(G):
                last = V.tensor_tensor(r_mask[:, :, g * EG:(g + 1) * EG], e_eq[:, :, :],
                                       bc(g_hot[:, :, g], 2, [NT, EG]), ALU.mult)
            last.then_inc(r_d, 1)
            V.wait_ge(r_a, 2)
            link_v(V.tensor_reduce(g_sum[:, :], g_ex[:, :, :], AX.X, ALU.add))
            link_v(V.tensor_scalar(m_r[:, :], m_ex[:, :], 1.0, None, ALU.add))
            link_v(V.tensor_tensor(m_r[:, :], m_r[:, :], g_sum[:, :], ALU.mult))
            link_v(V.reciprocal(wts[:, 0:NT], m_r[:, :]))
            link_v(V.tensor_tensor(wts[:, NT:], wts[:, 0:NT], m_ex[:, :], ALU.mult))
            V.memset(before[:, 0, :], 0.0).then_inc(r_d, 1)
            V.wait_ge(r_d, 4)
            V.wait_ge(rank_pe, 1)
            tot = bank[:, 6, 0:NT * N_EXP].rearrange("p (t e) -> p t e", t=NT)
            for t in range(1, NT):
                link_v(V.tensor_tensor(before[:, t, :], before[:, t - 1, :], tot[:, t - 1, :], ALU.add))
            link_v(V.tensor_tensor(rank[:, :, :], bank[:, 5, 0:NT * N_EXP].rearrange("p (t e) -> p t e", t=NT),
                                   before[:, :, :], ALU.add))
            link_v(V.tensor_tensor(over[0][:, :], before[:, NT - 1, :], tot[:, NT - 1, :], ALU.add))
            link_v(V.tensor_scalar(over[0][:, :], over[0][:, :], 1.0, -1.0, ALU.max, ALU.add))
            link_v(V.tensor_copy(c_int[:, :], over[0][:, :]))
            link_v(V.tensor_scalar(c_int[:, :], c_int[:, :], 7, None, ALU.arith_shift_right))
            link_v(V.tensor_copy(over[0][:, :], c_int[:, :]))
            link_v(V.tensor_copy(over[1][:, :], over[0][:, :]))
            src, dst = 1, 2
            for s in (1, 2, 4, 8, 16):
                V.tensor_copy(over[dst][:, 0:s], over[src][:, 0:s])
                link_v(V.tensor_tensor(over[dst][:, s:], over[src][:, s:], over[src][:, 0:N_EXP - s], ALU.add))
                src, dst = dst, src
            upto, spare = over[src], over[dst]
            link_v(V.tensor_tensor(exp_cmp[:, :, :], upto[0:1, :].unsqueeze(1).to_broadcast([1, N_OVER, N_EXP]),
                                   row(R_I16, N_OVER)[0:1, :].unsqueeze(2).to_broadcast([1, N_OVER, N_EXP]), ALU.is_le))
            link_v(V.tensor_reduce(exp_of[:, :], exp_cmp[:, :, :], AX.X, ALU.add))
            link_v(V.tensor_scalar(exp_of[:, :], exp_of[:, :], N_EXP - 1.0, None, ALU.min))
            V.tensor_copy(blk_exp[0:1, 0:N_EXP], row(R_BID, N_EXP)[0:1, :])
            V.tensor_copy(blk_exp[0:1, N_EXP:MAX_BLK], exp_of[:, :])
            link_v(V.tensor_scalar(blk_exp[0:1, MAX_BLK:MAX_BLK + 1], upto[0:1, N_EXP - 1:N_EXP], N_EXP - 3.0, None, ALU.add))
            link_v(V.tensor_tensor(spare[:, :], upto[:, :], over[0][:, :], ALU.subtract))
            link_v(V.scalar_tensor_tensor(out=spare[:, :], in0=spare[:, :], scalar=N_EXP - 1.0, in1=row(R_I32, N_EXP),
                                          op0=ALU.add, op1=ALU.subtract))
            link_v(V.tensor_copy(r_int[:, :, :], rank[:, :, :]))
            link_v(V.tensor_scalar(r_int[:, :, :], r_int[:, :, :], 7, None, ALU.arith_shift_right))
            link_v(V.tensor_copy(r_prod[:, :, :], r_int[:, :, :]))
            link_v(V.scalar_tensor_tensor(out=rank[:, :, :], in0=r_prod[:, :, :], scalar=-float(SLOTS), in1=rank[:, :, :],
                                          op0=ALU.mult, op1=ALU.add))
            link_v(V.tensor_tensor(r_blk[:, :, :], r_prod[:, :, :], bc(spare[:, :], 1, [NT, N_EXP]), ALU.add))
            link_v(V.scalar_tensor_tensor(out=r_blk[:, :, :], in0=r_prod[:, :, :], scalar=0.0, in1=r_blk[:, :, :],
                                          op0=ALU.is_gt, op1=ALU.mult))
            link_v(V.tensor_tensor(r_blk[:, :, :], r_blk[:, :, :], bc(row(R_I32, N_EXP), 1, [NT, N_EXP]), ALU.add))
            link_v(V.scalar_tensor_tensor(out=r_prod[:, :, :], in0=r_blk[:, :, :], scalar=float(SLOTS), in1=rank[:, :, :],
                                          op0=ALU.mult, op1=ALU.add))
            link_v(V.scalar_tensor_tensor(out=rank[:, :, :], in0=rank[:, :, :], scalar=float(MAX_BLK), in1=r_blk[:, :, :],
                                          op0=ALU.mult, op1=ALU.add))
            for k, hot in enumerate((hot1, hot2)):
                for g in range(G):
                    last = V.tensor_tensor(r_mask[:, :, g * EG:(g + 1) * EG], hot[:, :, :],
                                           bc(g_hot[:, :, g], 2, [NT, EG]), ALU.mult)
                link_v(last)
                for value, to in ((rank, sidx_f), (r_prod, dest_f)):
                    link_v(V.tensor_tensor(r_blk[:, :, :], r_mask[:, :, :], value[:, :, :], ALU.mult))
                    link_v(V.tensor_reduce(to[:, k * NT:(k + 1) * NT], r_blk[:, :, :], AX.X, ALU.add))
            V.tensor_copy(sidx[:, :], sidx_f[:, :])
            V.tensor_copy(dest[:, :], dest_f[:, :]).then_inc(dest_ok, 1)

        def h2_evac_act(n):
            half, f = n // KT, n % KT
            A.wait_ge(h2_pe, n + 1)
            A.activation(h2T[:, f, half * HALF:(half + 1) * HALF], bank[:, n % 4, :], ACT.Identity,
                         scale=scale2[:, f:f + 1], bias=mod[:, 24 + f:25 + f]).then_inc(h2_act, 1)

        links = {"a": 0, "v": 0}

        def link_a(ins):
            links["a"] += 1
            ins.then_inc(chain_a, 1)
            nc.scalar.wait_ge(chain_a, links["a"])

        def link_v(ins):
            links["v"] += 1
            ins.then_inc(chain_v, 1)
            nc.vector.wait_ge(chain_v, links["v"])

        V = nc.vector
        A = nc.scalar

        def merge_dve(half):
            V.wait_ge(mrec_ld, 48 * (half + 1))
            nm = [mrec[:, :, g, :, E + 1] for g in range(NG)]
            den = [mrec[:, :, g, :, E] for g in range(NG)]
            link_v(V.tensor_tensor(msm[:, 0, :, :], nm[0], nm[1], ALU.min))
            link_v(V.tensor_tensor(msm[:, 0, :, :], msm[:, 0, :, :], nm[2], ALU.min))
            for g in range(NG):
                last = V.tensor_tensor(msm[:, 1 + g, :, :], msm[:, 0, :, :], nm[g], ALU.subtract)
            last.then_inc(mrg_d, 1)
            V.wait_ge(mrg_e, half + 1)
            for g in range(NG):
                last = V.tensor_tensor(msm[:, 7 + g, :, :], msm[:, 4 + g, :, :], den[g], ALU.mult)
            link_v(last)
            link_v(V.tensor_tensor(msm[:, 10, :, :], msm[:, 7, :, :], msm[:, 8, :, :], ALU.add))
            link_v(V.tensor_tensor(msm[:, 10, :, :], msm[:, 10, :, :], msm[:, 9, :, :], ALU.add))
            link_v(V.reciprocal(msm[:, 11, :, :], msm[:, 10, :, :]))
            for g in range(NG):
                last = V.tensor_tensor(msm[:, 7 + g, :, :], msm[:, 4 + g, :, :], msm[:, 11, :, :], ALU.mult)
            link_v(last)
            if half:
                V.wait_ge(mrg_pe, 1)
            for g in range(NG):
                w = msm[:, 7 + g, :, :].unsqueeze(3).to_broadcast([P, 4, 4, E])
                last = V.tensor_tensor(macc[1 if g else 0][:, :, :, :], mrec[:, :, g, :, 0:E], w, ALU.mult)
                if g:
                    link_v(last)
                    last = V.tensor_tensor(macc[0][:, :, :, :], macc[0][:, :, :, :], macc[1][:, :, :, :], ALU.add)
                if g < NG - 1:
                    link_v(last)
            last.then_inc(mrg_y, 1)

        def merge_act(half):
            A.wait_ge(mrg_d, half + 1)
            A.activation(msm[:, 4:7, :, :], msm[:, 1:4, :, :], ACT.Exp).then_inc(mrg_e, 1)

        def merge_turn(half):
            pe = nc.tensor
            pe.wait_ge(mrg_y, half + 1)
            if half:
                pe.wait_ge(mrg_ev, 1)
            else:
                pe.wait_ge(pT_act, gbase[6] // 2)
                pe.wait_ge(pT_dve, gbase[6] // 2)
            y = macc[0][:, :, :, :].rearrange("p t h e -> p t (h e)")
            for f in range(2):
                for t in range(4):
                    mm = pe.transpose(bank[:, 5 + f, t * P:(t + 1) * P], y[:, t, f * P:(f + 1) * P], ident)
            mm.then_inc(mrg_pe, 1)

        def merge_out(half):
            A.wait_ge(mrg_pe, half + 1)
            for f in range(2):
                last = A.activation(y_f[:, 4 + f, half * HALF:(half + 1) * HALF], bank[:, 5 + f, :], ACT.Copy)
            last.then_inc(mrg_ev, 1)

        @block.sync
        def _(sp):
            for t in range(NT):
                sp.dma_start(xt[:, t, :], x[t * P:(t + 1) * P, :]).then_inc(tile_ld[t], 16)
            for n in range(24):
                if n >= 4:
                    sp.wait_ge(ada_pe, n - 3)
                sp.dma_start(ada_w[n % 4][:, :, :],
                             w_ada.rearrange("(k p) n -> p k n", p=P)[:, :, n * 256:(n + 1) * 256]).then_inc(ada_ld[n % 4], 16)
            sp.wait_ge(ada_pe, 24)
            for j in range(len(jobs) + 1):
                if j < len(jobs):
                    for i, (raw, src) in enumerate(raw_parts(j)):
                        if j:
                            sp.wait_ge(w_lo_ok, 2 * j)
                        sp.dma_start(raw, src).then_inc(w_ld[i], 16)
                if 1 <= j <= J_FOX and jobs[j - 1][0] == "qk":
                    jp = (j - 1) // 3 * 2 + (j - 1) % 3 - 1
                    g, h0 = jp // 2, 2 * (jp % 2)
                    sp.wait_ge(y_ok, 16 * (jp + 1))
                    sp.wait_ge(exp_ok, 16 * (jp + 1))
                    dst = d_rec[g, :, h0 * UW:(h0 + 2) * UW]
                    for q in range(NT):
                        o = (q * P, q // 2 + 512 * (q % 2), q)[g]
                        n = ORDER_STEP[g]
                        sp.dma_start(dst[o:min(o + n * P, T):n, :], rec[jp % 2][:, q, :]).then_inc(rec_st[jp % 2], 16)
                if j == J_FOX + 1:
                    sp.wait_ge(rec_st[0], 128 * NG)
                    sp.wait_ge(rec_st[1], 128 * NG)
                    for half in range(2):
                        if half:
                            sp.wait_ge(mrg_y, 1)
                        for g in range(NG):
                            src = d_rec[g, half * HALF:(half + 1) * HALF, :].rearrange("(t p) w -> p t w", p=P)
                            sp.dma_start(mrec[:, :, g, :, :].rearrange("p t h w -> p t (h w)"), src).then_inc(mrec_ld, 16)
                if j == J_FOX + 2:
                    sp.wait_ge(cumT_ev, 1)
                    sp.dma_start(d_cum, cumT[:, :]).then_inc(cum_st, 16)
                    sp.wait_ge(cum_st, 16)
                if j >= J_FOX + 2 and j < len(jobs):
                    p = j - J_FOX - 2
                    sp.wait_ge(min_ok, 16 * (6 + p))
                    sp.dma_start(cum_row[:, :, :].rearrange("p h t -> p (h t)"),
                                 d_cum[16 * p:16 * p + 16, :].rearrange("a b -> (a b)").partition_broadcast(P)).then_inc(cum_ld, 16)
            sp.wait_ge(proj_pe, 40)
            for f in range(KT):
                for i, raw, src in g_sources(f):
                    if f:
                        sp.wait_ge(g_lo_ok, 3 * (f - 1) + i + 1)
                    sp.dma_start(raw, src).then_inc(g_ld[i], 16)
                if f == 0:
                    sp.wait_ge(modT_ok, 1)
                    sp.dma_start(d_mod, mod_rows[:, :]).then_inc(mod_st, 16)
                    sp.wait_ge(mod_st, 16)
                    sp.wait_ge(min_ok, 160)
                    for i, r in enumerate((16, 40)):
                        sp.dma_start(gate_row[i][:, :], d_mod[r:r + 8, :].rearrange("a b -> (a b)").partition_broadcast(P)).then_inc(gate_ld, 16)
            sp.wait_ge(gate_pe, 64)
            for cc in range(3):
                sp.dma_start(o_raw[cc][:, :, :], w_out.rearrange("(k p) n -> p k n", p=P)[:, :, cc * OC:(cc + 1) * OC]).then_inc(o_ld[cc], 16)
            sp.wait_ge(merged_ok, 16)
            sp.dma_start(x2[:, :, :], x.rearrange("(t p) n -> p t n", p=P)).then_inc(x2_ld, 16)
            sp.wait_ge(o_lo_ok, 1)
            sp.dma_start(o_raw[0][:, :, :], w_out.rearrange("(k p) n -> p k n", p=P)[:, :, 3 * OC:4 * OC]).then_inc(o_ld[0], 16)
            sp.wait_ge(o_lo_ok, 3)
            sp.dma_start(w_rt[:, :, 0:N_GROUPS], w_rg.rearrange("(k p) n -> p k n", p=P)).then_inc(rt_ld, 16)
            sp.dma_start(w_rt[:, :, N_GROUPS:], w_re.rearrange("(k p) n -> p k n", p=P)).then_inc(rt_ld, 16)
            for t in range(NT):
                sp.wait_ge(xn2_ok, t + 1)
                sp.dma_start(d_xn[t * P:(t + 1) * P, :], xn2[t % 4][:, :]).then_inc(xn_st[t % 4], 16)
            sp.wait_ge(o_pe, 32)
            sp_up(sp, 0, 0)
            sp_up(sp, 1, 1)
            sp_down(sp, 1, 0)
            sp.wait_ge(dest_ok, 1)
            more = sp.value_load(blk_exp[0:1, MAX_BLK:MAX_BLK + 1], min_val=N_EXP - 3, max_val=MAX_BLK - 4)
            with sp.Fori(0, more + 1) as i:
                up = sp.value_load(blk_exp[0:1, bass.ds(i + 2, 1)], min_val=0, max_val=N_EXP - 1)
                down = sp.value_load(blk_exp[0:1, bass.ds(i + 1, 1)], min_val=0, max_val=N_EXP - 1)
                sp_up(sp, i + 2, up)
                sp_down(sp, i + 2, down)
            final = sp.value_load(blk_exp[0:1, bass.ds(more + 2, 1)], min_val=0, max_val=N_EXP - 1)
            sp_down(sp, more + 3, final, 0)
            for t in range(NT):
                sp.wait_ge(f_pool, t + 1)
                sp.dma_start(out[t * P:(t + 1) * P, :], x2[:, t, :]).then_inc(out_st, 16)
            sp.wait_ge(out_st, 16 * NT)

        @block.gpsimd
        def _(pool):
            pool.memset(ones[:, :], 1.0).then_inc(pool_set, 1)
            pool.memset(eps_col[:, :], EPS).then_inc(pool_set, 1)
            pool.wait_ge(rel_ev, 1)
            for g in range(NG):
                pool.dma_start(d_rel[4 * g:4 * g + 4, :, :], relrow[:, g, :].unsqueeze(1).to_broadcast([4, P, 384])).then_inc(rel_st, 16)
            pool.wait_ge(rel_st, 48)
            row = P * 384
            for h in range(DIL_HEADS):
                if h < 8:
                    src = bass.AP(d_rel.tensor, offset=h * row + 127, ap=[[383, P], [1, 256]])
                    pool.dma_start(bias01[:, h, :], src).then_inc(bias_ld, 16)
                else:
                    src = bass.AP(d_rel.tensor, offset=h * row + 255, ap=[[383, P], [1, P]])
                    pool.dma_start(bias2[:, h - 8, :], src).then_inc(bias_ld, 16)
            pool.memset(slot_tok[:, :], 0)
            pool.iota(tok_id[:, :], pattern=[[P, NT]], base=0, channel_multiplier=1).then_inc(tok_ok, 1)
            pool.wait_ge(tok_ok, 1)
            slots_v = d_slot.rearrange("(p b) o -> p (b o)", b=MAX_BLK)
            pool.dma_start(slots_v, slot_tok[:, :]).then_inc(slot_z, 16)
            for i in range(N_OVER * SLOTS // T):
                row = N_EXP * SLOTS + i * T
                pool.dma_start(d_y[row:row + T, :], x).then_inc(slot_z, 16)
            pool.wait_ge(slot_z, 16 * (1 + N_OVER * SLOTS // T))
            pool.wait_ge(dest_ok, 1)
            for k in range(2):
                for t in range(NT):
                    i = k * NT + t
                    pool.indirect_dma_start(d_slot, bass.IndirectOffsetOnAxis(ap=sidx[:, i:i + 1], axis=0),
                                            tok_id[:, t:t + 1], None).then_inc(scat, 16)
            pool.wait_ge(scat, 16 * 2 * NT)
            pool.dma_start(slot_tok[:, :], slots_v).then_inc(slot_ld, 16)
            pool.wait_ge(slot_ld, 16)
            for i in range(4):
                pool.wait_ge(xn_st[i], 32)
            pool_index(pool, 0, first=True)
            pool_gather(pool)
            pool_index(pool, 1)
            pool_gather(pool)
            pool_index(pool, 2)
            more = pool.value_load(blk_exp[0:1, MAX_BLK:MAX_BLK + 1], min_val=N_EXP - 3, max_val=MAX_BLK - 4)
            with pool.Fori(0, more + 1) as i:
                pool_gather(pool)
                pool_index(pool, i + 3)
            pool.wait_ge(ye_end, 16)
            for t in range(NT):
                for k in range(2):
                    pool.indirect_dma_start(y_slot[2 * t + k][:, :], None, d_y,
                                            bass.IndirectOffsetOnAxis(ap=dest[:, k * NT + t:k * NT + t + 1], axis=0)).then_inc(slot_y[t], 16)
            for t in range(NT):
                pool.wait_ge(f_dve, 2 * t + 2)
                pool.tensor_tensor(x2[:, t, :], x2[:, t, :], y_sum[t % 4][:, :], ALU.add).then_inc(f_pool, 1)

        @block.scalar
        def _(act):
            act.add_instruction(mybir.InstLoadActFuncSet(name=nc.get_next_instruction_name(),
                                                         act_func_set_id=EXP_AND_LN, engine=act.engine))
            A.dma_start(consts[:, :], cst).then_inc(small_ld, 16)
            for r0, src in ((C_C, c.rearrange("(a b) -> a b", b=P)), (C_N1, n1.rearrange("(a b) -> a b", b=P)),
                            (C_N2, n2.rearrange("(a b) -> a b", b=P)), (C_BADA, b_ada.rearrange("(a b) -> a b", b=P)),
                            (C_QG, qg.rearrange("(a b) e -> a (b e)", b=2)), (C_KG, kg.rearrange("(a b) e -> a (b e)", b=2))):
                A.dma_start(rows[r0:r0 + src.shape[0], :], src).then_inc(small_ld, 16)
            A.dma_start(ohs[0:33, :], oh).then_inc(small_ld, 16)
            A.dma_start(tab[0:32, :], rel).then_inc(small_ld, 16)
            A.dma_start(bfr[:, :], b_f.partition_broadcast(P)).then_inc(small_ld, 16)
            A.dma_start(brr[:, 0:N_GROUPS], b_rg.partition_broadcast(P)).then_inc(small_ld, 16)
            A.dma_start(brr[:, N_GROUPS:], b_re.partition_broadcast(P)).then_inc(small_ld, 16)
            act.wait_ge(rowsT_pe, 1)
            A.activation(col[:, :], bank[:, 0, 0:N_ROWS], ACT.Copy).then_inc(col_ok, 1)
            act.wait_ge(col_ok, 1)
            A.activation(silu_t[:, :], col[:, C_C:C_C + KT], ACT.Exp, scale=-1.0).then_inc(silu_e, 1)
            act.wait_ge(pool_set, 2)
            for t in range(NT):
                act.wait_ge(tile_ld[t], 16)
                link_a(A.activation(junk[:, :], xt[:, t, :], ACT.Square, accum_out=ssq[:, t:t + 1]))
            link_a(A.activation(rstd[:, :], ssq[:, :], ACT.Ln, scale=1.0 / D, bias=eps_col[:, :]))
            A.activation(rstd[:, :], rstd[:, :], ACT.Exp, scale=-0.5).then_inc(rstd_ok, 1)
            act.wait_ge(scl_ok, 1)
            for n in range(2 * KT):
                f, half = n // 2, n % 2
                act.wait_ge(xT_pe, n + 1)
                if n >= 2:
                    act.wait_ge(h_lo_ok, n - 1)
                A.activation(h_tmp[n % 2][:, :], bank[:, n % 4, :], ACT.Identity, scale=scale1[:, f:f + 1],
                             bias=mod[:, f:f + 1]).then_inc(xT_act, 1)
            act_split(act, 0)
            vj = 0
            for j, (kind, _, _) in enumerate(jobs):
                if kind == "v":
                    ev_values(act, act_copy, j, vj, 0, v_ev_act)
                    vj += 1
                    if j >= J_FOX:
                        merge_act(j - J_FOX)
                    act_split(act, j + 1)
                    if j == J_FOX + 1:
                        merge_out(0)
                        act.wait_ge(fg_ok, 1)
                        link_a(A.activation(fg[3][:, :, :], fg[2][:, :, :], ACT.Exp, scale=-1.0))
                        A.activation(fg[4][:, :, :], fg[3][:, :, :], ACT.Ln, bias=ones[:, 0:1]).then_inc(fg_act, 1)
                        act.wait_ge(cumT_pe, 1)
                        A.activation(cumT[:, :], bank[0:64, 4, P:2 * P], ACT.Copy).then_inc(cumT_ev, 1)
                        merge_out(1)
                else:
                    jp = (j // 3 * 2 + j % 3 - 1) if j < J_FOX else j - J_FOX - 2 + 6
                    act_pair(act, jp, j)
            act.wait_ge(modT_pe, 1)
            A.activation(mod_rows[:, :], bank[0:48, 0, 0:P], ACT.Copy).then_inc(modT_ok, 1)
            for f in range(KT):
                g_split_hi(f, 0)
                g_split_hi(f, 1)
                if f == 0:
                    act.wait_ge(pv_pe, 160)
                    act.wait_ge(yT_ok, 8)
                    act.wait_ge(mrg_ev, 2)
                    for k in range(6):
                        A.activation(y_hi[:, k, :], y_f[:, k, :], ACT.Copy).then_inc(y_hi_ok, 1)
                g_split_hi(f, 2)
                for half in range(2):
                    n = 2 * f + half
                    act.wait_ge(gate_pe, 4 * n + 2)
                    if n >= 2:
                        act.wait_ge(merged_ok, n - 1)
                    A.activation(g_tmp[n % 2][:, :, :], bank[:, 4 * half:4 * half + 2, :], ACT.Exp, scale=-1.0).then_inc(gate_e, 1)
            act.wait_ge(gate_pe, 64)
            act.wait_ge(merged_ok, 16)
            act.wait_ge(o_ld[0], 16)
            A.activation(o_hi[0][:, :, :], o_raw[0][:, :, :], ACT.Copy).then_inc(o_hi_ok, 1)
            for k in range(KT):
                A.activation(m_hi[:, k, :], merged[:, k, :], ACT.Copy).then_inc(m_hi_ok, 1)
            for cc in range(1, 4):
                act.wait_ge(o_ld[cc % 3], 32 if cc == 3 else 16)
                if cc >= 2:
                    act.wait_ge(o_pe, 8 * (cc - 1))
                A.activation(o_hi[cc % 2][:, :, :], o_raw[cc % 3][:, :, :], ACT.Copy).then_inc(o_hi_ok, 1)
            for t in range(NT):
                act.wait_ge(o_done, 24 + t + 1)
                link_a(A.activation(o_junk[:, :], x2[:, t, :], ACT.Square, accum_out=ssq[:, t:t + 1]))
                link_a(A.activation(rstd[:, t:t + 1], ssq[:, t:t + 1], ACT.Ln, scale=1.0 / D, bias=eps_col[:, :]))
                A.activation(rstd[:, t:t + 1], rstd[:, t:t + 1], ACT.Exp, scale=-0.5).then_inc(rs2_ok, 1)
                if t >= 4:
                    for f in range(2 * (t - 4), 2 * (t - 4) + 2):
                        h2_evac_act(f)
            for n in range(NT, 2 * NT):
                h2_evac_act(n)
            act.wait_ge(r_d, 1)
            A.activation(g_ex[:, :, :], g_ex[:, :, :], ACT.Exp).then_inc(r_a, 1)
            act.wait_ge(r_d, 2)
            A.activation(m_ex[:, :], m_ex[:, :], ACT.Exp).then_inc(r_a, 1)
            act.wait_ge(o_pe, 32)
            for i in range(4):
                chunk_hi(0, i, first=True)
            act_xmod(0, first=True)
            act_xT(0, first=True)
            act_step(0)
            act_step(1)
            more = act.value_load(blk_exp[0:1, MAX_BLK:MAX_BLK + 1], min_val=N_EXP - 3, max_val=MAX_BLK - 4)
            with act.Fori(0, more) as i:
                act_step(i + 2)
            act_step(more + 2, last=True)
            act_aT(more + 2)
            act_y(more + 2, 0)
            store_y(more + 2, ye_end)
            for t in range(NT):
                act.wait_ge(slot_y[t], 32)
                A.activation(y_slot[2 * t][:, :], y_slot[2 * t][:, :], ACT.Copy, scale=wts[:, t:t + 1]).then_inc(f_act, 1)

        @block.vector
        def _(dve):
            dve.wait_ge(small_ld, 16 * N_SMALL)
            link_v(V.memset(tab[32:33, :], 1.0))
            V.tensor_copy(id_bf[:, :], ident).then_inc(bf_set, 1)
            V.tensor_copy(cm_bf[:, :], consts[:, K_CM:K_CM + P]).then_inc(bf_set, 1)
            dve.wait_ge(rel_pe, 1)
            V.tensor_copy(relrow[:, :, :], bank[0:4, 1:4, 0:384]).then_inc(rel_ev, 1)
            dve.wait_ge(silu_e, 1)
            link_v(V.tensor_scalar(silu_t[:, :], silu_t[:, :], 1.0, None, ALU.add))
            link_v(V.reciprocal(silu_t[:, :], silu_t[:, :]))
            V.tensor_tensor(silu_c[:, :], col[:, C_C:C_C + KT], silu_t[:, :], ALU.mult).then_inc(col_ok, 1)
            V.tensor_scalar(qgain[:, :], col[:, C_QG:C_QG + 10], -(E ** -0.5), None, ALU.mult).then_inc(col_ok, 1)
            dve.wait_ge(rstd_ok, 1)
            for t in range(NT):
                V.tensor_scalar(xt[:, t, :], xt[:, t, :], rstd[:, t:t + 1], None, ALU.mult).then_inc(xn_ok, 1)
            dve.wait_ge(ada_pe, 24)
            link_v(V.tensor_tensor(mod[:, :], bank[:, 7, 0:48], col[:, C_BADA:C_BADA + 48], ALU.add))
            V.scalar_tensor_tensor(out=scale2[:, :], in0=mod[:, 32:40], scalar=1.0, in1=col[:, C_N2:C_N2 + KT],
                                   op0=ALU.add, op1=ALU.mult)
            V.scalar_tensor_tensor(out=scale1[:, :], in0=mod[:, 8:16], scalar=1.0, in1=col[:, C_N1:C_N1 + KT],
                                   op0=ALU.add, op1=ALU.mult).then_inc(scl_ok, 1)
            for n in range(2 * KT):
                f, half = n // 2, n % 2
                t = slice(half * HALF, (half + 1) * HALF)
                dve.wait_ge(xT_act, n + 1)
                V.tensor_copy(h_hi[:, f, t], h_tmp[n % 2][:, :]).then_inc(h_hi_ok, 1)
                dve.wait_ge(h_hi_ok, n + 1)
                V.tensor_tensor(h_lo[:, f, t], h_tmp[n % 2][:, :], h_hi[:, f, t].bitcast(F32),
                                ALU.subtract).then_inc(h_lo_ok, 1)
            dve_split(dve, 0)
            dve.wait_ge(bias_ld, 16 * DIL_HEADS)
            vj = 0
            for j, (kind, _, _) in enumerate(jobs):
                if kind == "v":
                    ev_values(dve, V.tensor_copy, j, vj, 1, v_ev_dve)
                    vj += 1
                    if j >= J_FOX:
                        merge_dve(j - J_FOX)
                    dve_split(dve, j + 1)
                    if j == J_FOX + 1:
                        dve.wait_ge(v_ev_act, 20)
                        dve.wait_ge(v_ev_dve, 20)
                        link_v(V.tensor_tensor(fg[1][:, :, :], fg[0][:, :, :],
                                               bfr[:, :].unsqueeze(2).to_broadcast([P, FOX_HEADS, NT]), ALU.add))
                        V.scalar_tensor_tensor(out=fg[2][:, :, :], in0=fg[1][:, :, :], scalar=-1.0,
                                               in1=fg[1][:, :, :], op0=ALU.mult, op1=ALU.max).then_inc(fg_ok, 1)
                        dve.wait_ge(fg_act, 1)
                        V.scalar_tensor_tensor(out=fg[5][:, :, :], in0=fg[1][:, :, :], scalar=0.0, in1=fg[4][:, :, :],
                                               op0=ALU.min, op1=ALU.subtract).then_inc(fg_ok, 1)
                        dve.wait_ge(fg_ok, 2)
                        link_v(V.memset(fg[1][:, :, 0:1], 0.0))
                        dve.wait_ge(cum_pe, 1)
                        tot = bank[:, 4, 64:128].rearrange("p (h t) -> p h t", t=NT)
                        for t in range(1, NT):
                            link_v(V.tensor_tensor(fg[1][:, :, t:t + 1], fg[1][:, :, t - 1:t], tot[:, :, t - 1:t], ALU.add))
                        V.tensor_tensor(fg[2][:, :, :], bank[:, 4, 0:64].rearrange("p (h t) -> p h t", t=NT),
                                        fg[1][:, :, :], ALU.add).then_inc(cum_dve, 1)
                else:
                    jp = (j // 3 * 2 + j % 3 - 1) if j < J_FOX else j - J_FOX - 2 + 6
                    dve_pair(dve, jp, j)
            for f in range(KT):
                g_split_lo(f, 0)
                g_split_lo(f, 1)
                if f == 0:
                    for k in range(6):
                        dve.wait_ge(y_hi_ok, k + 1)
                        V.tensor_tensor(y_lo[:, k, :], y_f[:, k, :], y_hi[:, k, :].bitcast(F32),
                                        ALU.subtract).then_inc(y_lo_ok, 1)
                g_split_lo(f, 2)
                for half in range(2):
                    n = 2 * f + half
                    g = g_tmp[n % 2]
                    dve.wait_ge(gate_e, n + 1)
                    link_v(V.tensor_scalar(g[:, :, :], g[:, :, :], 1.0, None, ALU.add))
                    link_v(V.reciprocal(g[:, :, :], g[:, :, :]))
                    dve.wait_ge(gate_pe, 4 * n + 4)
                    link_v(V.tensor_tensor(g[:, :, :], g[:, :, :], bank[:, 4 * half + 2:4 * half + 4, :], ALU.mult))
                    V.tensor_tensor(merged[:, f, half * HALF:(half + 1) * HALF], g[:, 0, :], g[:, 1, :],
                                    ALU.add).then_inc(merged_ok, 1)
            dve.wait_ge(o_hi_ok, 1)
            V.tensor_tensor(o_lo[0][:, :, :], o_raw[0][:, :, :], o_hi[0][:, :, :].bitcast(F32), ALU.subtract).then_inc(o_lo_ok, 1)
            for k in range(KT):
                dve.wait_ge(m_hi_ok, k + 1)
                V.tensor_tensor(m_lo[:, k, :], merged[:, k, :], m_hi[:, k, :].bitcast(F32), ALU.subtract).then_inc(m_lo_ok, 1)
            dve.wait_ge(m_lo_ok, KT)
            for cc in range(4):
                if cc < 3:
                    dve.wait_ge(o_hi_ok, cc + 2)
                    V.tensor_tensor(o_lo[(cc + 1) % 2][:, :, :], o_raw[(cc + 1) % 3][:, :, :],
                                    o_hi[(cc + 1) % 2][:, :, :].bitcast(F32), ALU.subtract).then_inc(o_lo_ok, 1)
                if cc == 0:
                    dve.wait_ge(gate_ld, 32)
                    dve.wait_ge(x2_ld, 16)
                c = slice(cc * OC, (cc + 1) * OC)
                for t in range(NT):
                    dve.wait_ge(o_pe, 8 * cc + t + 1)
                    link_v(V.tensor_tensor(o_tmp[:, t % 2, :], bank[:, t, (cc % 2) * OC:(cc % 2 + 1) * OC], gate_row[0][:, c], ALU.mult))
                    V.tensor_tensor(x2[:, t, c], x2[:, t, c], o_tmp[:, t % 2, :], ALU.add).then_inc(o_done, 1)
            for t in range(NT):
                dve.wait_ge(rs2_ok, t + 1)
                if t >= 4:
                    dve.wait_ge(xn_st[t % 4], 16)
                    dve.wait_ge(h2_pe, 8)
                V.tensor_scalar(xn2[t % 4][:, :], x2[:, t, :], rstd[:, t:t + 1], None, ALU.mult).then_inc(xn2_ok, 1)
            dve_route()
            for i in range(4):
                chunk_lo(0, i, first=True)
            dve_xT(0)
            dve_step(0)
            dve_step(1)
            more = dve.value_load(blk_exp[0:1, MAX_BLK:MAX_BLK + 1], min_val=N_EXP - 3, max_val=MAX_BLK - 4)
            with dve.Fori(0, more) as i:
                dve_step(i + 2)
            dve_step(more + 2, last=True)
            dve_aT(more + 2)
            dve_y(more + 2, 0)
            for t in range(NT):
                dve.wait_ge(f_act, t + 1)
                dve.wait_ge(slot_y[t], 32)
                if t >= 4:
                    dve.wait_ge(f_pool, t - 3)
                V.scalar_tensor_tensor(out=y_sum[t % 4][:, :], in0=y_slot[2 * t + 1][:, :], scalar=wts[:, NT + t:NT + t + 1],
                                       in1=y_slot[2 * t][:, :], op0=ALU.mult, op1=ALU.add).then_inc(f_dve, 1)
                dve.wait_ge(f_dve, 2 * t + 1)
                V.tensor_tensor(y_sum[t % 4][:, :], y_sum[t % 4][:, :], gate_row[1][:, :], ALU.mult).then_inc(f_dve, 1)

        @block.tensor
        def _(pe):
            pe.wait_ge(small_ld, 16 * N_SMALL)
            nc.tensor.transpose(bank[:, 0, 0:N_ROWS], rows[0:N_ROWS, :], ident[0:N_ROWS, 0:N_ROWS]).then_inc(rowsT_pe, 1)
            pe.wait_ge(pool_set, 2)
            pe.wait_ge(chain_v, 1)
            for g in range(NG):
                mm = nc.tensor.matmul(bank[0:4, 1 + g, 0:384], tab[0:33, 4 * g:4 * g + 4],
                                      ohs[0:33, g * 384:(g + 1) * 384], start=True, stop=True)
            mm.then_inc(rel_pe, 1)
            pe.wait_ge(col_ok, 2)
            for n in range(24):
                pe.wait_ge(ada_ld[n % 4], 16 * (n // 4 + 1))
                for i in range(2):
                    for k in range(KT):
                        mm = nc.tensor.matmul(bank[:, 7, 2 * n + i:2 * n + i + 1], ada_w[n % 4][:, k, i * P:(i + 1) * P],
                                              silu_c[:, k:k + 1], start=(k == 0), stop=(k == KT - 1))
                mm.then_inc(ada_pe, 1)
            pe.wait_ge(xn_ok, NT)
            pe.wait_ge(rel_ev, 1)
            for n in range(2 * KT):
                f, half = n // 2, n % 2
                if n >= 4:
                    pe.wait_ge(xT_act, n - 3)
                for t in range(4):
                    mm = nc.tensor.transpose(bank[:, n % 4, t * P:(t + 1) * P], xt[:, 4 * half + t, f * P:(f + 1) * P], ident)
                mm.then_inc(xT_pe, 1)
            pe.wait_ge(h_lo_ok, 2 * KT)
            pe.wait_ge(bf_set, 2)
            vj = 0
            for j, (kind, _, _) in enumerate(jobs):
                if kind == "v":
                    pe_values(pe, j, vj, j // 3 if j < J_FOX else -1)
                    vj += 1
                    if j == J_FOX + 1:
                        merge_turn(0)
                        pe.wait_ge(fg_ok, 2)
                        nc.tensor.matmul(bank[:, 4, 0:64], tri_incl, fg[5][:, :, :].rearrange("p h t -> p (h t)"),
                                         start=True, stop=True)
                        nc.tensor.matmul(bank[:, 4, 64:128], ones[:, :], fg[5][:, :, :].rearrange("p h t -> p (h t)"),
                                         start=True, stop=True).then_inc(cum_pe, 1)
                        pe.wait_ge(cum_dve, 1)
                        nc.tensor.transpose(bank[0:64, 4, P:2 * P], fg[2][:, :, :].rearrange("p h t -> p (h t)"),
                                            ident).then_inc(cumT_pe, 1)
                        merge_turn(1)
                        pe.wait_ge(mrg_ev, 2)
                else:
                    jp = (j // 3 * 2 + j % 3 - 1) if j < J_FOX else j - J_FOX - 2 + 6
                    pe_pair(pe, jp, j)
            pe.wait_ge(min_ok, 160)
            nc.tensor.transpose(bank[0:48, 0, 0:P], mod[:, :], ident).then_inc(modT_pe, 1)
            pe.wait_ge(modT_ok, 1)
            pe.wait_ge(y_ok, 160)
            pe.wait_ge(yT_ok, 8)
            for f in range(KT):
                for half in range(2):
                    n = 2 * f + half
                    t = slice(half * HALF, (half + 1) * HALF)
                    if n >= 2:
                        pe.wait_ge(merged_ok, n - 1)
                    for i in range(2):
                        pe.wait_ge(g_lo_ok, 3 * f + i + 1)
                        for k in range(KT):
                            mm = three(bank[:, 4 * half + i, :], (g_hi[i][:, k, :], g_lo[i][:, k, :]),
                                       (h_hi[:, k, t], h_lo[:, k, t]), k == 0, k == KT - 1)
                        mm.then_inc(gate_pe, 1)
                    pe.wait_ge(g_lo_ok, 3 * f + 3)
                    for i, ks in enumerate((range(0, 4), range(4, 6))):
                        for k in ks:
                            if n == 0:
                                pe.wait_ge(y_lo_ok, k + 1)
                            mm = three(bank[:, 4 * half + 2 + i, :], (g_hi[2][:, k, :], g_lo[2][:, k, :]),
                                       (y_hi[:, k, t], y_lo[:, k, t]), k == ks[0], k == ks[-1])
                        mm.then_inc(gate_pe, 1)
            pe.wait_ge(merged_ok, 16)
            pe.wait_ge(o_lo_ok, 1)
            for k in range(KT):
                pe.wait_ge(m_lo_ok, k + 1)
                for t in range(NT):
                    mm = three(bank[:, t, 0:OC], (m_hi[:, k, t * P:(t + 1) * P], m_lo[:, k, t * P:(t + 1) * P]),
                               (o_hi[0][:, k, :], o_lo[0][:, k, :]), k == 0, k == KT - 1)
                    if k == KT - 1:
                        mm.then_inc(o_pe, 1)
            for cc in range(1, 4):
                pe.wait_ge(o_lo_ok, cc + 1)
                for t in range(NT):
                    pe.wait_ge(o_done, 8 * (cc - 1) + t + 1)
                    for k in range(KT):
                        mm = three(bank[:, t, (cc % 2) * OC:(cc % 2 + 1) * OC],
                                   (m_hi[:, k, t * P:(t + 1) * P], m_lo[:, k, t * P:(t + 1) * P]),
                                   (o_hi[cc % 2][:, k, :], o_lo[cc % 2][:, k, :]), k == 0, k == KT - 1)
                    mm.then_inc(o_pe, 1)
            for n in range(2 * KT):
                half, f = n // KT, n % KT
                pe.wait_ge(xn2_ok, 4 * half + 4)
                if n < 4:
                    pe.wait_ge(o_done, 24 + n + 1)
                else:
                    pe.wait_ge(h2_act, n - 3)
                for t in range(4):
                    mm = nc.tensor.transpose(bank[:, n % 4, t * P:(t + 1) * P], xn2[t][:, f * P:(f + 1) * P], ident)
                mm.then_inc(h2_pe, 1)
            pe.wait_ge(h2_act, 16)
            pe.wait_ge(o_done, 32)
            pe.wait_ge(rt_ld, 32)
            for t in range(NT):
                for k in range(KT):
                    mm = nc.tensor.matmul(bank[:, 4, t * N_ROUTE:(t + 1) * N_ROUTE], h2T[:, k, t * P:(t + 1) * P],
                                          w_rt[:, k, :], start=(k == 0), stop=(k == KT - 1))
            mm.then_inc(rt_pe, 1)
            pe.wait_ge(r_d, 3)
            mask = r_mask[:, :, :].rearrange("p t e -> p (t e)")
            nc.tensor.matmul(bank[:, 5, 0:NT * N_EXP], tri_strict, mask, start=True, stop=True)
            nc.tensor.matmul(bank[:, 6, 0:NT * N_EXP], ones[:, :], mask, start=True, stop=True).then_inc(rank_pe, 1)
            pe.wait_ge(dest_ok, 1)
            pe_turn_x(0)
            pe_step(0)
            pe_step(1)
            more = pe.value_load(blk_exp[0:1, MAX_BLK:MAX_BLK + 1], min_val=N_EXP - 3, max_val=MAX_BLK - 4)
            with pe.Fori(0, more) as i:
                pe_step(i + 2)
            pe_step(more + 2, last=True)
            pe_turn_act(more + 2)
            pe_down(more + 2, 0)


def bucket_rows():
    import numpy as np

    half, far = 16, 2048
    hot = np.zeros((33, NG, 384), np.float32)
    for g, dil in enumerate(DILATION):
        for n in range(384):
            m = 255 - n
            if g == 2:
                m = m / 2 if m % 2 == 0 else -1
            if m < 0 or m > P:
                hot[32, g, n] = BIG
                continue
            dist = int(m * dil)
            if dist < half:
                b = dist
            else:
                big = np.log(np.float32(dist) / half) / np.log(far / half) * half
                b = min(half + int(np.float32(big)), 2 * half - 1)
            hot[b, g, n] = -1.0
    return hot.reshape(33, NG * 384)


def shape_constants():
    import numpy as np

    k = np.zeros((P, K_COLS), np.float32)
    i = np.arange(P)
    k[:, K_ID:K_ID + P] = np.eye(P)
    k[:, K_CM:K_CM + P] = np.where(i[None, :] > i[:, None], BIG, 0.0)
    k[:, K_BO:K_BO + P] = (i[None, :] // E == i[:, None] // E)
    k[:, K_TI:K_TI + P] = (i[:, None] <= i[None, :])
    k[:, K_TS:K_TS + P] = (i[:, None] < i[None, :])
    r = k[:, K_ROW:]
    r[:, R_PRI4:R_PRI4 + 4] = np.arange(4, 0, -1)
    r[:, R_PRI8:R_PRI8 + 8] = np.arange(8, 0, -1)
    r[:, R_I32:R_I32 + 32] = np.arange(32)
    r[:, R_I16:R_I16 + 16] = np.arange(16)
    r[:, R_BID:R_BID + MAX_BLK] = np.arange(MAX_BLK)
    return k


NAMES = ["x", "c", "rel_bias_table", "w_ada", "b_ada", "norm1_g", "w_in", "b_forget", "q_gain", "k_gain",
         "w_branch_a", "w_branch_b", "w_out", "norm2_g", "w_router_group", "b_router_group",
         "w_router_expert", "b_router_expert", "w1", "w3", "w2"]


def kernel(**inputs):
    import numpy as np
    import concourse.bacc as bacc
    from concourse.bass_utils import run_bass_kernel_spmd

    nc = bacc.Bacc("TRN2", target_bir_lowering=False, num_devices=1)
    arrays, args = {}, []
    for name in NAMES:
        a = np.ascontiguousarray(inputs[name])
        arrays[f"in_{name}"] = a.reshape(a.shape[1:]) if name != "rel_bias_table" else a
    arrays["shape_constants"] = shape_constants()
    arrays["bucket_rows"] = bucket_rows()
    for name, a in arrays.items():
        args.append(nc.dram_tensor(name, a.shape, mybir.dt.from_np(a.dtype), kind="ExternalInput").ap())
    args.append(nc.dram_tensor("out", (T, D), F32, kind="ExternalOutput").ap())
    build(nc, *args)
    r = run_bass_kernel_spmd(nc, [arrays], core_ids=[0])
    return np.asarray(r.results[0]["out"]).reshape(1, T, D)
```

```python
from contextlib import ExitStack

import concourse.bass as bass
from concourse import mybir
from concourse.alu_op_type import AluOpType as ALU

ACT = mybir.ActivationFunctionType
AX = mybir.AxisListType
F32 = mybir.dt.float32
F32R = mybir.dt.float32r
BF16 = mybir.dt.bfloat16
I32 = mybir.dt.int32
U32 = mybir.dt.uint32

P = 128
T = 1024
D = 1024
KT = D // P
NT = T // P
HALF = 512
E = 64
FOX_HEADS, DIL_HEADS, NG = 8, 12, 3
DILATION = (1, 4, 16)
ORDER_STEP = (1, 4, 8)
FOX_W, DIL_W = FOX_HEADS * E, DIL_HEADS * E
OFF_FQ, OFF_FK, OFF_FV = 0, FOX_W, 2 * FOX_W
OFF_DQ = 3 * FOX_W + FOX_HEADS
OFF_DK, OFF_DV = OFF_DQ + DIL_W, OFF_DQ + 2 * DIL_W
OFF_GA = OFF_DQ + 3 * DIL_W
OFF_GB = OFF_GA + D
N_GROUPS, PER_GROUP = 4, 8
N_EXP = N_GROUPS * PER_GROUP
HID = D // 2
N_ROUTE = N_GROUPS + N_EXP
SLOTS = 128
MAX_BLK = 48
N_OVER = MAX_BLK - N_EXP
UW = E + 2
BIG = 1e30
EXP_AND_LN = 6
N_ROWS_LD, N_SMALL = 7, 5
EPS = 1e-6
C_C, C_N1, C_N2, C_BADA, C_QG, C_KG, N_ROWS = 0, 8, 16, 24, 72, 82, 92
K_ID, K_CM, K_BO, K_TI, K_TS, K_ROW = 0, 128, 256, 384, 512, 640
R_PRI4, R_PRI8, R_I32, R_I16, R_BID = 0, 4, 12, 44, 60
K_COLS = K_ROW + R_BID + MAX_BLK


def build(nc, x, c, rel, w_ada, b_ada, n1, w_in, b_f, qg, kg, w_a, w_b, w_out, n2, w_rg, b_rg,
          w_re, b_re, w1, w3, w2, cst, oh, out):
    KB = 1024
    BASE = 16512
    RP, RA, RH, RB, RY, RW, RS, RK = (BASE + v * KB for v in (0, 15, 47, 111, 143, 167, 193, 201))

    ctx = ExitStack()
    with ctx:
        def at(name, shape, dt, offset):
            return nc.alloc_sbuf_tensor_at(name, shape, dt, offset=offset)

        def sems(text):
            return [ctx.enter_context(nc.semaphore(name)) for name in text.split()]

        def dram(name, shape, dt=F32):
            return nc.dram_tensor(name, shape, dt, kind="Internal").ap()

        cursor = [RP]

        def keep(name, cols, dt=F32):
            t = at(name, [P, cols], dt, cursor[0])
            cursor[0] += (cols * (2 if dt == BF16 else 4) + 31) // 32 * 32
            return t

        consts = keep("consts", K_COLS)
        ones = keep("ones", P)
        ident = consts[:, K_ID:K_ID + P]
        block_ones = consts[:, K_BO:K_BO + P]
        tri_incl = consts[:, K_TI:K_TI + P]
        tri_strict = consts[:, K_TS:K_TS + P]
        wide0 = cursor[0]
        gate_row = [at(f"gate_row{i}", [P, D], F32, wide0 + i * 4096) for i in range(2)]
        cum_row = at("cum_row", [P, 2, T], F32, wide0)
        bias01 = at("bias01", [P, 8, 256], F32, wide0)
        bias2 = at("bias2", [P, 4, P], F32, wide0 + 8192)
        assert wide0 + 8192 + 2048 <= RA
        cursor[0] = RK
        col = keep("col", N_ROWS)
        mod = keep("mod", 16)
        scale1 = keep("scale1", KT)
        eps_col = keep("eps_col", 1)
        id_bf = keep("id_bf", P, BF16)
        cm_bf = keep("cm_bf", P, BF16)
        silu_c = keep("silu_c", KT)
        silu_t = keep("silu_t", KT)
        qgain = keep("qgain", 10)
        ssq = keep("ssq", NT)
        rstd = keep("rstd", NT)
        nmin = keep("nmin", 4)
        denom = keep("denom", 4)
        rden = keep("rden", 4)
        bfr = keep("bfr", FOX_HEADS)
        brr = keep("brr", N_ROUTE)
        tab = keep("tab", DIL_HEADS)
        wts = keep("wts", 2 * NT)
        dest = keep("dest", 2 * NT, U32)
        sidx = keep("sidx", 2 * NT, U32)
        tok_id = keep("tok_id", NT, I32)
        slot_tok = keep("slot_tok", MAX_BLK, I32)
        blk_exp = keep("blk_exp", MAX_BLK + 2, I32)
        idx_now = keep("idx_now", 1, I32)
        assert cursor[0] <= 229344, cursor[0]

        rows = at("rows", [P, P], F32, RB)
        ohs = at("ohs", [P, NG * 384], F32, RB + 512)
        relrow = at("relrow", [4, NG, 384], F32, RB + 6 * KB)
        ada_w = [at(f"ada_w{i}", [P, KT, 256], F32, RW + i * 8 * KB) for i in range(4)]
        ada_row = at("ada_row", [1, 2 * D], F32, RB + 24 * KB)
        ADA_FIRST, ADA_CHUNKS = 2 * D // 256, 6 * D // 256
        bg_w = [at(f"bg_w{i}", [P, KT, 256], F32, RY + 8 * KB + i * 8 * KB) for i in range(2)]
        bg_b = [at(f"bg_b{i}", [1, 256], F32, RA + 8 * KB + i * KB) for i in range(2)]
        bg_g = [at(f"bg_g{i}", [1, 256], F32, RA + 10 * KB + i * KB) for i in range(2)]
        bg_row = [at(f"bg_row{i}", [1, 256], F32, RA + 12 * KB + i * KB) for i in range(4)]
        xt = at("xt", [P, NT, D], F32, RA)
        junk = at("junk", [P, D], F32, RB + 16 * KB)
        h_tmp = [at(f"h_tmp{i}", [P, HALF], F32, RB + 20 * KB + i * 2 * KB) for i in range(2)]
        h_hi = at("h_hi", [P, KT, T], F32R, RH)
        h_lo = at("h_lo", [P, KT, T], F32R, RH + 32 * KB)
        VN = 4 * E + FOX_HEADS
        v_raw = at("v_raw", [P, KT, VN], F32, RW)
        v_hi = at("v_hi", [P, KT, VN], F32R, RW + 8448)
        v_lo = at("v_lo", [P, KT, VN], F32R, RW + 2 * 8448)
        qk_raw = [at(f"qk_raw{i}", [P, KT, P], F32, RW + i * 4096) for i in range(2)]
        qk_hi = [at(f"qk_hi{i}", [P, KT, P], F32R, RW + 8448 + i * 8192) for i in range(2)]
        qk_lo = [at(f"qk_lo{i}", [P, KT, P], F32R, RW + 8448 + 4096 + i * 8192) for i in range(2)]
        v_fox = at("v_fox", [P, NT, FOX_W], F32, RA)
        v_dil = at("v_dil", [P, NT, 4 * E], F32, RA)
        rec = [at(f"rec{i}", [P, NT, 2 * UW], F32, RA + 16 * KB + i * 4224) for i in range(2)]
        logits = [at(f"logits{i}", [P, T], F32, RB + i * 4096) for i in range(2)]
        prob = [at(f"prob{i}", [P, T], F32, RB + 8 * KB + i * 4096) for i in range(2)]
        probT = [at(f"probT{i}", [P, NT, P], F32, RB + 16 * KB + i * 4096) for i in range(2)]
        square = at("square", [P, HALF], F32, RB + 24 * KB)
        rs_head = at("rs_head", [P, HALF], F32, RB + 26 * KB)
        y_pair = at("y_pair", [P, NT, P], F32, RB + 28 * KB)
        qkT_hi = [at(f"qkT_hi{i}", [P, T], F32R, RS + i * 4096) for i in range(2)]
        dil_lo = [at(f"dil_lo{i}", [P, T], F32R, RY + i * 4096) for i in range(2)]
        fox_lo = [at(f"fox_lo{i}", [P, T], F32R, RA + 16 * KB + i * 4096) for i in range(2)]
        normed = [at(f"normed{i}", [P, HALF], F32, RA + 28 * KB + i * 2048) for i in range(2)]
        fg = [at(f"fg{i}", [P, FOX_HEADS, NT], F32, RA + 25 * KB + i * 256) for i in range(6)]
        cumT = at("cumT", [FOX_HEADS * NT, P], F32, RA + 27 * KB)
        mrec = at("mrec", [P, 4, NG, 4, UW], F32, RB)
        macc = [at(f"macc{i}", [P, 4, 4, E], F32, RB + 13 * KB + i * 4096) for i in range(2)]
        msm = at("msm", [P, 12, 4, 4], F32, RB + 21 * KB)
        y_f = at("y_f", [P, 6, T], F32, RY)
        y_lo = at("y_lo", [P, 6, T], F32R, RY)
        y_hi = at("y_hi", [P, 6, T], F32R, RA)
        merged = at("merged", [P, KT, T], F32, RB)
        g_k = (KT, KT, 6)
        g_raw, g_hi, g_lo = [], [], []
        g_at = RW
        for part, (lst, dt) in {"raw": (g_raw, F32), "hi": (g_hi, F32R), "lo": (g_lo, F32R)}.items():
            for i in range(3):
                lst.append(at(f"g_{part}{i}", [P, g_k[i], P], dt, g_at))
                g_at += g_k[i] * P * 4
        assert g_at <= RK
        g_tmp = [at(f"g_tmp{i}", [P, 2, HALF], F32, RA + 24 * KB + i * 4096) for i in range(2)]
        m_hi = at("m_hi", [P, KT, T], F32R, RH)
        m_lo = at("m_lo", [P, KT, T], F32R, RH + 32 * KB)
        x2 = at("x2", [P, NT, D], F32, RA)
        OC = 256
        o_raw = [at(f"o_raw{i}", [P, KT, OC], F32, RY + i * 8192) for i in range(3)]
        o_hi = [at(f"o_hi{i}", [P, KT, OC], F32R, RW + i * 16384) for i in range(2)]
        o_lo = [at(f"o_lo{i}", [P, KT, OC], F32R, RW + i * 16384 + 8192) for i in range(2)]
        o_tmp = at("o_tmp", [P, 2, OC], F32, RB + 28 * KB)
        o_junk = at("o_junk", [P, D], F32, RW)
        XN = 6
        xn2 = [at(f"xn2_{i}", [P, D], F32, where)
               for i, where in enumerate([RY + i * 4096 for i in range(4)] + [RY + 20 * KB, RW + 4 * KB])]
        mod2_row = [at(f"mod2_row{i}", [P, D], F32, RW + 8 * KB + i * 4096) for i in range(2)]
        w_rt = at("w_rt", [P, KT, N_ROUTE], F32, RY + 16 * KB)
        h2T = at("h2T", [P, KT, T], F32, RB)
        CHUNKS = 12
        e_raw = [at(f"e_raw{i}", [P, 2, HID], F32, RW + i * 4096) for i in range(CHUNKS // 2)]
        e_hi = [at(f"e_hi{i}", [P, 2, HID], F32R, RH + i * 8192) for i in range(CHUNKS)]
        e_lo = [at(f"e_lo{i}", [P, 2, HID], F32R, RH + i * 8192 + 4096) for i in range(CHUNKS)]
        y_e = at("y_e", [P, D], F32, RY)
        gate_act = at("gate_act", [P, HID], F32, RY + 8 * KB)
        act_in = at("act_in", [P, HID], F32, RY + 10 * KB)
        xg = at("xg", [P, D], F32, RY + 12 * KB)
        xT_hi = at("xT_hi", [P, KT, P], F32R, RY + 16 * KB)
        xT_lo = at("xT_lo", [P, KT, P], F32R, RY + 20 * KB)
        aT_hi = at("aT_hi", [P, 4, P], F32R, RW + 30 * KB)
        aT_lo = at("aT_lo", [P, 4, P], F32R, RW + 32 * KB)
        y_slot = [at(f"y_slot{i}", [P, D], F32, RH + i * 4096) for i in range(2 * NT)]
        y_sum = [at(f"y_sum{i}", [P, D], F32, RB + i * 4096) for i in range(4)]
        free = [RW + 24 * KB, RY + 20 * KB + 1024]

        def scratch(name, shape, dt=F32, where=0):
            size = 4
            for v in shape:
                size *= v
            t = at(name, [P] + shape, dt, free[where])
            free[where] += (size + 31) // 32 * 32
            return t

        lg = scratch("lg", [NT, N_ROUTE])
        g_max, g_sum, g_w, g_first, m_one, m_two, m_ex, m_r, e_first = (
            scratch(n, [NT], where=1) for n in "g_max g_sum g_w g_first m_one m_two m_ex m_r e_first".split())
        g_ex, g_eq, g_hot = (scratch(n, [NT, N_GROUPS], where=1) for n in "g_ex g_eq g_hot".split())
        e_in, e_eq, hot1, hot2, e_next = (scratch(n, [NT, PER_GROUP], where=0) for n in "e_in e_eq hot1 hot2 e_next".split())
        r_prod, r_mask, rank, r_blk = (scratch(n, [NT, N_EXP]) for n in "r_prod r_mask rank r_blk".split())
        r_int = scratch("r_int", [NT, N_EXP], I32)
        assert free[0] <= RW + 34 * KB
        before = at("before", [P, NT, N_EXP], F32, RY + 19 * KB + 512)
        c_int = at("c_int", [P, N_EXP], I32, free[1])
        over = [at(f"over{i}", [P, N_EXP], F32, free[1] + 128 + 128 * i) for i in range(3)]
        dest_f = at("dest_f", [P, 2 * NT], F32, free[1] + 512)
        sidx_f = at("sidx_f", [P, 2 * NT], F32, free[1] + 576)
        assert free[1] + 640 <= RW
        exp_cmp = at("exp_cmp", [1, N_OVER, N_EXP], F32, RY + 17 * KB + 512)
        exp_of = at("exp_of", [1, N_OVER], F32, RY + 20 * KB + 512)

        bank = ctx.enter_context(nc.psum_tensor("bank", [P, 8, HALF], F32))

        d_rel = dram("d_rel", [DIL_HEADS, P, 384])
        d_cum = dram("d_cum", [FOX_HEADS * NT, P])
        d_rec = dram("d_rec", [NG, T, 4 * UW])
        d_mod = dram("d_mod", [48, P])
        d_h2 = dram("d_h2", [T, D])
        d_slot = dram("d_slot", [SLOTS * MAX_BLK, 1], I32)
        d_y = dram("d_y", [MAX_BLK * SLOTS, D])

        (rows_ld, small_ld, pool_set, bf_set, rowsT_pe, col_ok, silu_e, rel_pe, rel_ev, rel_st, bias_ld,
         ada_pe, mod_ok, scl_ok, chain_a, chain_v) = sems(
            "rows_ld small_ld pool_set bf_set rowsT_pe col_ok silu_e rel_pe rel_ev rel_st bias_ld "
            "ada_pe mod_ok scl_ok chain_a chain_v")
        tile_ld = sems(" ".join(f"tile_ld{t}" for t in range(NT // 2)))
        ada_ld = sems(" ".join(f"ada_ld{i}" for i in range(4)))
        rstd_ok, xn_ok, xT_pe, xT_act, h_hi_ok, h_lo_ok = sems(
            "rstd_ok xn_ok xT_pe xT_act h_hi_ok h_lo_ok")
        w_ld = sems("w_ld_a w_ld_b")
        w_hi_ok, w_lo_ok, v_pe, v_ev_act, v_ev_dve = sems(
            "w_hi_ok w_lo_ok v_pe v_ev_act v_ev_dve")
        proj_pe, sq_ok, ss_pe, ln_ok, rs_ok, norm_ok = sems("proj_pe sq_ok ss_pe ln_ok rs_ok norm_ok")
        qkT_hi_ok, qkT_lo_ok = sems("qkT_hi_ok qkT_lo_ok")
        qk_pe, min_ok, exp_ok, turn_pe, pT_act, pT_dve, pv_pe, rden_ok, y_ok, yT_pe, yT_ok = sems(
            "qk_pe min_ok exp_ok turn_pe pT_act pT_dve pv_pe rden_ok y_ok yT_pe yT_ok")
        rec_st = sems("rec_st0 rec_st1")
        fg_ok, fg_act, cum_pe, cum_dve, cumT_pe, cumT_ev, cum_st, cum_ld = sems(
            "fg_ok fg_act cum_pe cum_dve cumT_pe cumT_ev cum_st cum_ld")
        mrec_ld, mrg_d, mrg_e, mrg_y, mrg_pe, mrg_ev = sems("mrec_ld mrg_d mrg_e mrg_y mrg_pe mrg_ev")
        mod_st, gate_ld, y_hi_ok, y_lo_ok = sems("mod_st gate_ld y_hi_ok y_lo_ok")
        ada_ev, adaT_pe, bg_pe, bg_row_ok = sems("ada_ev adaT_pe bg_pe bg_row_ok")
        bg_ld = sems("bg_ld0 bg_ld1")
        g_ld = sems("g_ld0 g_ld1 g_ld2")
        g_hi_ok, g_lo_ok, gate_pe, gate_e, merged_ok = sems("g_hi_ok g_lo_ok gate_pe gate_e merged_ok")
        x2_ld, m_hi_ok, m_lo_ok, o_hi_ok, o_lo_ok, o_pe, o_done = sems("x2_ld m_hi_ok m_lo_ok o_hi_ok o_lo_ok o_pe o_done")
        o_ld = sems("o_ld0 o_ld1 o_ld2")
        rs2_ok, mod2_ld, xn2_ok, h2_pe, h2_act, rt_ld, rt_pe = sems("rs2_ok mod2_ld xn2_ok h2_pe h2_act rt_ld rt_pe")
        h2_st = sems("h2_st0 h2_st1 h2_st2")
        r_d, r_a, rank_pe, tok_ok, slot_z, scat, slot_ld, dest_ok = sems("r_d r_a rank_pe tok_ok slot_z scat slot_ld dest_ok")
        e_ld = sems(" ".join(f"e_ld{i}" for i in range(CHUNKS // 2)))
        e_hi_ok, e_lo_ok, e_used, xg_ld, xgT_pe, xT_hi_ok, xT_lo_ok = sems(
            "e_hi_ok e_lo_ok e_used xg_ld xgT_pe xT_hi_ok xT_lo_ok")
        idx_ok, ye_end = sems("idx_ok ye_end")
        slot_y = sems(" ".join(f"slot_y{t}" for t in range(NT // 2)))
        sig_e, silu_v, act_ok, actT_pe, aT_hi_ok, aT_lo_ok, ye_act, ye_dve, ye_st = sems(
            "sig_e silu_v act_ok actT_pe aT_hi_ok aT_lo_ok ye_act ye_dve ye_st")
        f_act, f_dve, f_pool, out_st = sems("f_act f_dve f_pool out_st")
        block = ctx.enter_context(nc.Block())

        links = {"a": 0, "v": 0}

        def link_a(ins):
            links["a"] += 1
            ins.then_inc(chain_a, 1)
            nc.scalar.wait_ge(chain_a, links["a"])

        def link_v(ins):
            links["v"] += 1
            ins.then_inc(chain_v, 1)
            nc.vector.wait_ge(chain_v, links["v"])

        small_rows = [(C_C, c.rearrange("(a b) -> a b", b=P)), (C_N1, n1.rearrange("(a b) -> a b", b=P)),
                      (C_N2, n2.rearrange("(a b) -> a b", b=P)), (C_BADA, b_ada.rearrange("(a b) -> a b", b=P)),
                      (C_QG, qg.rearrange("(a b) e -> a (b e)", b=2)), (C_KG, kg.rearrange("(a b) e -> a (b e)", b=2))]

        jobs = []
        for g in range(NG):
            jobs.append(("v", OFF_DV + g * 4 * E, 4 * E))
            for p in range(2):
                jobs.append(("qk", OFF_DQ + (2 * g + p) * P, OFF_DK + (2 * g + p) * P))
        jobs += [("v", OFF_FV, 4 * E), ("v", OFF_FV + 4 * E, VN)]
        for p in range(FOX_HEADS // 2):
            jobs.append(("qk", OFF_FQ + p * P, OFF_FK + p * P))
        J_FOX = 9
        bg_of = {j: 1 for j in range(J_FOX) if jobs[j][0] == "qk"}
        bg_of.update({3: 5, 6: 5})
        assert sum(bg_of.values()) == ADA_CHUNKS - ADA_FIRST

        def bg_chunks(j):
            n0 = ADA_FIRST + sum(c for i, c in bg_of.items() if i < j)
            return range(n0, n0 + bg_of.get(j, 0))

        def bg_gain(n):
            return 4 * D <= n * 256 < 5 * D

        def bg_loads(n):
            return sum(3 if bg_gain(i) else 2 for i in range(ADA_FIRST, n + 1) if i % 2 == n % 2)

        def pe_ada_bg(pe, j):
            for i, n in enumerate(bg_chunks(j)):
                done = n - ADA_FIRST - (1 if i else 0)
                if done > 0:
                    pe.wait_ge(bg_row_ok, done)
                pe.wait_ge(bg_ld[n % 2], 16 * bg_loads(n))
                for k in range(KT):
                    mm = nc.tensor.matmul(bank[0:1, (4, 7)[i % 2], 0:256], silu_c[:, k:k + 1], bg_w[n % 2][:, k, :],
                                          start=(k == 0), stop=(k == KT - 1))
                mm.then_inc(bg_pe, 1)

        def dve_ada_bg(dve, j):
            for i, n in enumerate(bg_chunks(j)):
                dve.wait_ge(bg_pe, n - ADA_FIRST + 1)
                row = bg_row[n % 4][:, :]
                if n - ADA_FIRST >= 4:
                    dve.wait_ge(mod_st, 16 * (n - ADA_FIRST - 3))
                last = nc.vector.tensor_tensor(row, bank[0:1, (4, 7)[i % 2], 0:256], bg_b[n % 2][:, :], ALU.add)
                if bg_gain(n):
                    link_v(last)
                    last = nc.vector.scalar_tensor_tensor(out=row, in0=row, scalar=1.0, in1=bg_g[n % 2][:, :],
                                                          op0=ALU.add, op1=ALU.mult)
                last.then_inc(bg_row_ok, 1)

        w_in_v = w_in.rearrange("(k p) n -> p k n", p=P)

        def raw_parts(j):
            kind, a, b = jobs[j]
            if kind == "v":
                return [(v_raw[:, 4 * i:4 * i + 4, 0:b], w_in_v[:, 4 * i:4 * i + 4, a:a + b]) for i in range(2)]
            return [(qk_raw[0][:, :, :], w_in_v[:, :, a:a + P]), (qk_raw[1][:, :, :], w_in_v[:, :, b:b + P])]

        def split_parts(j):
            kind, a, b = jobs[j]
            if kind == "v":
                return [tuple(t[:, 4 * i:4 * i + 4, 0:b] for t in (v_raw, v_hi, v_lo)) for i in range(2)]
            return [(qk_raw[i][:, :, :], qk_hi[i][:, :, :], qk_lo[i][:, :, :]) for i in range(2)]

        def products_done(eng, j):
            if jobs[j][0] == "v":
                eng.wait_ge(v_pe, NT * sum(job[0] == "v" for job in jobs[:j + 1]))
            else:
                eng.wait_ge(proj_pe, 4 * sum(job[0] == "qk" for job in jobs[:j + 1]))

        def act_split(act, j):
            for i, (raw, hi, _) in enumerate(split_parts(j)):
                act.wait_ge(w_ld[i], 16 * (j + 1))
                if j:
                    products_done(act, j - 1)
                nc.scalar.activation(hi, raw, ACT.Copy).then_inc(w_hi_ok, 1)

        def dve_split(dve, j):
            for i, (raw, hi, lo) in enumerate(split_parts(j)):
                dve.wait_ge(w_hi_ok, 2 * j + i + 1)
                nc.vector.tensor_tensor(lo, raw, hi.bitcast(F32), ALU.subtract).then_inc(w_lo_ok, 1)

        PROJ_BANK = (0, 2, 1, 3)

        def tokens_of(view, g, tile):
            if g == 0:
                return view[:, tile * P:(tile + 1) * P]
            if g == 1:
                r, b = tile // 2, tile % 2
                return view[:, r + 512 * b:min(r + 512 * b + 512, T):4]
            return view[:, tile:T:8]

        def placed(view, g, half):
            if g <= 0:
                return view[:, half * HALF:(half + 1) * HALF]
            r = ORDER_STEP[g]
            n = HALF // r
            return view.rearrange("p (r n) -> p n r", r=r)[:, half * n:(half + 1) * n, :]

        def units_of(g):
            out = []
            for q in range(NT):
                for a in range(2):
                    if g < 0:
                        out.append((q, a, 0, (q + 1) * P))
                    elif g == 2 or (g == 0 and q == 0) or (g == 1 and q % 2 == 0):
                        out.append((q, a, q * P, P))
                    else:
                        out.append((q, a, (q - 1) * P, 2 * P))
            return out

        def groups(g):
            n, out = 0, []
            for _, _, _, kw in units_of(g):
                here = []
                for b in range(0, kw // P, 4):
                    here.append((n, list(range(b, min(b + 4, kw // P)))))
                    n += 1
                out.append(here)
            return out, n

        def group_of_pair(jp):
            return jp // 2 if jp < 6 else -1

        gbase = [0]
        for jp in range(10):
            gbase.append(gbase[-1] + groups(group_of_pair(jp))[1])

        def s_at(u, kw):
            if kw <= HALF:
                return bank[:, 2 * (u % 2), 0:kw]
            b = 2 * (u % 2)
            return bank[:, b:b + 2, :].rearrange("p b n -> p (b n)")[:, 0:kw]

        def pe_proj(pe, dst, hi, lo, lhs, half):
            n = 0
            for k in range(KT):
                t = slice(half * HALF, (half + 1) * HALF)
                for w, h in ((hi, h_hi), (hi, h_lo), (lo, h_hi)):
                    mm = nc.tensor.matmul(dst, w[:, k, :], h[:, k, t], start=(n == 0), stop=(n == 3 * KT - 1))
                    n += 1
            return mm

        def pe_values(pe, j, vj, g):
            kind, a, ncol = jobs[j]
            if bg_of.get(j):
                pe.wait_ge(y_ok, 16 * (2 * vj if j <= J_FOX else 6))
                pe_ada_bg(pe, j)
                pe.wait_ge(bg_row_ok, bg_chunks(j)[-1] - ADA_FIRST + 1)
            pe.wait_ge(w_lo_ok, 2 * j + 1)
            for t in range(NT):
                m = vj * NT + t
                if t >= 4:
                    pe.wait_ge(v_ev_dve if t % 2 else v_ev_act, (m - 4) // 2 + 1)
                n = 0
                for k in range(KT):
                    if k == 4 and t == 0:
                        pe.wait_ge(w_lo_ok, 2 * j + 2)
                    for w, h in ((v_hi, h_hi), (v_hi, h_lo), (v_lo, h_hi)):
                        mm = nc.tensor.matmul(bank[:, t % 4, 0:ncol], tokens_of(h[:, k, :], max(g, 0), t),
                                              w[:, k, 0:ncol], start=(n == 0), stop=(n == 3 * KT - 1))
                        n += 1
                mm.then_inc(v_pe, 1)

        def ev_values(eng, op, j, vj, which, done):
            kind, a, ncol = jobs[j]
            if j == J_FOX:
                eng.wait_ge(mod_st, 16 * (ADA_CHUNKS - ADA_FIRST))
            for t in range(which, NT, 2):
                eng.wait_ge(v_pe, vj * NT + t + 1)
                if j < J_FOX:
                    dst = v_dil[:, t, :]
                else:
                    c0 = (j - J_FOX) * 4 * E
                    dst = v_fox[:, t, c0:c0 + 4 * E]
                last = op(dst, bank[:, t % 4, 0:4 * E])
                if ncol > 4 * E:
                    last = op(fg[0][:, :, t], bank[:, t % 4, 4 * E:VN])
                last.then_inc(done, 1)

        def act_copy(out_, in_):
            return nc.scalar.activation(out_, in_, ACT.Copy)

        def pe_pair(pe, jp, j):
            g = group_of_pair(jp)
            units, (turns, _) = units_of(g), groups(g)
            heads0 = 0 if g >= 0 else 2 * (jp - 6)

            def proj(n):
                i, half = n % 2, n // 2
                pe.wait_ge(w_lo_ok, 2 * j + i + 1)
                mm = pe_proj(pe, bank[:, PROJ_BANK[n], :], qk_hi[i], qk_lo[i], None, half)
                mm.then_inc(proj_pe, 1)

            def sum_squares(n):
                pe.wait_ge(sq_ok, 4 * jp + n + 1)
                if 4 * jp + n:
                    pe.wait_ge(ln_ok, 4 * jp + n)
                nc.tensor.matmul(bank[:, 7, :], block_ones, square[:, :], start=True, stop=True).then_inc(ss_pe, 1)

            def scores(u):
                q, a, k0, kw = units[u]
                pe.wait_ge(qkT_lo_ok, 4 * jp + (2 if g <= 0 and q < 4 else 4))
                if u >= 2:
                    pe.wait_ge(min_ok, 16 * jp + u - 1)
                dst = s_at(u, kw)
                h = slice(a * E, (a + 1) * E)
                lo = fox_lo if g < 0 else dil_lo
                for c in range(0, kw, HALF):
                    w = min(HALF, kw - c)
                    diag = g < 0 and c <= q * P < c + w
                    for n, (x, y) in enumerate(((qkT_hi, qkT_hi), (qkT_hi, lo), (lo, qkT_hi))):
                        mm = nc.tensor.matmul(dst[:, c:c + w], x[0][h, q * P:(q + 1) * P], y[1][h, k0 + c:k0 + c + w],
                                              start=n == 0, stop=n == 2 and not diag)
                    if diag:
                        mm = nc.tensor.matmul(dst[:, q * P:(q + 1) * P], id_bf[:, :], cm_bf[:, :],
                                              start=False, stop=True)
                mm.then_inc(qk_pe, 1)

            def turn(u):
                pe.wait_ge(exp_ok, 16 * jp + u + 1)
                for n, blocks in turns[u]:
                    G = gbase[jp] + n
                    if G >= 2:
                        pe.wait_ge((pT_act, pT_dve)[G % 2], G // 2)
                    for b in blocks:
                        mm = nc.tensor.transpose(bank[:, 5 + G % 2, (b % 4) * P:(b % 4 + 1) * P],
                                                 prob[u % 2][:, b * P:(b + 1) * P], ident)
                    mm.then_inc(turn_pe, 1)

            def values(u):
                q, a, k0, kw = units[u]
                for n, _ in turns[u]:
                    G = gbase[jp] + n
                    pe.wait_ge((pT_act, pT_dve)[G % 2], G // 2 + 1)
                if u >= 2 or jp:
                    pe.wait_ge(y_ok, 16 * jp + u - 1)
                if u == 0 and bg_of.get(j):
                    pe.wait_ge(bg_row_ok, bg_chunks(j)[-1] - ADA_FIRST + 1)
                for b in range(kw // P):
                    if g < 0:
                        v = v_fox[:, b, (heads0 + a) * E:(heads0 + a + 1) * E]
                    else:
                        v = v_dil[:, k0 // P + b, (2 * (jp % 2) + a) * E:(2 * (jp % 2) + a + 1) * E]
                    mm = nc.tensor.matmul(bank[:, (4, 7)[u % 2], 0:E], probT[u % 2][:, b, :], v,
                                          start=(b == 0), stop=(b == kw // P - 1))
                mm.then_inc(pv_pe, 1)

            def turn_y(half):
                pe.wait_ge(y_ok, 16 * jp + (16 if half else 10))
                for q in range(4):
                    mm = nc.tensor.transpose(bank[:, 7, q * P:(q + 1) * P], y_pair[:, 4 * half + q, :], ident)
                mm.then_inc(yT_pe, 1)

            early = g <= 0
            proj(0)
            proj(1)
            if jp:
                pe.wait_ge(y_ok, 16 * jp)
            if jp > 6:
                pe.wait_ge(yT_ok, 2 * (jp - 6))
            sum_squares(0)
            proj(2)
            sum_squares(1)
            proj(3)
            sum_squares(2)
            if not early:
                sum_squares(3)
            scores(0)
            scores(1)
            if early:
                sum_squares(3)
            if bg_of.get(j):
                pe_ada_bg(pe, j)
            for u in range(16):
                turn(u)
                if g < 0 and u == 12:
                    pe.wait_ge(yT_ok, 2 * (jp - 6) + 1)
                if u:
                    values(u - 1)
                if g < 0 and u == 10:
                    turn_y(0)
                if u + 2 < 16:
                    scores(u + 2)
            values(15)
            if g < 0:
                turn_y(1)

        def act_pair(act, jp, j):
            g = group_of_pair(jp)
            units, (turns, _) = units_of(g), groups(g)
            early = g <= 0

            def norm(n):
                N = 4 * jp + n
                act.wait_ge(proj_pe, N + 1)
                if N:
                    act.wait_ge(ss_pe, N)
                nc.scalar.activation(square[:, :], bank[:, PROJ_BANK[n], :], ACT.Square).then_inc(sq_ok, 1)

            def root(n):
                N = 4 * jp + n
                act.wait_ge(ss_pe, N + 1)
                if N:
                    act.wait_ge(norm_ok, N)
                nc.scalar.activation(rs_head[:, :], bank[:, 7, :], ACT.Ln, scale=1.0 / E,
                                     bias=eps_col[:, :]).then_inc(ln_ok, 1)
                act.wait_ge(ln_ok, N + 1)
                nc.scalar.activation(rs_head[:, :], rs_head[:, :], ACT.Exp, scale=-0.5).then_inc(rs_ok, 1)

            def exps(u):
                q, a, k0, kw = units[u]
                act.wait_ge(min_ok, 16 * jp + u + 1)
                if u >= 2:
                    act.wait_ge(turn_pe, gbase[jp] + turns[u - 2][-1][0] + 1)
                if g < 0:
                    lo, su = nmin[:, u % 4:u % 4 + 1], denom[:, u % 4:u % 4 + 1]
                    if u >= 4:
                        act.wait_ge(rden_ok, 16 * (jp - 6) + u - 3)
                else:
                    r = rec[jp % 2][:, q, a * UW:(a + 1) * UW]
                    su, lo = r[:, E:E + 1], r[:, E + 1:E + 2]
                nc.scalar.activation(prob[u % 2][:, 0:kw], logits[u % 2][:, 0:kw], ACT.Exp, bias=lo, scale=-1.0,
                                     accum_out=su).then_inc(exp_ok, 1)

            def copies(u):
                for n, blocks in turns[u]:
                    G = gbase[jp] + n
                    if G % 2 == 0:
                        act.wait_ge(turn_pe, G + 1)
                        if u >= 2:
                            act.wait_ge(pv_pe, 16 * jp + u - 1)
                        elif jp:
                            act.wait_ge(pv_pe, 16 * jp)
                        w = len(blocks)
                        nc.scalar.activation(probT[u % 2][:, blocks[0]:blocks[0] + w, :],
                                             bank[:, 5, 0:w * P].rearrange("p (b n) -> p b n", n=P),
                                             ACT.Copy).then_inc(pT_act, 1)

            def split(n):
                N = 4 * jp + n
                i, half = n % 2, n // 2
                act.wait_ge(norm_ok, N + 1)
                src, dst = normed[n % 2][:, :], placed(qkT_hi[i][:, :], g, half)
                if g > 0:
                    src = src.rearrange("p (n r) -> p n r", r=ORDER_STEP[g])
                if n == 0 and jp:
                    act.wait_ge(qk_pe, 16 * jp)
                nc.scalar.activation(dst, src, ACT.Copy).then_inc(qkT_hi_ok, 1)

            norm(0)
            root(0)
            norm(1)
            split(0)
            root(1)
            norm(2)
            split(1)
            root(2)
            norm(3)
            split(2)
            root(3)
            split(3)
            exps(0)
            exps(1)
            for u in range(16):
                copies(u)
                if u == 2 and j + 1 < len(jobs):
                    act_split(act, j + 1)
                if g < 0 and u == 11:
                    y_out(act, jp, 0)
                if u + 2 < 16:
                    exps(u + 2)
            if g < 0:
                y_out(act, jp, 1)

        def y_out(act, jp, half):
            act.wait_ge(yT_pe, 2 * (jp - 6) + half + 1)
            nc.scalar.activation(y_f[:, jp - 6, half * HALF:(half + 1) * HALF], bank[:, 7, :],
                                 ACT.Copy).then_inc(yT_ok, 1)

        def dve_pair(dve, jp, j):
            g = group_of_pair(jp)
            units, (turns, _) = units_of(g), groups(g)
            early = g <= 0

            def norm(n):
                i, half = n % 2, n // 2
                dve.wait_ge(rs_ok, 4 * jp + n + 1)
                gain = qgain if i == 0 else col[:, C_KG:C_KG + 10]
                p = jp - 6 if g < 0 else 4 + jp
                nc.vector.scalar_tensor_tensor(out=normed[n % 2][:, :], in0=bank[:, PROJ_BANK[n], :], scalar=gain[:, p:p + 1],
                                               in1=rs_head[:, :], op0=ALU.mult, op1=ALU.mult).then_inc(norm_ok, 1)

            def split(n):
                i, half = n % 2, n // 2
                src = normed[n % 2][:, :]
                hi, lo = (placed(t[i][:, :], g, half) for t in (qkT_hi, fox_lo if g < 0 else dil_lo))
                if g > 0:
                    src = src.rearrange("p (n r) -> p n r", r=ORDER_STEP[g])
                dve.wait_ge(qkT_hi_ok, 4 * jp + n + 1)
                nc.vector.tensor_tensor(lo, src, hi.bitcast(F32), ALU.subtract).then_inc(qkT_lo_ok, 1)

            def minimum(u):
                q, a, k0, kw = units[u]
                dve.wait_ge(qk_pe, 16 * jp + u + 1)
                if u >= 2:
                    dve.wait_ge(exp_ok, 16 * jp + u - 1)
                elif u == 0:
                    if jp:
                        dve.wait_ge(exp_ok, 16 * jp)
                    if g < 0:
                        dve.wait_ge(cum_ld, 16 * (jp - 5))
                    elif jp >= 2:
                        dve.wait_ge(rec_st[jp % 2], 128 * (jp // 2))
                if g < 0:
                    add, lo = cum_row[:, a, 0:kw], nmin[:, u % 4:u % 4 + 1]
                else:
                    h = 2 * (jp % 2) + a
                    add = bias2[:, h, :] if g == 2 else bias01[:, 4 * g + h, 256 - kw:256]
                    lo = rec[jp % 2][:, q, a * UW + E + 1:a * UW + E + 2]
                nc.vector.tensor_tensor_reduce(out=logits[u % 2][:, 0:kw], in0=s_at(u, kw), in1=add,
                                               scale=1.0, scalar=3e38, op0=ALU.add, op1=ALU.min,
                                               accum_out=lo).then_inc(min_ok, 1)

            def copies(u):
                for n, blocks in turns[u]:
                    G = gbase[jp] + n
                    if G % 2:
                        dve.wait_ge(turn_pe, G + 1)
                        if u >= 2:
                            dve.wait_ge(pv_pe, 16 * jp + u - 1)
                        elif jp:
                            dve.wait_ge(pv_pe, 16 * jp)
                        w = len(blocks)
                        nc.vector.tensor_copy(probT[u % 2][:, blocks[0]:blocks[0] + w, :],
                                              bank[:, 6, 0:w * P].rearrange("p (b n) -> p b n", n=P)).then_inc(pT_dve, 1)

            def result(u):
                q, a, _, _ = units[u]
                src = bank[:, (4, 7)[u % 2], 0:E]
                if g < 0:
                    if u == 0 and jp > 6:
                        dve.wait_ge(yT_pe, 2 * (jp - 6))
                    dve.wait_ge(exp_ok, 16 * jp + u + 1)
                    nc.vector.reciprocal(rden[:, u % 4:u % 4 + 1], denom[:, u % 4:u % 4 + 1]).then_inc(rden_ok, 1)
                    dve.wait_ge(pv_pe, 16 * jp + u + 1)
                    dve.wait_ge(rden_ok, 16 * (jp - 6) + u + 1)
                    nc.vector.tensor_scalar(y_pair[:, q, a * E:(a + 1) * E], src, rden[:, u % 4:u % 4 + 1], None,
                                            ALU.mult).then_inc(y_ok, 1)
                else:
                    dve.wait_ge(pv_pe, 16 * jp + u + 1)
                    nc.vector.tensor_copy(rec[jp % 2][:, q, a * UW:a * UW + E], src).then_inc(y_ok, 1)

            norm(0)
            split(0)
            norm(1)
            split(1)
            norm(2)
            split(2)
            if not early:
                norm(3)
                split(3)
            minimum(0)
            minimum(1)
            if early:
                norm(3)
                split(3)
            dve_ada_bg(dve, j)
            for u in range(16):
                copies(u)
                if u == 2 and j + 1 < len(jobs):
                    dve_split(dve, j + 1)
                if u:
                    result(u - 1)
                if u + 2 < 16:
                    minimum(u + 2)
            result(15)
        def g_sources(f):
            c = slice(f * P, (f + 1) * P)
            return [(0, g_raw[0][:, :, :], w_in_v[:, :, OFF_GA + f * P:OFF_GA + (f + 1) * P]),
                    (1, g_raw[1][:, :, :], w_in_v[:, :, OFF_GB + f * P:OFF_GB + (f + 1) * P]),
                    (2, g_raw[2][:, 0:4, :], w_a.rearrange("(k p) n -> p k n", p=P)[:, :, c]),
                    (2, g_raw[2][:, 4:6, :], w_b.rearrange("(k p) n -> p k n", p=P)[:, :, c])]

        def g_split_hi(f, i):
            A.wait_ge(g_ld[i], (32 if i == 2 else 16) * (f + 1))
            if f:
                A.wait_ge(gate_pe, 8 * (f - 1) + (8 if i == 2 else 5 + i))
            else:
                A.wait_ge(proj_pe, 40)
            A.activation(g_hi[i][:, :, :], g_raw[i][:, :, :], ACT.Copy).then_inc(g_hi_ok, 1)

        def g_split_lo(f, i):
            V.wait_ge(g_hi_ok, 3 * f + i + 1)
            V.tensor_tensor(g_lo[i][:, :, :], g_raw[i][:, :, :], g_hi[i][:, :, :].bitcast(F32),
                            ALU.subtract).then_inc(g_lo_ok, 1)

        def at_start(b):
            return type(b) is int and b == 0

        def loads_before(step, at):
            n = 2 * step + at // 6 + 1
            return n if at % 6 < 2 or at_start(step) else n - 1

        def chunk_hi(step, i, place=None, first=False):
            place = i if place is None else place
            A.wait_ge(e_ld[place % 6], 16 * loads_before(step, place))
            if not first:
                A.wait_ge(e_used, CHUNKS * (step - 1) + i + 1)
            A.activation(e_hi[i][:, :, :], e_raw[place % 6][:, :, :], ACT.Copy).then_inc(
                e_hi_ok, 5 if first and i == 7 else 1)

        def chunk_lo(step, i, place=None, first=False):
            place = i if place is None else place
            V.wait_ge(e_hi_ok, CHUNKS * step + place + 1)
            V.tensor_tensor(e_lo[i][:, :, :], e_raw[place % 6][:, :, :], e_hi[i][:, :, :].bitcast(F32),
                            ALU.subtract).then_inc(e_lo_ok, 5 if first and i == 7 else 1)

        def chunk_load(sp, step, place, src):
            if not at_start(step) or place >= 6:
                sp.wait_ge(e_lo_ok, CHUNKS * step + place - 5)
            sp.dma_start(e_raw[place % 6][:, :, :], src).then_inc(e_ld[place % 6], 16)

        def three(dst, lhs, rhs, first, last):
            for n, (a, b) in enumerate(((0, 0), (0, 1), (1, 0))):
                mm = nc.tensor.matmul(dst, lhs[a], rhs[b], start=first and n == 0, stop=last and n == 2)
            return mm

        def pe_up(e, which, first=False):
            if which == 0:
                nc.tensor.wait_ge(xT_lo_ok, e + 1)
            if not first:
                nc.tensor.wait_ge(act_ok, e)
            for i in range(4):
                c = 4 * which + i
                nc.tensor.wait_ge(e_lo_ok, CHUNKS * e + c + 1)
                for kk in range(2):
                    k = 2 * i + kk
                    mm = three(bank[:, which, :], (xT_hi[:, k, :], xT_lo[:, k, :]),
                               (e_hi[c][:, kk, :], e_lo[c][:, kk, :]), k == 0, k == KT - 1)
                mm.then_inc(e_used, 5 if first and c == 7 else 1)

        def pe_turn_act(b):
            nc.tensor.wait_ge(act_ok, b + 1)
            if not at_start(b):
                nc.tensor.wait_ge(aT_lo_ok, b)
            for k in range(4):
                mm = nc.tensor.transpose(bank[:, 4, k * P:(k + 1) * P], act_in[:, k * P:(k + 1) * P], ident)
            mm.then_inc(actT_pe, 1)

        def pe_turn_x(b):
            nc.tensor.wait_ge(xg_ld, 16 * (b + 1))
            if not at_start(b):
                nc.tensor.wait_ge(xT_lo_ok, b)
            for k in range(KT):
                mm = nc.tensor.transpose(bank[:, 5 + k // 4, k % 4 * P:(k % 4 + 1) * P], xg[:, k * P:(k + 1) * P], ident)
            mm.then_inc(xgT_pe, 1)

        def pe_down(b, place=8):
            nc.tensor.wait_ge(aT_lo_ok, b + 1)
            if not at_start(b):
                nc.tensor.wait_ge(ye_act, b)
                nc.tensor.wait_ge(ye_dve, b)
            for i in range(4):
                c = 8 + i
                nc.tensor.wait_ge(e_lo_ok, CHUNKS * (b + 1) + place + i + 1)
                for kk in range(2):
                    k = 2 * (i % 2) + kk
                    mm = three(bank[:, 2 + i // 2, :], (aT_hi[:, k, :], aT_lo[:, k, :]),
                               (e_hi[c][:, kk, :], e_lo[c][:, kk, :]), k == 0, k == 3)
                mm.then_inc(e_used, 1)

        turned_x = bank[:, 5:7, :].rearrange("p b (k n) -> p (b k) n", n=P)
        turned_act = bank[:, 4, :].rearrange("p (k n) -> p k n", n=P)

        def act_xT(b, first=False):
            A.wait_ge(xgT_pe, b + 1)
            if not first:
                A.wait_ge(e_used, CHUNKS * (b - 1) + 8)
            A.activation(xT_hi[:, :, :], turned_x, ACT.Copy).then_inc(xT_hi_ok, 1)

        def dve_xT(b):
            V.wait_ge(xT_hi_ok, b + 1)
            V.tensor_tensor(xT_lo[:, :, :], turned_x, xT_hi[:, :, :].bitcast(F32), ALU.subtract).then_inc(xT_lo_ok, 1)

        def act_sig(e, first=False):
            A.wait_ge(e_used, CHUNKS * e + 4)
            if not first:
                A.wait_ge(act_ok, e)
            A.activation(gate_act[:, :], bank[:, 0, :], ACT.Exp, scale=-1.0).then_inc(sig_e, 1)
            A.wait_ge(sig_e, 3 * e + 1)
            A.activation(gate_act[:, :], gate_act[:, :], ACT.Ln, bias=ones[:, 0:1]).then_inc(sig_e, 1)
            A.wait_ge(sig_e, 3 * e + 2)
            A.activation(gate_act[:, :], gate_act[:, :], ACT.Exp, scale=-1.0).then_inc(sig_e, 1)

        def dve_silu(e):
            V.wait_ge(sig_e, 3 * e + 3)
            V.tensor_tensor(gate_act[:, :], gate_act[:, :], bank[:, 0, :], ALU.mult).then_inc(silu_v, 1)

        def dve_act(e, first=False):
            V.wait_ge(silu_v, e + 1)
            V.wait_ge(e_used, CHUNKS * e + 8)
            if not first:
                V.wait_ge(actT_pe, e)
            V.tensor_tensor(act_in[:, :], gate_act[:, :], bank[:, 1, :], ALU.mult).then_inc(act_ok, 1)

        def act_aT(b):
            A.wait_ge(actT_pe, b + 1)
            if not at_start(b):
                A.wait_ge(e_used, CHUNKS * (b + 1))
            A.activation(aT_hi[:, :, :], turned_act, ACT.Copy).then_inc(aT_hi_ok, 1)

        def dve_aT(b):
            V.wait_ge(aT_hi_ok, b + 1)
            V.tensor_tensor(aT_lo[:, :, :], turned_act, aT_hi[:, :, :].bitcast(F32), ALU.subtract).then_inc(aT_lo_ok, 1)

        def act_y(b, place=8):
            if not at_start(b):
                A.wait_ge(ye_st, 16 * b)
            A.wait_ge(e_used, CHUNKS * (b + 1) + place + 2)
            A.activation(y_e[:, 0:HALF], bank[:, 2, :], ACT.Copy).then_inc(ye_act, 1)

        def dve_y(b, place=8):
            if not at_start(b):
                V.wait_ge(ye_st, 16 * b)
            V.wait_ge(e_used, CHUNKS * (b + 1) + place + 4)
            V.tensor_copy(y_e[:, HALF:D], bank[:, 3, :]).then_inc(ye_dve, 1)

        def store_y(b, signal=None):
            row = b * SLOTS
            A.wait_ge(ye_act, b + 1)
            A.wait_ge(ye_dve, b + 1)
            A.dma_start(d_y[bass.ds(row, SLOTS), :], y_e[:, :]).then_inc(signal or ye_st, 16)

        def act_step(e, last=False):
            first = at_start(e)
            if not last:
                chunk_hi(e + 1, 0)
                chunk_hi(e + 1, 1)
            if not first:
                act_aT(e - 1)
            if not last:
                chunk_hi(e + 1, 2)
                chunk_hi(e + 1, 3)
            act_sig(e, first)
            if not last:
                chunk_hi(e + 1, 4)
                chunk_hi(e + 1, 5)
                chunk_hi(e + 1, 6)
                chunk_hi(e + 1, 7)
                act_xT(e + 1)
            for i in range(4):
                chunk_hi(e + 1, 8 + i, i if last else None, first)
                if not first and i == 1:
                    act_y(e - 1)
            if not first:
                store_y(e - 1)

        def dve_step(e, last=False):
            first = at_start(e)
            if not last:
                chunk_lo(e + 1, 0)
                chunk_lo(e + 1, 1)
            if not first:
                dve_aT(e - 1)
            if not last:
                chunk_lo(e + 1, 2)
                chunk_lo(e + 1, 3)
            dve_silu(e)
            if not last:
                chunk_lo(e + 1, 4)
                chunk_lo(e + 1, 5)
            dve_act(e, first)
            if not last:
                chunk_lo(e + 1, 6)
                chunk_lo(e + 1, 7)
                dve_xT(e + 1)
            for i in range(4):
                chunk_lo(e + 1, 8 + i, i if last else None)
            if not first:
                dve_y(e - 1)

        def pe_step(e, last=False):
            first = at_start(e)
            pe_up(e, 0, first)
            if not first:
                pe_turn_act(e - 1)
            if not last:
                pe_turn_x(e + 1)
            pe_up(e, 1, first)
            if not first:
                pe_down(e - 1)

        w1_v = w1.rearrange("e (k p) n -> (e k) p n", p=P)
        w3_v = w3.rearrange("e (k p) n -> (e k) p n", p=P)
        w2_v = w2.rearrange("e (k p) n -> (e k) p n", p=P)

        def sp_up(sp, step, expert):
            for i in range(8):
                src = (w1_v, w3_v)[i // 4][bass.ds(expert * 8 + 2 * (i % 4), 2), :, :]
                chunk_load(sp, step, i, src.rearrange("k p n -> p k n"))

        def sp_down(sp, step, expert, place=8):
            for i in range(4):
                c = slice(i // 2 * HID, (i // 2 + 1) * HID)
                src = w2_v[bass.ds(expert * 4 + 2 * (i % 2), 2), :, c]
                chunk_load(sp, step, place + i, src.rearrange("k p n -> p k n"))

        def pool_index(pool, b, first=False):
            if not first:
                pool.wait_ge(xgT_pe, b)
            pool.tensor_copy(idx_now[:, :], slot_tok[:, bass.ds(b, 1)]).then_inc(idx_ok, 1)
            pool.wait_ge(idx_ok, b + 1)

        def pool_gather(pool):
            pool.indirect_dma_start(xg[:, :], None, d_h2, bass.IndirectOffsetOnAxis(ap=idx_now[:, :], axis=0)).then_inc(xg_ld, 16)

        def bc(ap, axis, shape):
            return ap.unsqueeze(axis).to_broadcast([P] + shape)

        def pick(dst, scores, top, priority, groups):
            link_v(V.tensor_reduce(top[:, :], scores, AX.X, ALU.max))
            link_v(V.tensor_tensor(dst[:, :, :], scores, bc(top[:, :], 2, [NT, groups]), ALU.is_equal))
            link_v(V.tensor_tensor(dst[:, :, :], dst[:, :, :], bc(priority, 1, [NT, groups]), ALU.mult))
            link_v(V.tensor_reduce(e_first[:, :], dst[:, :, :], AX.X, ALU.max))
            link_v(V.tensor_tensor(dst[:, :, :], dst[:, :, :], bc(e_first[:, :], 2, [NT, groups]), ALU.is_equal))

        def dve_route():
            row = lambda at, n: consts[:, K_ROW + at:K_ROW + at + n]
            G, EG = N_GROUPS, PER_GROUP
            V.wait_ge(rt_pe, 1)
            V.wait_ge(h2_st[2], 16 * (NT - 2))
            link_v(V.tensor_tensor(lg[:, :, :], bank[:, 4, 0:NT * N_ROUTE].rearrange("p (t n) -> p t n", t=NT),
                                   bc(brr[:, :], 1, [NT, N_ROUTE]), ALU.add))
            gl = lg[:, :, 0:G]
            el = lg[:, :, G:].rearrange("p t (g e) -> p t g e", g=G)
            pick(g_hot, gl, g_max, row(R_PRI4, G), G)
            V.tensor_tensor(g_ex[:, :, :], gl, bc(g_max[:, :], 2, [NT, G]), ALU.subtract).then_inc(r_d, 1)
            pr = r_prod[:, :, :].rearrange("p t (g e) -> p t g e", g=G)
            link_v(V.tensor_tensor(pr, el, bc(g_hot[:, :, :], 3, [NT, G, EG]), ALU.mult))
            link_v(V.tensor_reduce(e_in[:, :, :], r_prod[:, :, :].rearrange("p t (g e) -> p t e g", g=G), AX.X, ALU.add))
            pick(hot1, e_in[:, :, :], m_one, row(R_PRI8, EG), EG)
            link_v(V.tensor_scalar(e_next[:, :, :], hot1[:, :, :], -3e38, None, ALU.mult))
            link_v(V.tensor_tensor(e_next[:, :, :], e_next[:, :, :], e_in[:, :, :], ALU.add))
            pick(hot2, e_next[:, :, :], m_two, row(R_PRI8, EG), EG)
            V.tensor_tensor(m_ex[:, :], m_two[:, :], m_one[:, :], ALU.subtract).then_inc(r_d, 1)
            link_v(V.tensor_tensor(e_eq[:, :, :], hot1[:, :, :], hot2[:, :, :], ALU.add))
            for g in range(G):
                last = V.tensor_tensor(r_mask[:, :, g * EG:(g + 1) * EG], e_eq[:, :, :],
                                       bc(g_hot[:, :, g], 2, [NT, EG]), ALU.mult)
            last.then_inc(r_d, 1)
            V.wait_ge(r_a, 2)
            link_v(V.tensor_reduce(g_sum[:, :], g_ex[:, :, :], AX.X, ALU.add))
            link_v(V.tensor_scalar(m_r[:, :], m_ex[:, :], 1.0, None, ALU.add))
            link_v(V.tensor_tensor(m_r[:, :], m_r[:, :], g_sum[:, :], ALU.mult))
            link_v(V.reciprocal(wts[:, 0:NT], m_r[:, :]))
            link_v(V.tensor_tensor(wts[:, NT:], wts[:, 0:NT], m_ex[:, :], ALU.mult))
            V.memset(before[:, 0, :], 0.0).then_inc(r_d, 1)
            V.wait_ge(r_d, 4)
            V.wait_ge(rank_pe, 1)
            tot = bank[:, 6, 0:NT * N_EXP].rearrange("p (t e) -> p t e", t=NT)
            for t in range(1, NT):
                link_v(V.tensor_tensor(before[:, t, :], before[:, t - 1, :], tot[:, t - 1, :], ALU.add))
            link_v(V.tensor_tensor(rank[:, :, :], bank[:, 5, 0:NT * N_EXP].rearrange("p (t e) -> p t e", t=NT),
                                   before[:, :, :], ALU.add))
            link_v(V.tensor_tensor(over[0][:, :], before[:, NT - 1, :], tot[:, NT - 1, :], ALU.add))
            link_v(V.tensor_scalar(over[0][:, :], over[0][:, :], 1.0, -1.0, ALU.max, ALU.add))
            link_v(V.tensor_copy(c_int[:, :], over[0][:, :]))
            link_v(V.tensor_scalar(c_int[:, :], c_int[:, :], 7, None, ALU.arith_shift_right))
            link_v(V.tensor_copy(over[0][:, :], c_int[:, :]))
            link_v(V.tensor_copy(over[1][:, :], over[0][:, :]))
            src, dst = 1, 2
            for s in (1, 2, 4, 8, 16):
                V.tensor_copy(over[dst][:, 0:s], over[src][:, 0:s])
                link_v(V.tensor_tensor(over[dst][:, s:], over[src][:, s:], over[src][:, 0:N_EXP - s], ALU.add))
                src, dst = dst, src
            upto, spare = over[src], over[dst]
            link_v(V.tensor_tensor(exp_cmp[:, :, :], upto[0:1, :].unsqueeze(1).to_broadcast([1, N_OVER, N_EXP]),
                                   row(R_I16, N_OVER)[0:1, :].unsqueeze(2).to_broadcast([1, N_OVER, N_EXP]), ALU.is_le))
            link_v(V.tensor_reduce(exp_of[:, :], exp_cmp[:, :, :], AX.X, ALU.add))
            link_v(V.tensor_scalar(exp_of[:, :], exp_of[:, :], N_EXP - 1.0, None, ALU.min))
            V.tensor_copy(blk_exp[0:1, 0:N_EXP], row(R_BID, N_EXP)[0:1, :])
            V.tensor_copy(blk_exp[0:1, N_EXP:MAX_BLK], exp_of[:, :])
            link_v(V.tensor_scalar(blk_exp[0:1, MAX_BLK:MAX_BLK + 1], upto[0:1, N_EXP - 1:N_EXP], N_EXP - 3.0, None, ALU.add))
            link_v(V.tensor_tensor(spare[:, :], upto[:, :], over[0][:, :], ALU.subtract))
            link_v(V.scalar_tensor_tensor(out=spare[:, :], in0=spare[:, :], scalar=N_EXP - 1.0, in1=row(R_I32, N_EXP),
                                          op0=ALU.add, op1=ALU.subtract))
            link_v(V.tensor_copy(r_int[:, :, :], rank[:, :, :]))
            link_v(V.tensor_scalar(r_int[:, :, :], r_int[:, :, :], 7, None, ALU.arith_shift_right))
            link_v(V.tensor_copy(r_prod[:, :, :], r_int[:, :, :]))
            link_v(V.scalar_tensor_tensor(out=rank[:, :, :], in0=r_prod[:, :, :], scalar=-float(SLOTS), in1=rank[:, :, :],
                                          op0=ALU.mult, op1=ALU.add))
            link_v(V.tensor_tensor(r_blk[:, :, :], r_prod[:, :, :], bc(spare[:, :], 1, [NT, N_EXP]), ALU.add))
            link_v(V.scalar_tensor_tensor(out=r_blk[:, :, :], in0=r_prod[:, :, :], scalar=0.0, in1=r_blk[:, :, :],
                                          op0=ALU.is_gt, op1=ALU.mult))
            link_v(V.tensor_tensor(r_blk[:, :, :], r_blk[:, :, :], bc(row(R_I32, N_EXP), 1, [NT, N_EXP]), ALU.add))
            link_v(V.scalar_tensor_tensor(out=r_prod[:, :, :], in0=r_blk[:, :, :], scalar=float(SLOTS), in1=rank[:, :, :],
                                          op0=ALU.mult, op1=ALU.add))
            link_v(V.scalar_tensor_tensor(out=rank[:, :, :], in0=rank[:, :, :], scalar=float(MAX_BLK), in1=r_blk[:, :, :],
                                          op0=ALU.mult, op1=ALU.add))
            for k, hot in enumerate((hot1, hot2)):
                for g in range(G):
                    last = V.tensor_tensor(r_mask[:, :, g * EG:(g + 1) * EG], hot[:, :, :],
                                           bc(g_hot[:, :, g], 2, [NT, EG]), ALU.mult)
                link_v(last)
                for value, to in ((rank, sidx_f), (r_prod, dest_f)):
                    link_v(V.tensor_tensor(r_blk[:, :, :], r_mask[:, :, :], value[:, :, :], ALU.mult))
                    link_v(V.tensor_reduce(to[:, k * NT:(k + 1) * NT], r_blk[:, :, :], AX.X, ALU.add))
            V.tensor_copy(sidx[:, :], sidx_f[:, :])
            V.tensor_copy(dest[:, :], dest_f[:, :]).then_inc(dest_ok, 1)

        def dve_norm2(dve, t):
            dve.wait_ge(rs2_ok, t + 1)
            if t == 0:
                dve.wait_ge(mod2_ld, 32)
            if t >= XN:
                dve.wait_ge(h2_st[t - XN], 16)
                dve.wait_ge(h2_pe, KT)
            tile = xn2[t % XN]
            link_v(V.scalar_tensor_tensor(out=tile[:, :], in0=x2[:, t, :], scalar=rstd[:, t:t + 1],
                                          in1=mod2_row[0][:, :], op0=ALU.mult, op1=ALU.mult))
            V.tensor_tensor(tile[:, :], tile[:, :], mod2_row[1][:, :], ALU.add).then_inc(xn2_ok, 1)

        def h2_evac_act(n):
            half, f = n // KT, n % KT
            A.wait_ge(h2_pe, n + 1)
            A.activation(h2T[:, f, half * HALF:(half + 1) * HALF], bank[:, n % 4, :],
                         ACT.Copy).then_inc(h2_act, 1)

        V = nc.vector
        A = nc.scalar

        def merge_dve(half):
            V.wait_ge(mrec_ld, 48 * (half + 1))
            nm = [mrec[:, :, g, :, E + 1] for g in range(NG)]
            den = [mrec[:, :, g, :, E] for g in range(NG)]
            link_v(V.tensor_tensor(msm[:, 0, :, :], nm[0], nm[1], ALU.min))
            link_v(V.tensor_tensor(msm[:, 0, :, :], msm[:, 0, :, :], nm[2], ALU.min))
            for g in range(NG):
                last = V.tensor_tensor(msm[:, 1 + g, :, :], msm[:, 0, :, :], nm[g], ALU.subtract)
            last.then_inc(mrg_d, 1)
            V.wait_ge(mrg_e, half + 1)
            for g in range(NG):
                last = V.tensor_tensor(msm[:, 7 + g, :, :], msm[:, 4 + g, :, :], den[g], ALU.mult)
            link_v(last)
            link_v(V.tensor_tensor(msm[:, 10, :, :], msm[:, 7, :, :], msm[:, 8, :, :], ALU.add))
            link_v(V.tensor_tensor(msm[:, 10, :, :], msm[:, 10, :, :], msm[:, 9, :, :], ALU.add))
            link_v(V.reciprocal(msm[:, 11, :, :], msm[:, 10, :, :]))
            for g in range(NG):
                last = V.tensor_tensor(msm[:, 7 + g, :, :], msm[:, 4 + g, :, :], msm[:, 11, :, :], ALU.mult)
            link_v(last)
            if half:
                V.wait_ge(mrg_pe, 1)
            for g in range(NG):
                w = msm[:, 7 + g, :, :].unsqueeze(3).to_broadcast([P, 4, 4, E])
                last = V.tensor_tensor(macc[1 if g else 0][:, :, :, :], mrec[:, :, g, :, 0:E], w, ALU.mult)
                if g:
                    link_v(last)
                    last = V.tensor_tensor(macc[0][:, :, :, :], macc[0][:, :, :, :], macc[1][:, :, :, :], ALU.add)
                if g < NG - 1:
                    link_v(last)
            last.then_inc(mrg_y, 1)

        def merge_act(half):
            A.wait_ge(mrg_d, half + 1)
            A.activation(msm[:, 4:7, :, :], msm[:, 1:4, :, :], ACT.Exp).then_inc(mrg_e, 1)

        def merge_turn(half):
            pe = nc.tensor
            pe.wait_ge(mrg_y, half + 1)
            if half:
                pe.wait_ge(mrg_ev, 1)
            else:
                pe.wait_ge(pT_act, gbase[6] // 2)
                pe.wait_ge(pT_dve, gbase[6] // 2)
            y = macc[0][:, :, :, :].rearrange("p t h e -> p t (h e)")
            for f in range(2):
                for t in range(4):
                    mm = pe.transpose(bank[:, 5 + f, t * P:(t + 1) * P], y[:, t, f * P:(f + 1) * P], ident)
            mm.then_inc(mrg_pe, 1)

        def merge_out(half):
            A.wait_ge(mrg_pe, half + 1)
            for f in range(2):
                last = A.activation(y_f[:, 4 + f, half * HALF:(half + 1) * HALF], bank[:, 5 + f, :], ACT.Copy)
            last.then_inc(mrg_ev, 1)

        @block.sync
        def _(sp):
            sp.dma_start(consts[:, :], cst).then_inc(rows_ld, 16)
            for r0, src in small_rows[3:6]:
                sp.dma_start(rows[r0:r0 + src.shape[0], :], src).then_inc(rows_ld, 16)
            w_ada_v = w_ada.rearrange("(k p) n -> p k n", p=P)
            for n in range(4):
                sp.dma_start(ada_w[n][:, :, :], w_ada_v[:, :, n * 256:(n + 1) * 256]).then_inc(ada_ld[n], 16)
            for t in range(0, NT, 2):
                sp.dma_start(xt[:, t:t + 2, :], x[t * P:(t + 2) * P, :].rearrange("(t p) n -> p t n", p=P)).then_inc(tile_ld[t // 2], 16)
            for n in range(4, ADA_FIRST):
                sp.wait_ge(ada_pe, n - 3)
                sp.dma_start(ada_w[n % 4][:, :, :], w_ada_v[:, :, n * 256:(n + 1) * 256]).then_inc(ada_ld[n % 4], 16)
            sp.wait_ge(ada_pe, ADA_FIRST)
            for j in range(len(jobs) + 1):
                if j < len(jobs):
                    for i, (raw, src) in enumerate(raw_parts(j)):
                        if j:
                            sp.wait_ge(w_lo_ok, 2 * j)
                        sp.dma_start(raw, src).then_inc(w_ld[i], 16)
                if 1 <= j <= J_FOX and jobs[j - 1][0] == "qk":
                    jp = (j - 1) // 3 * 2 + (j - 1) % 3 - 1
                    g, h0 = jp // 2, 2 * (jp % 2)
                    sp.wait_ge(y_ok, 16 * (jp + 1))
                    sp.wait_ge(exp_ok, 16 * (jp + 1))
                    dst = d_rec[g, :, h0 * UW:(h0 + 2) * UW]
                    for q in range(NT):
                        o = (q * P, q // 2 + 512 * (q % 2), q)[g]
                        n = ORDER_STEP[g]
                        sp.dma_start(dst[o:min(o + n * P, T):n, :], rec[jp % 2][:, q, :]).then_inc(rec_st[jp % 2], 16)
                if j == J_FOX + 1:
                    sp.wait_ge(rec_st[0], 128 * NG)
                    sp.wait_ge(rec_st[1], 128 * NG)
                    for half in range(2):
                        if half:
                            sp.wait_ge(mrg_y, 1)
                        for g in range(NG):
                            src = d_rec[g, half * HALF:(half + 1) * HALF, :].rearrange("(t p) w -> p t w", p=P)
                            sp.dma_start(mrec[:, :, g, :, :].rearrange("p t h w -> p t (h w)"), src).then_inc(mrec_ld, 16)
                if j == J_FOX + 2:
                    sp.wait_ge(cumT_ev, 1)
                    sp.dma_start(d_cum, cumT[:, :]).then_inc(cum_st, 16)
                    sp.wait_ge(cum_st, 16)
                if j >= J_FOX + 2 and j < len(jobs):
                    p = j - J_FOX - 2
                    sp.wait_ge(min_ok, 16 * (6 + p))
                    sp.dma_start(cum_row[:, :, :].rearrange("p h t -> p (h t)"),
                                 d_cum[16 * p:16 * p + 16, :].rearrange("a b -> (a b)").partition_broadcast(P)).then_inc(cum_ld, 16)
            sp.wait_ge(proj_pe, 40)
            for f in range(KT):
                for i, raw, src in g_sources(f):
                    if f:
                        sp.wait_ge(g_lo_ok, 3 * (f - 1) + i + 1)
                    sp.dma_start(raw, src).then_inc(g_ld[i], 16)
                if f == 0:
                    sp.wait_ge(mod_st, 16 * (ADA_CHUNKS - ADA_FIRST))
                    sp.wait_ge(min_ok, 160)
                    for i, r in enumerate((16, 40)):
                        sp.dma_start(gate_row[i][:, :], d_mod[r:r + 8, :].rearrange("a b -> (a b)").partition_broadcast(P)).then_inc(gate_ld, 16)
            sp.wait_ge(gate_pe, 64)
            for cc in range(3):
                sp.dma_start(o_raw[cc][:, :, :], w_out.rearrange("(k p) n -> p k n", p=P)[:, :, cc * OC:(cc + 1) * OC]).then_inc(o_ld[cc], 16)
            sp.wait_ge(merged_ok, 16)
            sp.dma_start(x2[:, :, :], x.rearrange("(t p) n -> p t n", p=P)).then_inc(x2_ld, 16)
            sp.wait_ge(o_lo_ok, 1)
            sp.dma_start(o_raw[0][:, :, :], w_out.rearrange("(k p) n -> p k n", p=P)[:, :, 3 * OC:4 * OC]).then_inc(o_ld[0], 16)
            sp.wait_ge(o_lo_ok, 3)
            sp.dma_start(w_rt[:, :, 0:N_GROUPS], w_rg.rearrange("(k p) n -> p k n", p=P)).then_inc(rt_ld, 16)
            sp.dma_start(w_rt[:, :, N_GROUPS:], w_re.rearrange("(k p) n -> p k n", p=P)).then_inc(rt_ld, 16)
            sp.wait_ge(o_pe, 24)
            for i, r in enumerate((32, 24)):
                sp.dma_start(mod2_row[i][:, :], d_mod[r:r + 8, :].rearrange("a b -> (a b)").partition_broadcast(P)).then_inc(mod2_ld, 16)
            for t in range(NT):
                sp.wait_ge(xn2_ok, t + 1)
                sp.dma_start(d_h2[t * P:(t + 1) * P, :], xn2[t % XN][:, :]).then_inc(h2_st[min(t, 2)], 16)
            sp.wait_ge(h2_pe, 2 * KT)
            sp.wait_ge(h2_st[2], 16 * (NT - 2))
            sp_up(sp, 0, 0)
            sp_up(sp, 1, 1)
            sp_down(sp, 1, 0)
            sp.wait_ge(dest_ok, 1)
            more = sp.value_load(blk_exp[0:1, MAX_BLK:MAX_BLK + 1], min_val=N_EXP - 3, max_val=MAX_BLK - 4)
            with sp.Fori(0, more + 1) as i:
                up = sp.value_load(blk_exp[0:1, bass.ds(i + 2, 1)], min_val=0, max_val=N_EXP - 1)
                down = sp.value_load(blk_exp[0:1, bass.ds(i + 1, 1)], min_val=0, max_val=N_EXP - 1)
                sp_up(sp, i + 2, up)
                sp_down(sp, i + 2, down)
            final = sp.value_load(blk_exp[0:1, bass.ds(more + 2, 1)], min_val=0, max_val=N_EXP - 1)
            sp_down(sp, more + 3, final, 0)
            for t in range(NT):
                sp.wait_ge(f_pool, t + 1)
                sp.dma_start(out[t * P:(t + 1) * P, :], x2[:, t, :]).then_inc(out_st, 16)
            sp.wait_ge(out_st, 16 * NT)

        @block.gpsimd
        def _(pool):
            pool.memset(ones[:, :], 1.0).then_inc(pool_set, 1)
            pool.memset(eps_col[:, :], EPS).then_inc(pool_set, 1)
            pool.wait_ge(rel_ev, 1)
            for g in range(NG):
                pool.dma_start(d_rel[4 * g:4 * g + 4, :, :], relrow[:, g, :].unsqueeze(1).to_broadcast([4, P, 384])).then_inc(rel_st, 16)
            pool.wait_ge(rel_st, 48)
            row = P * 384
            for h in range(DIL_HEADS):
                if h < 8:
                    src = bass.AP(d_rel.tensor, offset=h * row + 127, ap=[[383, P], [1, 256]])
                    pool.dma_start(bias01[:, h, :], src).then_inc(bias_ld, 16)
                else:
                    src = bass.AP(d_rel.tensor, offset=h * row + 255, ap=[[383, P], [1, P]])
                    pool.dma_start(bias2[:, h - 8, :], src).then_inc(bias_ld, 16)
            pool.memset(slot_tok[:, :], 0)
            pool.iota(tok_id[:, :], pattern=[[P, NT]], base=0, channel_multiplier=1).then_inc(tok_ok, 1)
            pool.wait_ge(tok_ok, 1)
            slots_v = d_slot.rearrange("(p b) o -> p (b o)", b=MAX_BLK)
            pool.dma_start(slots_v, slot_tok[:, :]).then_inc(slot_z, 16)
            for i in range(N_OVER * SLOTS // T):
                row = N_EXP * SLOTS + i * T
                pool.dma_start(d_y[row:row + T, :], x).then_inc(slot_z, 16)
            pool.wait_ge(slot_z, 16 * (1 + N_OVER * SLOTS // T))
            flat = d_mod.rearrange("a b -> (a b)")
            for n in range(ADA_FIRST, ADA_CHUNKS + 2):
                c = slice(n * 256, (n + 1) * 256)
                if n < ADA_CHUNKS:
                    if n - ADA_FIRST >= 2:
                        pool.wait_ge(bg_row_ok, n - ADA_FIRST - 1)
                    else:
                        pool.wait_ge(h_lo_ok, 2 * KT)
                    pool.dma_start(bg_w[n % 2][:, :, :], w_ada.rearrange("(k p) n -> p k n", p=P)[:, :, c]).then_inc(bg_ld[n % 2], 16)
                    pool.dma_start(bg_b[n % 2][:, :], b_ada[c].rearrange("(a b) -> a b", a=1)).then_inc(bg_ld[n % 2], 16)
                    if bg_gain(n):
                        g = slice(c.start - 4 * D, c.stop - 4 * D)
                        pool.dma_start(bg_g[n % 2][:, :], n2[g].rearrange("(a b) -> a b", a=1)).then_inc(bg_ld[n % 2], 16)
                if n - ADA_FIRST >= 2:
                    m = n - 2
                    pool.wait_ge(bg_row_ok, m - ADA_FIRST + 1)
                    pool.dma_start(flat[m * 256:(m + 1) * 256].rearrange("(a b) -> a b", a=1), bg_row[m % 4][:, :]).then_inc(mod_st, 16)
            pool.wait_ge(dest_ok, 1)
            for k in range(2):
                for t in range(NT):
                    i = k * NT + t
                    pool.indirect_dma_start(d_slot, bass.IndirectOffsetOnAxis(ap=sidx[:, i:i + 1], axis=0),
                                            tok_id[:, t:t + 1], None).then_inc(scat, 16)
            pool.wait_ge(scat, 16 * 2 * NT)
            pool.dma_start(slot_tok[:, :], slots_v).then_inc(slot_ld, 16)
            pool.wait_ge(slot_ld, 16)
            for i in range(3):
                pool.wait_ge(h2_st[i], 16 * (1 if i < 2 else NT - 2))
            pool_index(pool, 0, first=True)
            pool_gather(pool)
            pool_index(pool, 1)
            pool_gather(pool)
            pool_index(pool, 2)
            more = pool.value_load(blk_exp[0:1, MAX_BLK:MAX_BLK + 1], min_val=N_EXP - 3, max_val=MAX_BLK - 4)
            with pool.Fori(0, more + 1) as i:
                pool_gather(pool)
                pool_index(pool, i + 3)
            pool.wait_ge(ye_end, 16)
            for t in range(NT):
                for k in range(2):
                    pool.indirect_dma_start(y_slot[2 * t + k][:, :], None, d_y,
                                            bass.IndirectOffsetOnAxis(ap=dest[:, k * NT + t:k * NT + t + 1], axis=0)).then_inc(slot_y[t // 2], 16)
            for t in range(NT):
                pool.wait_ge(f_dve, 2 * t + 2)
                pool.tensor_tensor(x2[:, t, :], x2[:, t, :], y_sum[t % 4][:, :], ALU.add).then_inc(f_pool, 1)

        @block.scalar
        def _(act):
            act.add_instruction(mybir.InstLoadActFuncSet(name=nc.get_next_instruction_name(),
                                                         act_func_set_id=EXP_AND_LN, engine=act.engine))
            for r0, src in small_rows[0:3]:
                A.dma_start(rows[r0:r0 + src.shape[0], :], src).then_inc(rows_ld, 16)
            A.dma_start(ohs[0:33, :], oh).then_inc(small_ld, 16)
            A.dma_start(tab[0:32, :], rel).then_inc(small_ld, 16)
            A.dma_start(bfr[:, :], b_f.partition_broadcast(P)).then_inc(small_ld, 16)
            A.dma_start(brr[:, 0:N_GROUPS], b_rg.partition_broadcast(P)).then_inc(small_ld, 16)
            A.dma_start(brr[:, N_GROUPS:], b_re.partition_broadcast(P)).then_inc(small_ld, 16)
            act.wait_ge(rowsT_pe, 1)
            A.activation(col[:, :], bank[:, 0, 0:N_ROWS], ACT.Copy).then_inc(col_ok, 1)
            act.wait_ge(col_ok, 1)
            A.activation(silu_t[:, :], col[:, C_C:C_C + KT], ACT.Exp, scale=-1.0).then_inc(silu_e, 1)
            act.wait_ge(pool_set, 2)
            for t in range(NT):
                act.wait_ge(tile_ld[t // 2], 16)
                link_a(A.activation(junk[:, :], xt[:, t, :], ACT.Square, accum_out=ssq[:, t:t + 1]))
            link_a(A.activation(rstd[:, :], ssq[:, :], ACT.Ln, scale=1.0 / D, bias=eps_col[:, :]))
            A.activation(rstd[:, :], rstd[:, :], ACT.Exp, scale=-0.5).then_inc(rstd_ok, 1)
            for n in range(ADA_FIRST):
                act.wait_ge(ada_pe, n + 1)
                A.activation(ada_row[:, n * 256:(n + 1) * 256], bank[0:1, 4 + n % 4, 0:256], ACT.Copy).then_inc(ada_ev, 1)
            act.wait_ge(scl_ok, 1)
            for n in range(2 * KT):
                f, half = n // 2, n % 2
                if n == 10:
                    act_split(act, 0)
                act.wait_ge(xT_pe, n + 1)
                if n >= 2:
                    act.wait_ge(h_lo_ok, n - 1)
                A.activation(h_tmp[n % 2][:, :], bank[:, n % 4, :], ACT.Identity, scale=scale1[:, f:f + 1],
                             bias=mod[:, f:f + 1]).then_inc(xT_act, 1)
            vj = 0
            for j, (kind, _, _) in enumerate(jobs):
                if kind == "v":
                    ev_values(act, act_copy, j, vj, 0, v_ev_act)
                    vj += 1
                    if j >= J_FOX:
                        merge_act(j - J_FOX)
                    act_split(act, j + 1)
                    if j == J_FOX + 1:
                        merge_out(0)
                        act.wait_ge(fg_ok, 1)
                        link_a(A.activation(fg[3][:, :, :], fg[2][:, :, :], ACT.Exp, scale=-1.0))
                        A.activation(fg[4][:, :, :], fg[3][:, :, :], ACT.Ln, bias=ones[:, 0:1]).then_inc(fg_act, 1)
                        act.wait_ge(cumT_pe, 1)
                        A.activation(cumT[:, :], bank[0:64, 4, P:2 * P], ACT.Copy).then_inc(cumT_ev, 1)
                        merge_out(1)
                else:
                    jp = (j // 3 * 2 + j % 3 - 1) if j < J_FOX else j - J_FOX - 2 + 6
                    act_pair(act, jp, j)
            for f in range(KT):
                g_split_hi(f, 0)
                g_split_hi(f, 1)
                if f == 0:
                    act.wait_ge(pv_pe, 160)
                    act.wait_ge(yT_ok, 8)
                    act.wait_ge(mrg_ev, 2)
                    for k in range(6):
                        A.activation(y_hi[:, k, :], y_f[:, k, :], ACT.Copy).then_inc(y_hi_ok, 1)
                g_split_hi(f, 2)
                for half in range(2):
                    n = 2 * f + half
                    act.wait_ge(gate_pe, 4 * n + 2)
                    if n >= 2:
                        act.wait_ge(merged_ok, n - 1)
                    A.activation(g_tmp[n % 2][:, :, :], bank[:, 4 * half:4 * half + 2, :], ACT.Exp, scale=-1.0).then_inc(gate_e, 1)
                    act.wait_ge(gate_e, 3 * n + 1)
                    A.activation(g_tmp[n % 2][:, :, :], g_tmp[n % 2][:, :, :], ACT.Ln, bias=ones[:, 0:1]).then_inc(gate_e, 1)
                    act.wait_ge(gate_e, 3 * n + 2)
                    A.activation(g_tmp[n % 2][:, :, :], g_tmp[n % 2][:, :, :], ACT.Exp, scale=-1.0).then_inc(gate_e, 1)
            act.wait_ge(gate_pe, 64)
            act.wait_ge(merged_ok, 16)
            act.wait_ge(o_ld[0], 16)
            A.activation(o_hi[0][:, :, :], o_raw[0][:, :, :], ACT.Copy).then_inc(o_hi_ok, 1)
            for k in range(KT):
                A.activation(m_hi[:, k, :], merged[:, k, :], ACT.Copy).then_inc(m_hi_ok, 1)
            for cc in range(1, 4):
                act.wait_ge(o_ld[cc % 3], 32 if cc == 3 else 16)
                if cc >= 2:
                    act.wait_ge(o_pe, 8 * (cc - 1))
                A.activation(o_hi[cc % 2][:, :, :], o_raw[cc % 3][:, :, :], ACT.Copy).then_inc(o_hi_ok, 1)
            for t in range(NT):
                act.wait_ge(o_done, 24 + t + 1)
                link_a(A.activation(o_junk[:, :], x2[:, t, :], ACT.Square, accum_out=ssq[:, t:t + 1]))
                link_a(A.activation(rstd[:, t:t + 1], ssq[:, t:t + 1], ACT.Ln, scale=1.0 / D, bias=eps_col[:, :]))
                A.activation(rstd[:, t:t + 1], rstd[:, t:t + 1], ACT.Exp, scale=-0.5).then_inc(rs2_ok, 1)
            for n in range(2 * KT):
                h2_evac_act(n)
            act.wait_ge(r_d, 1)
            A.activation(g_ex[:, :, :], g_ex[:, :, :], ACT.Exp).then_inc(r_a, 1)
            act.wait_ge(r_d, 2)
            A.activation(m_ex[:, :], m_ex[:, :], ACT.Exp).then_inc(r_a, 1)
            act.wait_ge(o_pe, 32)
            for i in range(8):
                chunk_hi(0, i, first=True)
            act_xT(0, first=True)
            act_step(0)
            act_step(1)
            more = act.value_load(blk_exp[0:1, MAX_BLK:MAX_BLK + 1], min_val=N_EXP - 3, max_val=MAX_BLK - 4)
            with act.Fori(0, more) as i:
                act_step(i + 2)
            act_step(more + 2, last=True)
            act_aT(more + 2)
            act_y(more + 2, 0)
            store_y(more + 2, ye_end)
            for t in range(NT):
                act.wait_ge(slot_y[t // 2], 64)
                A.activation(y_slot[2 * t][:, :], y_slot[2 * t][:, :], ACT.Copy, scale=wts[:, t:t + 1]).then_inc(f_act, 1)

        @block.vector
        def _(dve):
            dve.wait_ge(silu_e, 1)
            link_v(V.tensor_scalar(silu_t[:, :], silu_t[:, :], 1.0, None, ALU.add))
            link_v(V.reciprocal(silu_t[:, :], silu_t[:, :]))
            V.tensor_tensor(silu_c[:, :], col[:, C_C:C_C + KT], silu_t[:, :], ALU.mult).then_inc(col_ok, 1)
            V.tensor_scalar(qgain[:, :], col[:, C_QG:C_QG + 10], -(E ** -0.5), None, ALU.mult).then_inc(col_ok, 1)
            dve.wait_ge(small_ld, 16 * N_SMALL)
            V.memset(tab[32:33, :], 1.0).then_inc(bf_set, 1)
            V.tensor_copy(id_bf[:, :], ident).then_inc(bf_set, 1)
            V.tensor_copy(cm_bf[:, :], consts[:, K_CM:K_CM + P]).then_inc(bf_set, 1)
            dve.wait_ge(rel_pe, 1)
            V.tensor_copy(relrow[:, :, :], bank[0:4, 1:4, 0:384]).then_inc(rel_ev, 1)
            dve.wait_ge(rstd_ok, 1)
            for t in range(NT):
                V.tensor_scalar(xt[:, t, :], xt[:, t, :], rstd[:, t:t + 1], None, ALU.mult).then_inc(xn_ok, 1)
            dve.wait_ge(adaT_pe, 1)
            link_v(V.tensor_tensor(mod[:, :], bank[:, 3, 0:16], col[:, C_BADA:C_BADA + 16], ALU.add))
            V.scalar_tensor_tensor(out=scale1[:, :], in0=mod[:, 8:16], scalar=1.0, in1=col[:, C_N1:C_N1 + KT],
                                   op0=ALU.add, op1=ALU.mult).then_inc(scl_ok, 1)
            for n in range(2 * KT):
                f, half = n // 2, n % 2
                t = slice(half * HALF, (half + 1) * HALF)
                if n == 10:
                    dve_split(dve, 0)
                dve.wait_ge(xT_act, n + 1)
                V.tensor_copy(h_hi[:, f, t], h_tmp[n % 2][:, :]).then_inc(h_hi_ok, 1)
                dve.wait_ge(h_hi_ok, n + 1)
                V.tensor_tensor(h_lo[:, f, t], h_tmp[n % 2][:, :], h_hi[:, f, t].bitcast(F32),
                                ALU.subtract).then_inc(h_lo_ok, 1)
            dve.wait_ge(bias_ld, 16 * DIL_HEADS)
            vj = 0
            for j, (kind, _, _) in enumerate(jobs):
                if kind == "v":
                    dve_ada_bg(dve, j)
                    ev_values(dve, V.tensor_copy, j, vj, 1, v_ev_dve)
                    vj += 1
                    if j >= J_FOX:
                        merge_dve(j - J_FOX)
                    dve_split(dve, j + 1)
                    if j == J_FOX + 1:
                        dve.wait_ge(v_ev_act, 20)
                        dve.wait_ge(v_ev_dve, 20)
                        link_v(V.tensor_tensor(fg[1][:, :, :], fg[0][:, :, :],
                                               bfr[:, :].unsqueeze(2).to_broadcast([P, FOX_HEADS, NT]), ALU.add))
                        V.scalar_tensor_tensor(out=fg[2][:, :, :], in0=fg[1][:, :, :], scalar=-1.0,
                                               in1=fg[1][:, :, :], op0=ALU.mult, op1=ALU.max).then_inc(fg_ok, 1)
                        dve.wait_ge(fg_act, 1)
                        V.scalar_tensor_tensor(out=fg[5][:, :, :], in0=fg[1][:, :, :], scalar=0.0, in1=fg[4][:, :, :],
                                               op0=ALU.min, op1=ALU.subtract).then_inc(fg_ok, 1)
                        dve.wait_ge(fg_ok, 2)
                        link_v(V.memset(fg[1][:, :, 0:1], 0.0))
                        dve.wait_ge(cum_pe, 1)
                        tot = bank[:, 4, 64:128].rearrange("p (h t) -> p h t", t=NT)
                        for t in range(1, NT):
                            link_v(V.tensor_tensor(fg[1][:, :, t:t + 1], fg[1][:, :, t - 1:t], tot[:, :, t - 1:t], ALU.add))
                        V.tensor_tensor(fg[2][:, :, :], bank[:, 4, 0:64].rearrange("p (h t) -> p h t", t=NT),
                                        fg[1][:, :, :], ALU.add).then_inc(cum_dve, 1)
                else:
                    jp = (j // 3 * 2 + j % 3 - 1) if j < J_FOX else j - J_FOX - 2 + 6
                    dve_pair(dve, jp, j)
            for f in range(KT):
                g_split_lo(f, 0)
                g_split_lo(f, 1)
                if f == 0:
                    for k in range(6):
                        dve.wait_ge(y_hi_ok, k + 1)
                        V.tensor_tensor(y_lo[:, k, :], y_f[:, k, :], y_hi[:, k, :].bitcast(F32),
                                        ALU.subtract).then_inc(y_lo_ok, 1)
                g_split_lo(f, 2)
                for half in range(2):
                    n = 2 * f + half
                    g = g_tmp[n % 2]
                    dve.wait_ge(gate_e, 3 * n + 3)
                    dve.wait_ge(gate_pe, 4 * n + 4)
                    link_v(V.tensor_tensor(g[:, :, :], g[:, :, :], bank[:, 4 * half + 2:4 * half + 4, :], ALU.mult))
                    V.tensor_tensor(merged[:, f, half * HALF:(half + 1) * HALF], g[:, 0, :], g[:, 1, :],
                                    ALU.add).then_inc(merged_ok, 1)
            dve.wait_ge(o_hi_ok, 1)
            V.tensor_tensor(o_lo[0][:, :, :], o_raw[0][:, :, :], o_hi[0][:, :, :].bitcast(F32), ALU.subtract).then_inc(o_lo_ok, 1)
            for k in range(KT):
                dve.wait_ge(m_hi_ok, k + 1)
                V.tensor_tensor(m_lo[:, k, :], merged[:, k, :], m_hi[:, k, :].bitcast(F32), ALU.subtract).then_inc(m_lo_ok, 1)
            dve.wait_ge(m_lo_ok, KT)
            for cc in range(4):
                if cc < 3:
                    dve.wait_ge(o_hi_ok, cc + 2)
                    V.tensor_tensor(o_lo[(cc + 1) % 2][:, :, :], o_raw[(cc + 1) % 3][:, :, :],
                                    o_hi[(cc + 1) % 2][:, :, :].bitcast(F32), ALU.subtract).then_inc(o_lo_ok, 1)
                if cc == 0:
                    dve.wait_ge(gate_ld, 32)
                    dve.wait_ge(x2_ld, 16)
                c = slice(cc * OC, (cc + 1) * OC)
                for t in range(NT):
                    dve.wait_ge(o_pe, 8 * cc + t + 1)
                    link_v(V.tensor_tensor(o_tmp[:, t % 2, :], bank[:, t, (cc % 2) * OC:(cc % 2 + 1) * OC], gate_row[0][:, c], ALU.mult))
                    V.tensor_tensor(x2[:, t, c], x2[:, t, c], o_tmp[:, t % 2, :], ALU.add).then_inc(o_done, 1)
                    if cc == 3 and t:
                        dve_norm2(dve, t - 1)
            dve_norm2(dve, NT - 1)
            dve_route()
            for i in range(8):
                chunk_lo(0, i, first=True)
            dve_xT(0)
            dve_step(0)
            dve_step(1)
            more = dve.value_load(blk_exp[0:1, MAX_BLK:MAX_BLK + 1], min_val=N_EXP - 3, max_val=MAX_BLK - 4)
            with dve.Fori(0, more) as i:
                dve_step(i + 2)
            dve_step(more + 2, last=True)
            dve_aT(more + 2)
            dve_y(more + 2, 0)
            for t in range(NT):
                dve.wait_ge(f_act, t + 1)
                dve.wait_ge(slot_y[t // 2], 64)
                if t >= 4:
                    dve.wait_ge(f_pool, t - 3)
                V.scalar_tensor_tensor(out=y_sum[t % 4][:, :], in0=y_slot[2 * t + 1][:, :], scalar=wts[:, NT + t:NT + t + 1],
                                       in1=y_slot[2 * t][:, :], op0=ALU.mult, op1=ALU.add).then_inc(f_dve, 1)
                dve.wait_ge(f_dve, 2 * t + 1)
                V.tensor_tensor(y_sum[t % 4][:, :], y_sum[t % 4][:, :], gate_row[1][:, :], ALU.mult).then_inc(f_dve, 1)

        @block.tensor
        def _(pe):
            pe.wait_ge(rows_ld, 16 * N_ROWS_LD)
            nc.tensor.transpose(bank[:, 0, 0:N_ROWS], rows[0:N_ROWS, :], ident[0:N_ROWS, 0:N_ROWS]).then_inc(rowsT_pe, 1)
            pe.wait_ge(col_ok, 2)
            for n in range(ADA_FIRST):
                if n == 4:
                    pe.wait_ge(pool_set, 2)
                    pe.wait_ge(bf_set, 1)
                    pe.wait_ge(small_ld, 16 * N_SMALL)
                    for g in range(NG):
                        mm = nc.tensor.matmul(bank[0:4, 1 + g, 0:384], tab[0:33, 4 * g:4 * g + 4],
                                          ohs[0:33, g * 384:(g + 1) * 384],
                                          start=True, stop=True)
                    mm.then_inc(rel_pe, 1)
                pe.wait_ge(ada_ld[n % 4], 16 * (n // 4 + 1))
                if n >= 4:
                    pe.wait_ge(ada_ev, n - 3)
                for k in range(KT):
                    mm = nc.tensor.matmul(bank[0:1, 4 + n % 4, 0:256], silu_c[:, k:k + 1], ada_w[n % 4][:, k, :],
                                          start=(k == 0), stop=(k == KT - 1))
                mm.then_inc(ada_pe, 1)
            pe.wait_ge(ada_ev, ADA_FIRST)
            pe.wait_ge(rel_ev, 1)
            for i in range(2 * KT):
                mm = nc.tensor.matmul(bank[:, 3, i:i + 1], ada_row[:, i * P:(i + 1) * P], ones[0:1, 0:1],
                                      start=True, stop=True)
            mm.then_inc(adaT_pe, 1)
            pe.wait_ge(xn_ok, NT)
            pe.wait_ge(scl_ok, 1)
            for n in range(2 * KT):
                f, half = n // 2, n % 2
                if n >= 4:
                    pe.wait_ge(xT_act, n - 3)
                for t in range(4):
                    mm = nc.tensor.transpose(bank[:, n % 4, t * P:(t + 1) * P], xt[:, 4 * half + t, f * P:(f + 1) * P], ident)
                mm.then_inc(xT_pe, 1)
            pe.wait_ge(h_lo_ok, 2 * KT)
            pe.wait_ge(bf_set, 3)
            vj = 0
            for j, (kind, _, _) in enumerate(jobs):
                if kind == "v":
                    pe_values(pe, j, vj, j // 3 if j < J_FOX else -1)
                    vj += 1
                    if j == J_FOX + 1:
                        merge_turn(0)
                        pe.wait_ge(fg_ok, 2)
                        nc.tensor.matmul(bank[:, 4, 0:64], tri_incl, fg[5][:, :, :].rearrange("p h t -> p (h t)"),
                                         start=True, stop=True)
                        nc.tensor.matmul(bank[:, 4, 64:128], ones[:, :], fg[5][:, :, :].rearrange("p h t -> p (h t)"),
                                         start=True, stop=True).then_inc(cum_pe, 1)
                        pe.wait_ge(cum_dve, 1)
                        nc.tensor.transpose(bank[0:64, 4, P:2 * P], fg[2][:, :, :].rearrange("p h t -> p (h t)"),
                                            ident).then_inc(cumT_pe, 1)
                        merge_turn(1)
                        pe.wait_ge(mrg_ev, 2)
                else:
                    jp = (j // 3 * 2 + j % 3 - 1) if j < J_FOX else j - J_FOX - 2 + 6
                    pe_pair(pe, jp, j)
            pe.wait_ge(min_ok, 160)
            pe.wait_ge(y_ok, 160)
            pe.wait_ge(yT_ok, 8)
            for f in range(KT):
                for half in range(2):
                    n = 2 * f + half
                    t = slice(half * HALF, (half + 1) * HALF)
                    if n >= 2:
                        pe.wait_ge(merged_ok, n - 1)
                    for i in range(2):
                        pe.wait_ge(g_lo_ok, 3 * f + i + 1)
                        for k in range(KT):
                            mm = three(bank[:, 4 * half + i, :], (g_hi[i][:, k, :], g_lo[i][:, k, :]),
                                       (h_hi[:, k, t], h_lo[:, k, t]), k == 0, k == KT - 1)
                        mm.then_inc(gate_pe, 1)
                    pe.wait_ge(g_lo_ok, 3 * f + 3)
                    for i, ks in enumerate((range(0, 4), range(4, 6))):
                        for k in ks:
                            if n == 0:
                                pe.wait_ge(y_lo_ok, k + 1)
                            mm = three(bank[:, 4 * half + 2 + i, :], (g_hi[2][:, k, :], g_lo[2][:, k, :]),
                                       (y_hi[:, k, t], y_lo[:, k, t]), k == ks[0], k == ks[-1])
                        mm.then_inc(gate_pe, 1)
            pe.wait_ge(merged_ok, 16)
            pe.wait_ge(o_lo_ok, 1)
            for k in range(KT):
                pe.wait_ge(m_lo_ok, k + 1)
                for t in range(NT):
                    mm = three(bank[:, t, 0:OC], (m_hi[:, k, t * P:(t + 1) * P], m_lo[:, k, t * P:(t + 1) * P]),
                               (o_hi[0][:, k, :], o_lo[0][:, k, :]), k == 0, k == KT - 1)
                    if k == KT - 1:
                        mm.then_inc(o_pe, 1)
            for cc in range(1, 4):
                pe.wait_ge(o_lo_ok, cc + 1)
                for t in range(NT):
                    pe.wait_ge(o_done, 8 * (cc - 1) + t + 1)
                    for k in range(KT):
                        mm = three(bank[:, t, (cc % 2) * OC:(cc % 2 + 1) * OC],
                                   (m_hi[:, k, t * P:(t + 1) * P], m_lo[:, k, t * P:(t + 1) * P]),
                                   (o_hi[cc % 2][:, k, :], o_lo[cc % 2][:, k, :]), k == 0, k == KT - 1)
                    mm.then_inc(o_pe, 1)
            for half in range(2):
                pe.wait_ge(xn2_ok, 4 * half + 4)
                for f in range(KT):
                    n = half * KT + f
                    if n < 4:
                        pe.wait_ge(o_done, 24 + n + 1)
                    else:
                        pe.wait_ge(h2_act, n - 3)
                    for t in range(4):
                        mm = nc.tensor.transpose(bank[:, n % 4, t * P:(t + 1) * P],
                                                 xn2[(4 * half + t) % XN][:, f * P:(f + 1) * P], ident)
                    mm.then_inc(h2_pe, 1)
                pe.wait_ge(h2_act, KT * (half + 1))
                pe.wait_ge(o_done, 32)
                pe.wait_ge(rt_ld, 32)
                for t in range(4 * half, 4 * half + 4):
                    for k in range(KT):
                        mm = nc.tensor.matmul(bank[:, 4, t * N_ROUTE:(t + 1) * N_ROUTE], h2T[:, k, t * P:(t + 1) * P],
                                              w_rt[:, k, :], start=(k == 0), stop=(k == KT - 1))
            mm.then_inc(rt_pe, 1)
            pe.wait_ge(r_d, 3)
            mask = r_mask[:, :, :].rearrange("p t e -> p (t e)")
            nc.tensor.matmul(bank[:, 5, 0:NT * N_EXP], tri_strict, mask, start=True, stop=True)
            nc.tensor.matmul(bank[:, 6, 0:NT * N_EXP], ones[:, :], mask, start=True, stop=True).then_inc(rank_pe, 1)
            pe.wait_ge(dest_ok, 1)
            pe_turn_x(0)
            pe_step(0)
            pe_step(1)
            more = pe.value_load(blk_exp[0:1, MAX_BLK:MAX_BLK + 1], min_val=N_EXP - 3, max_val=MAX_BLK - 4)
            with pe.Fori(0, more) as i:
                pe_step(i + 2)
            pe_step(more + 2, last=True)
            pe_turn_act(more + 2)
            pe_down(more + 2, 0)


def bucket_rows():
    import numpy as np

    half, far = 16, 2048
    hot = np.zeros((33, NG, 384), np.float32)
    for g, dil in enumerate(DILATION):
        for n in range(384):
            m = 255 - n
            if g == 2:
                m = m / 2 if m % 2 == 0 else -1
            if m < 0 or m > P:
                hot[32, g, n] = BIG
                continue
            dist = int(m * dil)
            if dist < half:
                b = dist
            else:
                big = np.log(np.float32(dist) / half) / np.log(far / half) * half
                b = min(half + int(np.float32(big)), 2 * half - 1)
            hot[b, g, n] = -1.0
    return hot.reshape(33, NG * 384)


def shape_constants():
    import numpy as np

    k = np.zeros((P, K_COLS), np.float32)
    i = np.arange(P)
    k[:, K_ID:K_ID + P] = np.eye(P)
    k[:, K_CM:K_CM + P] = np.where(i[None, :] > i[:, None], BIG, 0.0)
    k[:, K_BO:K_BO + P] = (i[None, :] // E == i[:, None] // E)
    k[:, K_TI:K_TI + P] = (i[:, None] <= i[None, :])
    k[:, K_TS:K_TS + P] = (i[:, None] < i[None, :])
    r = k[:, K_ROW:]
    r[:, R_PRI4:R_PRI4 + 4] = np.arange(4, 0, -1)
    r[:, R_PRI8:R_PRI8 + 8] = np.arange(8, 0, -1)
    r[:, R_I32:R_I32 + 32] = np.arange(32)
    r[:, R_I16:R_I16 + 16] = np.arange(16)
    r[:, R_BID:R_BID + MAX_BLK] = np.arange(MAX_BLK)
    return k


NAMES = ["x", "c", "rel_bias_table", "w_ada", "b_ada", "norm1_g", "w_in", "b_forget", "q_gain", "k_gain",
         "w_branch_a", "w_branch_b", "w_out", "norm2_g", "w_router_group", "b_router_group",
         "w_router_expert", "b_router_expert", "w1", "w3", "w2"]


def kernel(**inputs):
    import numpy as np
    import concourse.bacc as bacc
    from concourse.bass_utils import run_bass_kernel_spmd

    nc = bacc.Bacc("TRN2", target_bir_lowering=False, num_devices=1)
    arrays, args = {}, []
    for name in NAMES:
        a = np.ascontiguousarray(inputs[name])
        arrays[f"in_{name}"] = a.reshape(a.shape[1:]) if name != "rel_bias_table" else a
    arrays["shape_constants"] = shape_constants()
    arrays["bucket_rows"] = bucket_rows()
    for name, a in arrays.items():
        args.append(nc.dram_tensor(name, a.shape, mybir.dt.from_np(a.dtype), kind="ExternalInput").ap())
    args.append(nc.dram_tensor("out", (T, D), F32, kind="ExternalOutput").ap())
    build(nc, *args)
    r = run_bass_kernel_spmd(nc, [arrays], core_ids=[0])
    return np.asarray(r.results[0]["out"]).reshape(1, T, D)
```

```python
from contextlib import ExitStack

import concourse.bass as bass
from concourse import mybir
from concourse.alu_op_type import AluOpType as ALU

ACT = mybir.ActivationFunctionType
AX = mybir.AxisListType
F32 = mybir.dt.float32
F32R = mybir.dt.float32r
BF16 = mybir.dt.bfloat16
I32 = mybir.dt.int32
U32 = mybir.dt.uint32

P = 128
T = 1024
D = 1024
KT = D // P
NT = T // P
HALF = 512
E = 64
FOX_HEADS, DIL_HEADS, NG = 8, 12, 3
DILATION = (1, 4, 16)
ORDER_STEP = (1, 4, 8)
FOX_W, DIL_W = FOX_HEADS * E, DIL_HEADS * E
OFF_FQ, OFF_FK, OFF_FV = 0, FOX_W, 2 * FOX_W
OFF_DQ = 3 * FOX_W + FOX_HEADS
OFF_DK, OFF_DV = OFF_DQ + DIL_W, OFF_DQ + 2 * DIL_W
OFF_GA = OFF_DQ + 3 * DIL_W
OFF_GB = OFF_GA + D
N_GROUPS, PER_GROUP = 4, 8
N_EXP = N_GROUPS * PER_GROUP
HID = D // 2
N_ROUTE = N_GROUPS + N_EXP
SLOTS = 128
MAX_BLK = 48
N_OVER = MAX_BLK - N_EXP
UW = E + 2
BIG = 1e30
EXP_AND_LN = 6
N_ROWS_LD, N_SMALL = 7, 5
EPS = 1e-6
C_C, C_N1, C_N2, C_BADA, C_QG, C_KG, N_ROWS = 0, 8, 16, 24, 72, 82, 92
K_ID, K_CM, K_BO, K_TI, K_TS, K_ROW = 0, 128, 256, 384, 512, 640
R_PRI4, R_PRI8, R_IOTA, R_TOK = 0, 4, 12, 12 + P
K_COLS = K_ROW + R_TOK + NT


def build(nc, x, c, rel, w_ada, b_ada, n1, w_in, b_f, qg, kg, w_a, w_b, w_out, n2, w_rg, b_rg,
          w_re, b_re, w1, w3, w2, cst, oh, out):
    KB = 1024
    BASE = 16512
    RP, RA, RH, RB, RY, RW, RS, RK = (BASE + v * KB for v in (0, 15, 47, 111, 143, 167, 193, 201))

    ctx = ExitStack()
    with ctx:
        def at(name, shape, dt, offset):
            return nc.alloc_sbuf_tensor_at(name, shape, dt, offset=offset)

        def sems(text):
            return [ctx.enter_context(nc.semaphore(name)) for name in text.split()]

        def dram(name, shape, dt=F32):
            return nc.dram_tensor(name, shape, dt, kind="Internal").ap()

        cursor = [RP]

        def keep(name, cols, dt=F32):
            t = at(name, [P, cols], dt, cursor[0])
            cursor[0] += (cols * (2 if dt == BF16 else 4) + 31) // 32 * 32
            return t

        consts = keep("consts", K_COLS)
        ones = keep("ones", P)
        ident = consts[:, K_ID:K_ID + P]
        block_ones = consts[:, K_BO:K_BO + P]
        tri_incl = consts[:, K_TI:K_TI + P]
        tri_strict = consts[:, K_TS:K_TS + P]
        wide0 = cursor[0]
        gate_row = [at(f"gate_row{i}", [P, D], F32, wide0 + i * 4096) for i in range(2)]
        cum_row = at("cum_row", [P, 2, T], F32, wide0)
        bias01 = at("bias01", [P, 8, 256], F32, wide0)
        bias2 = at("bias2", [P, 4, P], F32, wide0 + 8192)
        assert wide0 + 8192 + 2048 <= RA
        cursor[0] = RK
        col = keep("col", N_ROWS)
        mod = keep("mod", 16)
        scale1 = keep("scale1", KT)
        eps_col = keep("eps_col", 1)
        id_bf = keep("id_bf", P, BF16)
        cm_bf = keep("cm_bf", P, BF16)
        silu_c = keep("silu_c", KT)
        silu_t = keep("silu_t", KT)
        qgain = keep("qgain", 10)
        ssq = keep("ssq", NT)
        rstd = keep("rstd", NT)
        nmin = keep("nmin", 4)
        denom = keep("denom", 4)
        rden = keep("rden", 4)
        bfr = keep("bfr", FOX_HEADS)
        brr = keep("brr", N_ROUTE)
        tab = keep("tab", DIL_HEADS)
        wts = keep("wts", 2 * NT)
        dest = keep("dest", 2 * NT, U32)
        slot_tok = keep("slot_tok", MAX_BLK, I32)
        blk_exp = keep("blk_exp", MAX_BLK + 2, I32)
        idx_now = keep("idx_now", 1, I32)
        assert cursor[0] <= 229344, cursor[0]

        rows = at("rows", [P, P], F32, RB)
        ohs = at("ohs", [P, NG * 384], F32, RB + 512)
        relrow = at("relrow", [4, NG, 384], F32, RB + 6 * KB)
        ada_w = [at(f"ada_w{i}", [P, KT, 256], F32, RW + i * 8 * KB) for i in range(4)]
        ada_row = at("ada_row", [1, 2 * D], F32, RB + 24 * KB)
        ADA_FIRST, ADA_CHUNKS = 2 * D // 256, 6 * D // 256
        bg_w = [at(f"bg_w{i}", [P, KT, 256], F32, RY + 8 * KB + i * 8 * KB) for i in range(2)]
        bg_b = [at(f"bg_b{i}", [P, 256], F32, RA + (8 + i) * KB) for i in range(2)]
        bg_gain = at("bg_gain", [1, D], F32, RA + 10 * KB)
        bg_row = [at(f"bg_row{i}", [1, 256], F32, RA + (14 + i) * KB) for i in range(2)]
        bg_sum = [at(f"bg_sum{i}", [P, 256], F32, RA + (26 + i) * KB) for i in range(2)]
        xt = at("xt", [P, NT, D], F32, RA)
        junk = at("junk", [P, D], F32, RB + 16 * KB)
        h_tmp = [at(f"h_tmp{i}", [P, HALF], F32, RB + 20 * KB + i * 2 * KB) for i in range(2)]
        h_hi = at("h_hi", [P, KT, T], F32R, RH)
        h_lo = at("h_lo", [P, KT, T], F32R, RH + 32 * KB)
        VN = 4 * E + FOX_HEADS
        v_raw = at("v_raw", [P, KT, VN], F32, RW)
        v_hi = at("v_hi", [P, KT, VN], F32R, RW + 8448)
        v_lo = at("v_lo", [P, KT, VN], F32R, RW + 2 * 8448)
        qk_raw = [at(f"qk_raw{i}", [P, KT, P], F32, RW + i * 4096) for i in range(2)]
        qk_hi = [at(f"qk_hi{i}", [P, KT, P], F32R, RW + 8448 + i * 8192) for i in range(2)]
        qk_lo = [at(f"qk_lo{i}", [P, KT, P], F32R, RW + 8448 + 4096 + i * 8192) for i in range(2)]
        v_fox = at("v_fox", [P, NT, FOX_W], F32, RA)
        v_dil = at("v_dil", [P, NT, 4 * E], F32, RA)
        rec = [at(f"rec{i}", [P, NT, 2 * UW], F32, RA + 16 * KB + i * 4224) for i in range(2)]
        logits = [at(f"logits{i}", [P, T], F32, RB + i * 4096) for i in range(2)]
        prob = [at(f"prob{i}", [P, T], F32, RB + 8 * KB + i * 4096) for i in range(2)]
        probT = [at(f"probT{i}", [P, NT, P], F32, RB + 16 * KB + i * 4096) for i in range(2)]
        square = at("square", [P, HALF], F32, RB + 24 * KB)
        rs_head = at("rs_head", [P, HALF], F32, RB + 26 * KB)
        y_pair = at("y_pair", [P, NT, P], F32, RB + 28 * KB)
        qkT_hi = [at(f"qkT_hi{i}", [P, T], F32R, RS + i * 4096) for i in range(2)]
        dil_lo = [at(f"dil_lo{i}", [P, T], F32R, RY + i * 4096) for i in range(2)]
        fox_lo = [at(f"fox_lo{i}", [P, T], F32R, RA + 16 * KB + i * 4096) for i in range(2)]
        normed = [at(f"normed{i}", [P, HALF], F32, RA + 28 * KB + i * 2048) for i in range(2)]
        fg = [at(f"fg{i}", [P, FOX_HEADS, NT], F32, RA + 25 * KB + i * 256) for i in range(6)]
        cumT = at("cumT", [FOX_HEADS * NT, P], F32, RA + 27 * KB)
        mrec = at("mrec", [P, 4, NG, 4, UW], F32, RB)
        macc = [at(f"macc{i}", [P, 4, 4, E], F32, RB + 13 * KB + i * 4096) for i in range(2)]
        msm = at("msm", [P, 12, 4, 4], F32, RB + 21 * KB)
        y_f = at("y_f", [P, 6, T], F32, RY)
        y_lo = at("y_lo", [P, 6, T], F32R, RY)
        y_hi = at("y_hi", [P, 6, T], F32R, RA)
        merged = at("merged", [P, KT, T], F32, RB)
        g_k = (KT, KT, 6)
        g_raw, g_hi, g_lo = [], [], []
        g_at = RW
        for part, (lst, dt) in {"raw": (g_raw, F32), "hi": (g_hi, F32R), "lo": (g_lo, F32R)}.items():
            for i in range(3):
                lst.append(at(f"g_{part}{i}", [P, g_k[i], P], dt, g_at))
                g_at += g_k[i] * P * 4
        assert g_at <= RK
        g_tmp = [at(f"g_tmp{i}", [P, 2, HALF], F32, RA + 24 * KB + i * 4096) for i in range(2)]
        m_hi = at("m_hi", [P, KT, T], F32R, RH)
        m_lo = at("m_lo", [P, KT, T], F32R, RH + 32 * KB)
        x2 = at("x2", [P, NT, D], F32, RA)
        OC = 256
        o_raw = [at(f"o_raw{i}", [P, KT, OC], F32, RY + i * 8192) for i in range(3)]
        o_hi = [at(f"o_hi{i}", [P, KT, OC], F32R, RW + i * 16384) for i in range(2)]
        o_lo = [at(f"o_lo{i}", [P, KT, OC], F32R, RW + i * 16384 + 8192) for i in range(2)]
        o_tmp = at("o_tmp", [P, 2, OC], F32, RB + 28 * KB)
        o_junk = at("o_junk", [P, D], F32, RW)
        XN = 6
        xn2 = [at(f"xn2_{i}", [P, D], F32, where)
               for i, where in enumerate([RY + i * 4096 for i in range(4)] + [RY + 20 * KB, RW + 4 * KB])]
        mod2_row = [at(f"mod2_row{i}", [P, D], F32, RW + 8 * KB + i * 4096) for i in range(2)]
        w_rt = at("w_rt", [P, KT, N_ROUTE], F32, RY + 16 * KB)
        h2T = at("h2T", [P, KT, T], F32, RB)
        CHUNKS = 12
        e_raw = [at(f"e_raw{i}", [P, 2, HID], F32, RW + i * 4096) for i in range(CHUNKS // 2)]
        e_hi = [at(f"e_hi{i}", [P, 2, HID], F32R, RH + i * 8192) for i in range(CHUNKS)]
        e_lo = [at(f"e_lo{i}", [P, 2, HID], F32R, RH + i * 8192 + 4096) for i in range(CHUNKS)]
        y_e = at("y_e", [P, D], F32, RY)
        gate_act = at("gate_act", [P, HID], F32, RY + 8 * KB)
        act_in = at("act_in", [P, HID], F32, RY + 10 * KB)
        xg = at("xg", [P, D], F32, RY + 12 * KB)
        xT_hi = at("xT_hi", [P, KT, P], F32R, RY + 16 * KB)
        xT_lo = at("xT_lo", [P, KT, P], F32R, RY + 20 * KB)
        aT_hi = at("aT_hi", [P, 4, P], F32R, RW + 30 * KB)
        aT_lo = at("aT_lo", [P, 4, P], F32R, RW + 32 * KB)
        y_slot = [at(f"y_slot{i}", [P, D], F32, RH + i * 4096) for i in range(2 * NT)]
        y_sum = [at(f"y_sum{i}", [P, D], F32, RB + i * 4096) for i in range(4)]
        free = [RW + 24 * KB, RY + 20 * KB + 1024]

        def scratch(name, shape, dt=F32, where=0):
            size = 4
            for v in shape:
                size *= v
            t = at(name, [P] + shape, dt, free[where])
            free[where] += (size + 31) // 32 * 32
            return t

        lg = scratch("lg", [NT, N_ROUTE])
        g_max, g_sum, m_one, m_two, m_ex, m_r, e_first = (
            scratch(n, [NT], where=1) for n in "g_max g_sum m_one m_two m_ex m_r e_first".split())
        g_ex, g_hot = (scratch(n, [NT, N_GROUPS], where=1) for n in "g_ex g_hot".split())
        e_in, e_eq, hot1, hot2, e_next = (scratch(n, [NT, PER_GROUP], where=0) for n in "e_in e_eq hot1 hot2 e_next".split())
        r_prod, r_mask, rank, r_blk = (scratch(n, [NT, N_EXP]) for n in "r_prod r_mask rank r_blk".split())
        r_int = scratch("r_int", [NT, N_EXP], I32)
        assert free[0] <= RW + 34 * KB
        before = at("before", [P, NT, N_EXP], F32, RY + 19 * KB + 512)
        c_int = at("c_int", [P, N_EXP], I32, free[1])
        over = [at(f"over{i}", [P, N_EXP], F32, free[1] + 128 + 128 * i) for i in range(3)]
        dest_f = at("dest_f", [P, 2 * NT], F32, free[1] + 512)
        place_f = at("place_f", [P, 2 * NT], F32, free[1] + 576)
        blk_f = at("blk_f", [P, 2 * NT], F32, free[1] + 640)
        hot_place = at("hot_place", [P, 2 * NT, SLOTS], F32, RY)
        hot_blk = at("hot_blk", [P, 2, NT, MAX_BLK], F32, RY + 8 * KB)
        assert free[1] + 704 <= RW
        exp_cmp = at("exp_cmp", [1, N_OVER, N_EXP], F32, RY + 17 * KB + 512)
        exp_of = at("exp_of", [1, N_OVER], F32, RY + 20 * KB + 512)

        bank = ctx.enter_context(nc.psum_tensor("bank", [P, 8, HALF], F32))

        d_rel = dram("d_rel", [DIL_HEADS, P, 384])
        d_cum = dram("d_cum", [FOX_HEADS * NT, P])
        d_rec = dram("d_rec", [NG, T, 4 * UW])
        d_mod = dram("d_mod", [48, P])
        d_h2 = dram("d_h2", [T, D])
        d_y = dram("d_y", [MAX_BLK * SLOTS, D])

        (rows_ld, small_ld, pool_set, bf_set, rowsT_pe, col_ok, silu_e, rel_pe, rel_ev, rel_st, bias_ld,
         ada_pe, scl_ok, chain_a, chain_v) = sems(
            "rows_ld small_ld pool_set bf_set rowsT_pe col_ok silu_e rel_pe rel_ev rel_st bias_ld "
            "ada_pe scl_ok chain_a chain_v")
        tile_ld = sems(" ".join(f"tile_ld{t}" for t in range(NT // 2)))
        ada_ld = sems(" ".join(f"ada_ld{i}" for i in range(4)))
        rstd_ok, xn_ok, xT_pe, xT_act, h_hi_ok, h_lo_ok = sems(
            "rstd_ok xn_ok xT_pe xT_act h_hi_ok h_lo_ok")
        w_ld = sems("w_ld_a w_ld_b")
        w_hi_ok, w_lo_ok, v_pe, v_ev_act, v_ev_dve = sems(
            "w_hi_ok w_lo_ok v_pe v_ev_act v_ev_dve")
        proj_pe, sq_ok, ss_pe, ln_ok, rs_ok, norm_ok = sems("proj_pe sq_ok ss_pe ln_ok rs_ok norm_ok")
        qkT_hi_ok, qkT_lo_ok = sems("qkT_hi_ok qkT_lo_ok")
        qk_pe, min_ok, exp_ok, turn_pe, pT_act, pT_dve, pv_pe, rden_ok, y_ok, yT_pe, yT_ok = sems(
            "qk_pe min_ok exp_ok turn_pe pT_act pT_dve pv_pe rden_ok y_ok yT_pe yT_ok")
        rec_st = sems("rec_st0 rec_st1")
        fg_ok, fg_act, cum_pe, cum_dve, cumT_pe, cumT_ev, cum_st, cum_ld = sems(
            "fg_ok fg_act cum_pe cum_dve cumT_pe cumT_ev cum_st cum_ld")
        mrec_ld, mrg_d, mrg_e, mrg_y, mrg_pe, mrg_ev = sems("mrec_ld mrg_d mrg_e mrg_y mrg_pe mrg_ev")
        gate_ld, y_hi_ok, y_lo_ok = sems("gate_ld y_hi_ok y_lo_ok")
        mod_st = sems("mod_st0 mod_st1")
        gain_ld, bg_zero = sems("gain_ld bg_zero")
        ada_ev, adaT_pe, bg_pe, bg_row_ok, bg_sum_ok = sems("ada_ev adaT_pe bg_pe bg_row_ok bg_sum_ok")
        bg_ld = sems("bg_ld0 bg_ld1")
        g_ld = sems("g_ld0 g_ld1 g_ld2")
        g_hi_ok, g_lo_ok, gate_pe, gate_e, gated_ok, merged_ok = sems("g_hi_ok g_lo_ok gate_pe gate_e gated_ok merged_ok")
        x2_ld, m_hi_ok, m_lo_ok, o_hi_ok, o_lo_ok, o_pe, o_done = sems("x2_ld m_hi_ok m_lo_ok o_hi_ok o_lo_ok o_pe o_done")
        o_ld = sems("o_ld0 o_ld1 o_ld2")
        rs2_ok, mod2_ld, xn2_ok, h2_pe, h2_act, rt_ld, rt_pe = sems("rs2_ok mod2_ld xn2_ok h2_pe h2_act rt_ld rt_pe")
        h2_st = sems("h2_st0 h2_st1 h2_st2")
        r_d, r_a, rank_pe, fill_st, hot_ok, slot_pe, dest_ok = sems("r_d r_a rank_pe fill_st hot_ok slot_pe dest_ok")
        e_ld = sems(" ".join(f"e_ld{i}" for i in range(CHUNKS // 2)))
        e_hi_ok, e_lo_ok, e_used, xg_ld, xgT_pe, xT_hi_ok, xT_lo_ok = sems(
            "e_hi_ok e_lo_ok e_used xg_ld xgT_pe xT_hi_ok xT_lo_ok")
        idx_ok, ye_end = sems("idx_ok ye_end")
        slot_y = sems(" ".join(f"slot_y{t}" for t in range(NT // 2)))
        sig_e, silu_v, act_ok, actT_pe, aT_hi_ok, aT_lo_ok, ye_act, ye_dve, ye_st = sems(
            "sig_e silu_v act_ok actT_pe aT_hi_ok aT_lo_ok ye_act ye_dve ye_st")
        f_act, f_dve, f_pool, out_st = sems("f_act f_dve f_pool out_st")
        block = ctx.enter_context(nc.Block())

        links = {"a": 0, "v": 0}

        def link_a(ins):
            links["a"] += 1
            ins.then_inc(chain_a, 1)
            nc.scalar.wait_ge(chain_a, links["a"])

        def link_v(ins):
            links["v"] += 1
            ins.then_inc(chain_v, 1)
            nc.vector.wait_ge(chain_v, links["v"])

        small_rows = [(C_C, c.rearrange("(a b) -> a b", b=P)), (C_N1, n1.rearrange("(a b) -> a b", b=P)),
                      (C_N2, n2.rearrange("(a b) -> a b", b=P)), (C_BADA, b_ada.rearrange("(a b) -> a b", b=P)),
                      (C_QG, qg.rearrange("(a b) e -> a (b e)", b=2)), (C_KG, kg.rearrange("(a b) e -> a (b e)", b=2))]

        jobs = []
        for g in range(NG):
            jobs.append(("v", OFF_DV + g * 4 * E, 4 * E))
            for p in range(2):
                jobs.append(("qk", OFF_DQ + (2 * g + p) * P, OFF_DK + (2 * g + p) * P))
        jobs += [("v", OFF_FV, 4 * E), ("v", OFF_FV + 4 * E, VN)]
        for p in range(FOX_HEADS // 2):
            jobs.append(("qk", OFF_FQ + p * P, OFF_FK + p * P))
        J_FOX = 9
        bg_of = {j: 2 for j in range(1, J_FOX)}
        assert sum(bg_of.values()) == ADA_CHUNKS - ADA_FIRST

        def bg_chunks(j):
            n0 = ADA_FIRST + sum(c for i, c in bg_of.items() if i < j)
            return range(n0, n0 + bg_of.get(j, 0))

        BG_STEPS = 5

        def pool_ada_bg(pool, n):
            done = n - ADA_FIRST
            w, total = bg_w[n % 2], bg_sum[n % 2]
            pool.wait_ge(bg_ld[n % 2], 32 * (done // 2 + 1))
            if done >= 2:
                pool.wait_ge(bg_pe, done - 1)
            by_k = silu_c[:, :].unsqueeze(2).to_broadcast([P, KT, 256])
            for step, (out_, a, b, op) in enumerate((
                    (w[:, :, :], w[:, :, :], by_k, ALU.mult),
                    (w[:, 0:4, :], w[:, 0:4, :], w[:, 4:8, :], ALU.add),
                    (w[:, 0:2, :], w[:, 0:2, :], w[:, 2:4, :], ALU.add),
                    (total[:, :], w[:, 0, :], w[:, 1, :], ALU.add),
                    (total[:, :], total[:, :], bg_b[n % 2][:, :], ALU.add))):
                if step:
                    pool.wait_ge(bg_sum_ok, BG_STEPS * done + step)
                pool.tensor_tensor(out_, a, b, op).then_inc(bg_sum_ok, 1)

        def pe_ada_bg(pe, j):
            for i, n in enumerate(bg_chunks(j)):
                done = n - ADA_FIRST
                if done and i == 0:
                    pe.wait_ge(bg_row_ok, done)
                pe.wait_ge(bg_sum_ok, BG_STEPS * (done + 1))
                nc.tensor.matmul(bank[0:1, (4, 6)[i], 0:256], ones[:, 0:1], bg_sum[n % 2][:, :],
                                 start=True, stop=True).then_inc(bg_pe, 1)

        def rows_stored(eng):
            for i in range(2):
                eng.wait_ge(mod_st[i], 16 * (ADA_CHUNKS - ADA_FIRST) // 2)

        def dve_ada_bg(dve, j):
            for i, n in enumerate(bg_chunks(j)):
                dve.wait_ge(bg_pe, n - ADA_FIRST + 1)
                row, src = bg_row[n % 2][:, :], bank[0:1, (4, 6)[i], 0:256]
                if n - ADA_FIRST >= 2:
                    dve.wait_ge(mod_st[n % 2], 16 * ((n - ADA_FIRST) // 2))
                at_col = n * 256 - 4 * D
                if 0 <= at_col < D:
                    dve.wait_ge(gain_ld, 16)
                    last = nc.vector.scalar_tensor_tensor(out=row, in0=src, scalar=1.0, in1=bg_gain[:, at_col:at_col + 256],
                                                          op0=ALU.add, op1=ALU.mult)
                else:
                    last = nc.vector.tensor_copy(row, src)
                last.then_inc(bg_row_ok, 1)

        w_in_v = w_in.rearrange("(k p) n -> p k n", p=P)

        def raw_parts(j):
            kind, a, b = jobs[j]
            if kind == "v":
                return [(v_raw[:, 4 * i:4 * i + 4, 0:b], w_in_v[:, 4 * i:4 * i + 4, a:a + b]) for i in range(2)]
            return [(qk_raw[0][:, :, :], w_in_v[:, :, a:a + P]), (qk_raw[1][:, :, :], w_in_v[:, :, b:b + P])]

        def split_parts(j):
            kind, a, b = jobs[j]
            if kind == "v":
                return [tuple(t[:, 4 * i:4 * i + 4, 0:b] for t in (v_raw, v_hi, v_lo)) for i in range(2)]
            return [(qk_raw[i][:, :, :], qk_hi[i][:, :, :], qk_lo[i][:, :, :]) for i in range(2)]

        def products_done(eng, j):
            if jobs[j][0] == "v":
                eng.wait_ge(v_pe, NT * sum(job[0] == "v" for job in jobs[:j + 1]))
            else:
                eng.wait_ge(proj_pe, 4 * sum(job[0] == "qk" for job in jobs[:j + 1]))

        def quarters(j):
            for i, part in enumerate(split_parts(j)):
                n = part[0].shape[1] // 2
                for q in range(2):
                    yield (i, q == 1) + tuple(t[:, q * n:(q + 1) * n, :] for t in part)

        def act_split(act, j, only=range(4)):
            for n, (i, last, raw, hi, _) in enumerate(quarters(j)):
                if n in only:
                    act.wait_ge(w_ld[i], 16 * (j + 1))
                    if j:
                        products_done(act, j - 1)
                    nc.scalar.activation(hi, raw, ACT.Copy).then_inc(w_hi_ok, 1)

        def dve_split(dve, j, only=range(4)):
            for n, (i, last, raw, hi, lo) in enumerate(quarters(j)):
                if n in only:
                    dve.wait_ge(w_hi_ok, 4 * j + n + 1)
                    nc.vector.tensor_tensor(lo, raw, hi.bitcast(F32), ALU.subtract).then_inc(w_lo_ok, 1)

        PROJ_BANK = (0, 2, 1, 3)

        def tokens_of(view, g, tile):
            if g == 0:
                return view[:, tile * P:(tile + 1) * P]
            if g == 1:
                r, b = tile // 2, tile % 2
                return view[:, r + 512 * b:min(r + 512 * b + 512, T):4]
            return view[:, tile:T:8]

        def placed(view, g, half):
            if g <= 0:
                return view[:, half * HALF:(half + 1) * HALF]
            r = ORDER_STEP[g]
            n = HALF // r
            return view.rearrange("p (r n) -> p n r", r=r)[:, half * n:(half + 1) * n, :]

        def units_of(g):
            out = []
            for q in range(NT):
                for a in range(2):
                    if g < 0:
                        out.append((q, a, 0, (q + 1) * P))
                    elif g == 2 or (g == 0 and q == 0) or (g == 1 and q % 2 == 0):
                        out.append((q, a, q * P, P))
                    else:
                        out.append((q, a, (q - 1) * P, 2 * P))
            return out

        def groups(g):
            n, out = 0, []
            for _, _, _, kw in units_of(g):
                here = []
                for b in range(0, kw // P, 4):
                    here.append((n, list(range(b, min(b + 4, kw // P)))))
                    n += 1
                out.append(here)
            return out, n

        def group_of_pair(jp):
            return jp // 2 if jp < 6 else -1

        gbase = [0]
        for jp in range(10):
            gbase.append(gbase[-1] + groups(group_of_pair(jp))[1])

        def s_at(u, kw):
            if kw <= HALF:
                return bank[:, 2 * (u % 2), 0:kw]
            b = 2 * (u % 2)
            return bank[:, b:b + 2, :].rearrange("p b n -> p (b n)")[:, 0:kw]

        def pe_proj(dst, hi, lo, half, ks):
            t = slice(half * HALF, (half + 1) * HALF)
            for k in ks:
                for n, (w, h) in enumerate(((hi, h_hi), (hi, h_lo), (lo, h_hi))):
                    mm = nc.tensor.matmul(dst, w[:, k, :], h[:, k, t], start=(k == 0 and n == 0),
                                          stop=(k == KT - 1 and n == 2))
            return mm

        def pe_values(pe, j, vj, g):
            kind, a, ncol = jobs[j]
            if bg_of.get(j):
                pe.wait_ge(y_ok, 32 * vj)
                pe.wait_ge(pT_dve, gbase[2 * vj] // 2)
                pe_ada_bg(pe, j)
            for t in range(NT):
                m = vj * NT + t
                if t >= 4:
                    pe.wait_ge(v_ev_dve if t % 2 else v_ev_act, (m - 4) // 2 + 1)
                n = 0
                for k in range(KT):
                    if k % 2 == 0 and t == 0:
                        pe.wait_ge(w_lo_ok, 4 * j + k // 2 + 1)
                    for w, h in ((v_hi, h_hi), (v_hi, h_lo), (v_lo, h_hi)):
                        mm = nc.tensor.matmul(bank[:, t % 4, 0:ncol], tokens_of(h[:, k, :], max(g, 0), t),
                                              w[:, k, 0:ncol], start=(n == 0), stop=(n == 3 * KT - 1))
                        n += 1
                mm.then_inc(v_pe, 1)

        def ev_values(eng, op, j, vj, which, done):
            kind, a, ncol = jobs[j]
            if j == J_FOX:
                rows_stored(eng)
            for t in range(which, NT, 2):
                eng.wait_ge(v_pe, vj * NT + t + 1)
                if j < J_FOX:
                    dst = v_dil[:, t, :]
                else:
                    c0 = (j - J_FOX) * 4 * E
                    dst = v_fox[:, t, c0:c0 + 4 * E]
                last = op(dst, bank[:, t % 4, 0:4 * E])
                if ncol > 4 * E:
                    last = op(fg[0][:, :, t], bank[:, t % 4, 4 * E:VN])
                last.then_inc(done, 1)

        def act_copy(out_, in_):
            return nc.scalar.activation(out_, in_, ACT.Copy)

        V = nc.vector
        A = nc.scalar

        def merge_dve(half):
            V.wait_ge(mrec_ld, 48 * (half + 1))
            nm = [mrec[:, :, g, :, E + 1] for g in range(NG)]
            den = [mrec[:, :, g, :, E] for g in range(NG)]
            link_v(V.tensor_tensor(msm[:, 0, :, :], nm[0], nm[1], ALU.min))
            link_v(V.tensor_tensor(msm[:, 0, :, :], msm[:, 0, :, :], nm[2], ALU.min))
            for g in range(NG):
                last = V.tensor_tensor(msm[:, 1 + g, :, :], msm[:, 0, :, :], nm[g], ALU.subtract)
            last.then_inc(mrg_d, 1)
            V.wait_ge(mrg_e, half + 1)
            for g in range(NG):
                last = V.tensor_tensor(msm[:, 7 + g, :, :], msm[:, 4 + g, :, :], den[g], ALU.mult)
            link_v(last)
            link_v(V.tensor_tensor(msm[:, 10, :, :], msm[:, 7, :, :], msm[:, 8, :, :], ALU.add))
            link_v(V.tensor_tensor(msm[:, 10, :, :], msm[:, 10, :, :], msm[:, 9, :, :], ALU.add))
            link_v(V.reciprocal(msm[:, 11, :, :], msm[:, 10, :, :]))
            for g in range(NG):
                last = V.tensor_tensor(msm[:, 7 + g, :, :], msm[:, 4 + g, :, :], msm[:, 11, :, :], ALU.mult)
            link_v(last)
            if half:
                V.wait_ge(mrg_pe, 1)
            for g in range(NG):
                w = msm[:, 7 + g, :, :].unsqueeze(3).to_broadcast([P, 4, 4, E])
                last = V.tensor_tensor(macc[1 if g else 0][:, :, :, :], mrec[:, :, g, :, 0:E], w, ALU.mult)
                if g:
                    link_v(last)
                    last = V.tensor_tensor(macc[0][:, :, :, :], macc[0][:, :, :, :], macc[1][:, :, :, :], ALU.add)
                if g < NG - 1:
                    link_v(last)
            last.then_inc(mrg_y, 1)

        def merge_act(half):
            A.wait_ge(mrg_d, half + 1)
            A.activation(msm[:, 4:7, :, :], msm[:, 1:4, :, :], ACT.Exp).then_inc(mrg_e, 1)

        def merge_turn(half):
            pe = nc.tensor
            pe.wait_ge(mrg_y, half + 1)
            if half:
                pe.wait_ge(mrg_ev, 1)
            else:
                pe.wait_ge(pT_act, gbase[6] // 2)
                pe.wait_ge(pT_dve, gbase[6] // 2)
            y = macc[0][:, :, :, :].rearrange("p t h e -> p t (h e)")
            for f in range(2):
                for t in range(4):
                    mm = pe.transpose(bank[:, 5 + f, t * P:(t + 1) * P], y[:, t, f * P:(f + 1) * P], ident)
            mm.then_inc(mrg_pe, 1)

        def merge_out(half):
            A.wait_ge(mrg_pe, half + 1)
            for f in range(2):
                last = A.activation(y_f[:, 4 + f, half * HALF:(half + 1) * HALF], bank[:, 5 + f, :], ACT.Copy)
            last.then_inc(mrg_ev, 1)

        def pe_pair(pe, jp, j):
            g = group_of_pair(jp)
            units, (turns, _) = units_of(g), groups(g)
            heads0 = 0 if g >= 0 else 2 * (jp - 6)

            def proj(n, squares=None):
                i, half = n % 2, n // 2
                pe.wait_ge(w_lo_ok, 4 * j + 2 * i + 1)
                pe_proj(bank[:, PROJ_BANK[n], :], qk_hi[i], qk_lo[i], half, range(0, 4))
                if squares is not None:
                    sum_squares(squares)
                pe.wait_ge(w_lo_ok, 4 * j + 2 * i + 2)
                pe_proj(bank[:, PROJ_BANK[n], :], qk_hi[i], qk_lo[i], half, range(4, KT)).then_inc(proj_pe, 1)

            def sum_squares(n):
                pe.wait_ge(sq_ok, 4 * jp + n + 1)
                if 4 * jp + n:
                    pe.wait_ge(ln_ok, 4 * jp + n)
                nc.tensor.matmul(bank[:, 7, :], block_ones, square[:, :], start=True, stop=True).then_inc(ss_pe, 1)

            def scores(u):
                q, a, k0, kw = units[u]
                pe.wait_ge(qkT_lo_ok, 4 * jp + (2 if g <= 0 and q < 4 else 4))
                if u >= 2:
                    pe.wait_ge(min_ok, 16 * jp + u - 1)
                dst = s_at(u, kw)
                h = slice(a * E, (a + 1) * E)
                lo = fox_lo if g < 0 else dil_lo
                for c in range(0, kw, HALF):
                    w = min(HALF, kw - c)
                    diag = g < 0 and c <= q * P < c + w
                    for n, (x, y) in enumerate(((qkT_hi, qkT_hi), (qkT_hi, lo), (lo, qkT_hi))):
                        mm = nc.tensor.matmul(dst[:, c:c + w], x[0][h, q * P:(q + 1) * P], y[1][h, k0 + c:k0 + c + w],
                                              start=n == 0, stop=n == 2 and not diag)
                    if diag:
                        mm = nc.tensor.matmul(dst[:, q * P:(q + 1) * P], id_bf[:, :], cm_bf[:, :],
                                              start=False, stop=True)
                mm.then_inc(qk_pe, 1)

            def turn(u):
                pe.wait_ge(exp_ok, 16 * jp + u + 1)
                for n, blocks in turns[u]:
                    G = gbase[jp] + n
                    if G >= 2:
                        pe.wait_ge((pT_act, pT_dve)[G % 2], G // 2)
                    if n == 1 and bg_of.get(j):
                        pe.wait_ge(bg_row_ok, bg_chunks(j)[-1] - ADA_FIRST + 1)
                    for b in blocks:
                        mm = nc.tensor.transpose(bank[:, 5 + G % 2, (b % 4) * P:(b % 4 + 1) * P],
                                                 prob[u % 2][:, b * P:(b + 1) * P], ident)
                    mm.then_inc(turn_pe, 1)

            def values(u):
                q, a, k0, kw = units[u]
                for n, _ in turns[u]:
                    G = gbase[jp] + n
                    pe.wait_ge((pT_act, pT_dve)[G % 2], G // 2 + 1)
                if u >= 2 or jp:
                    pe.wait_ge(y_ok, 16 * jp + u - 1)
                if u == 0 and bg_of.get(j):
                    pe.wait_ge(bg_row_ok, bg_chunks(j)[0] - ADA_FIRST + 1)
                for b in range(kw // P):
                    if g < 0:
                        v = v_fox[:, b, (heads0 + a) * E:(heads0 + a + 1) * E]
                    else:
                        v = v_dil[:, k0 // P + b, (2 * (jp % 2) + a) * E:(2 * (jp % 2) + a + 1) * E]
                    mm = nc.tensor.matmul(bank[:, (4, 7)[u % 2], 0:E], probT[u % 2][:, b, :], v,
                                          start=(b == 0), stop=(b == kw // P - 1))
                mm.then_inc(pv_pe, 1)

            def turn_y(half):
                pe.wait_ge(y_ok, 16 * jp + (16 if half else 10))
                for q in range(4):
                    mm = nc.tensor.transpose(bank[:, 7, q * P:(q + 1) * P], y_pair[:, 4 * half + q, :], ident)
                mm.then_inc(yT_pe, 1)

            early = g <= 0
            proj(0)
            if jp:
                pe.wait_ge(y_ok, 16 * jp)
            if jp > 6:
                pe.wait_ge(yT_ok, 2 * (jp - 6))
            for n in range(1, 4):
                proj(n, n - 1)
            if jp == 6:
                merge_turn(1)
            if not early:
                sum_squares(3)
                if bg_of.get(j):
                    pe_ada_bg(pe, j)
            scores(0)
            scores(1)
            if early:
                sum_squares(3)
            if bg_of.get(j) and early:
                pe_ada_bg(pe, j)
            if jp == 6:
                pe.wait_ge(mrg_ev, 2)
            for u in range(16):
                turn(u)
                if g < 0 and u == 12:
                    pe.wait_ge(yT_ok, 2 * (jp - 6) + 1)
                if u:
                    values(u - 1)
                if g < 0 and u == 10:
                    turn_y(0)
                if u + 2 < 16:
                    scores(u + 2)
            values(15)
            if g < 0:
                turn_y(1)

        def act_pair(act, jp, j):
            g = group_of_pair(jp)
            units, (turns, _) = units_of(g), groups(g)
            early = g <= 0

            def norm(n):
                N = 4 * jp + n
                act.wait_ge(proj_pe, N + 1)
                if N:
                    act.wait_ge(ss_pe, N)
                nc.scalar.activation(square[:, :], bank[:, PROJ_BANK[n], :], ACT.Square).then_inc(sq_ok, 1)

            def root(n):
                N = 4 * jp + n
                act.wait_ge(ss_pe, N + 1)
                if N:
                    act.wait_ge(norm_ok, N)
                nc.scalar.activation(rs_head[:, :], bank[:, 7, :], ACT.Ln, scale=1.0 / E,
                                     bias=eps_col[:, :]).then_inc(ln_ok, 1)
                act.wait_ge(ln_ok, N + 1)
                nc.scalar.activation(rs_head[:, :], rs_head[:, :], ACT.Exp, scale=-0.5).then_inc(rs_ok, 1)

            def exps(u):
                q, a, k0, kw = units[u]
                act.wait_ge(min_ok, 16 * jp + u + 1)
                if u >= 2:
                    act.wait_ge(turn_pe, gbase[jp] + turns[u - 2][-1][0] + 1)
                if g < 0:
                    lo, su = nmin[:, u % 4:u % 4 + 1], denom[:, u % 4:u % 4 + 1]
                    if u >= 4:
                        act.wait_ge(rden_ok, 16 * (jp - 6) + u - 3)
                else:
                    r = rec[jp % 2][:, q, a * UW:(a + 1) * UW]
                    su, lo = r[:, E:E + 1], r[:, E + 1:E + 2]
                nc.scalar.activation(prob[u % 2][:, 0:kw], logits[u % 2][:, 0:kw], ACT.Exp, bias=lo, scale=-1.0,
                                     accum_out=su).then_inc(exp_ok, 1)

            def copies(u):
                for n, blocks in turns[u]:
                    G = gbase[jp] + n
                    if G % 2 == 0:
                        act.wait_ge(turn_pe, G + 1)
                        if u >= 2:
                            act.wait_ge(pv_pe, 16 * jp + u - 1)
                        elif jp:
                            act.wait_ge(pv_pe, 16 * jp)
                        w = len(blocks)
                        nc.scalar.activation(probT[u % 2][:, blocks[0]:blocks[0] + w, :],
                                             bank[:, 5, 0:w * P].rearrange("p (b n) -> p b n", n=P),
                                             ACT.Copy).then_inc(pT_act, 1)

            def split(n):
                N = 4 * jp + n
                i, half = n % 2, n // 2
                act.wait_ge(norm_ok, N + 1)
                src, dst = normed[n % 2][:, :], placed(qkT_hi[i][:, :], g, half)
                if g > 0:
                    src = src.rearrange("p (n r) -> p n r", r=ORDER_STEP[g])
                if n == 0 and jp:
                    act.wait_ge(qk_pe, 16 * jp)
                nc.scalar.activation(dst, src, ACT.Copy).then_inc(qkT_hi_ok, 1)

            norm(0)
            root(0)
            norm(1)
            split(0)
            root(1)
            norm(2)
            split(1)
            root(2)
            split(2)
            norm(3)
            if jp == 6:
                merge_out(1)
            if early:
                exps(0)
                exps(1)
            root(3)
            split(3)
            if not early:
                exps(0)
                exps(1)
            for u in range(16):
                copies(u)
                if u in (2, 4, 6, 8) and j + 1 < len(jobs):
                    act_split(act, j + 1, [u // 2 - 1])
                if g < 0 and u == 11:
                    y_out(act, jp, 0)
                if u + 2 < 16:
                    exps(u + 2)
            if g < 0:
                y_out(act, jp, 1)

        def y_out(act, jp, half):
            act.wait_ge(yT_pe, 2 * (jp - 6) + half + 1)
            nc.scalar.activation(y_f[:, jp - 6, half * HALF:(half + 1) * HALF], bank[:, 7, :],
                                 ACT.Copy).then_inc(yT_ok, 1)

        def dve_pair(dve, jp, j):
            g = group_of_pair(jp)
            units, (turns, _) = units_of(g), groups(g)
            early = g <= 0

            def norm(n):
                i, half = n % 2, n // 2
                dve.wait_ge(rs_ok, 4 * jp + n + 1)
                gain = qgain if i == 0 else col[:, C_KG:C_KG + 10]
                p = jp - 6 if g < 0 else 4 + jp
                nc.vector.scalar_tensor_tensor(out=normed[n % 2][:, :], in0=bank[:, PROJ_BANK[n], :], scalar=gain[:, p:p + 1],
                                               in1=rs_head[:, :], op0=ALU.mult, op1=ALU.mult).then_inc(norm_ok, 1)

            def split(n):
                i, half = n % 2, n // 2
                src = normed[n % 2][:, :]
                hi, lo = (placed(t[i][:, :], g, half) for t in (qkT_hi, fox_lo if g < 0 else dil_lo))
                if g > 0:
                    src = src.rearrange("p (n r) -> p n r", r=ORDER_STEP[g])
                dve.wait_ge(qkT_hi_ok, 4 * jp + n + 1)
                nc.vector.tensor_tensor(lo, src, hi.bitcast(F32), ALU.subtract).then_inc(qkT_lo_ok, 1)

            def minimum(u):
                q, a, k0, kw = units[u]
                dve.wait_ge(qk_pe, 16 * jp + u + 1)
                if u >= 2:
                    dve.wait_ge(exp_ok, 16 * jp + u - 1)
                elif u == 0:
                    if jp:
                        dve.wait_ge(exp_ok, 16 * jp)
                    if g < 0:
                        dve.wait_ge(cum_ld, 16 * (jp - 5))
                    elif jp >= 2:
                        dve.wait_ge(rec_st[jp % 2], 128 * (jp // 2))
                if g < 0:
                    add, lo = cum_row[:, a, 0:kw], nmin[:, u % 4:u % 4 + 1]
                else:
                    h = 2 * (jp % 2) + a
                    add = bias2[:, h, :] if g == 2 else bias01[:, 4 * g + h, 256 - kw:256]
                    lo = rec[jp % 2][:, q, a * UW + E + 1:a * UW + E + 2]
                nc.vector.tensor_tensor_reduce(out=logits[u % 2][:, 0:kw], in0=s_at(u, kw), in1=add,
                                               scale=1.0, scalar=3e38, op0=ALU.add, op1=ALU.min,
                                               accum_out=lo).then_inc(min_ok, 1)

            def copies(u):
                for n, blocks in turns[u]:
                    G = gbase[jp] + n
                    if G % 2:
                        dve.wait_ge(turn_pe, G + 1)
                        if u >= 2:
                            dve.wait_ge(pv_pe, 16 * jp + u - 1)
                        elif jp:
                            dve.wait_ge(pv_pe, 16 * jp)
                        w = len(blocks)
                        nc.vector.tensor_copy(probT[u % 2][:, blocks[0]:blocks[0] + w, :],
                                              bank[:, 6, 0:w * P].rearrange("p (b n) -> p b n", n=P)).then_inc(pT_dve, 1)

            def result(u):
                q, a, _, _ = units[u]
                src = bank[:, (4, 7)[u % 2], 0:E]
                if g < 0:
                    if u == 0 and jp > 6:
                        dve.wait_ge(yT_pe, 2 * (jp - 6))
                    dve.wait_ge(exp_ok, 16 * jp + u + 1)
                    nc.vector.reciprocal(rden[:, u % 4:u % 4 + 1], denom[:, u % 4:u % 4 + 1]).then_inc(rden_ok, 1)
                    dve.wait_ge(pv_pe, 16 * jp + u + 1)
                    dve.wait_ge(rden_ok, 16 * (jp - 6) + u + 1)
                    nc.vector.tensor_scalar(y_pair[:, q, a * E:(a + 1) * E], src, rden[:, u % 4:u % 4 + 1], None,
                                            ALU.mult).then_inc(y_ok, 1)
                else:
                    dve.wait_ge(pv_pe, 16 * jp + u + 1)
                    nc.vector.tensor_copy(rec[jp % 2][:, q, a * UW:a * UW + E], src).then_inc(y_ok, 1)

            norm(0)
            split(0)
            norm(1)
            split(1)
            norm(2)
            split(2)
            if not early:
                norm(3)
                split(3)
            minimum(0)
            minimum(1)
            if early:
                norm(3)
                split(3)
            dve_ada_bg(dve, j)
            for u in range(16):
                copies(u)
                if u in (2, 4, 6, 8) and j + 1 < len(jobs):
                    dve_split(dve, j + 1, [u // 2 - 1])
                if u:
                    result(u - 1)
                if u + 2 < 16:
                    minimum(u + 2)
            result(15)
        def at_start(b):
            return type(b) is int and b == 0

        def g_load(sp, f):
            c = bass.ds(f * P, P)
            sources = [(0, g_raw[0][:, :, :], w_in_v[:, :, bass.ds(f * P + OFF_GA, P)]),
                       (1, g_raw[1][:, :, :], w_in_v[:, :, bass.ds(f * P + OFF_GB, P)]),
                       (2, g_raw[2][:, 0:4, :], w_a.rearrange("(k p) n -> p k n", p=P)[:, :, c]),
                       (2, g_raw[2][:, 4:6, :], w_b.rearrange("(k p) n -> p k n", p=P)[:, :, c])]
            for n, (i, raw, src) in enumerate(sources):
                if not at_start(f) and n < 2:
                    sp.wait_ge(g_lo_ok, 3 * (f - 1) + (1, 3)[n])
                sp.dma_start(raw, src).then_inc(g_ld[i], 16)

        def g_split_hi(f, i):
            A.wait_ge(g_ld[i], (32 if i == 2 else 16) * (f + 1))
            if not at_start(f):
                A.wait_ge(gate_pe, 8 * (f - 1) + (8 if i == 2 else 5 + i))
            else:
                A.wait_ge(proj_pe, 40)
            A.activation(g_hi[i][:, :, :], g_raw[i][:, :, :], ACT.Copy).then_inc(g_hi_ok, 1)

        def g_split_lo(f, i):
            V.wait_ge(g_hi_ok, 3 * f + i + 1)
            V.tensor_tensor(g_lo[i][:, :, :], g_raw[i][:, :, :], g_hi[i][:, :, :].bitcast(F32),
                            ALU.subtract).then_inc(g_lo_ok, 1)

        def act_gates(f):
            g_split_hi(f, 0)
            g_split_hi(f, 1)
            if at_start(f):
                A.wait_ge(pv_pe, 160)
                A.wait_ge(yT_ok, 8)
                A.wait_ge(mrg_ev, 2)
                for k in range(6):
                    A.activation(y_hi[:, k, :], y_f[:, k, :], ACT.Copy).then_inc(y_hi_ok, 1)
            g_split_hi(f, 2)
            for half in range(2):
                g = g_tmp[half]
                A.wait_ge(gate_pe, 8 * f + 4 * half + 2)
                if not at_start(f):
                    A.wait_ge(merged_ok, 2 * (f - 1) + half + 1)
                A.activation(g[:, :, :], bank[:, 4 * half:4 * half + 2, :], ACT.Exp, scale=-1.0).then_inc(gate_e, 1)
                A.wait_ge(gate_e, 6 * f + 3 * half + 1)
                A.activation(g[:, :, :], g[:, :, :], ACT.Ln, bias=ones[:, 0:1]).then_inc(gate_e, 1)
                A.wait_ge(gate_e, 6 * f + 3 * half + 2)
                A.activation(g[:, :, :], g[:, :, :], ACT.Exp, scale=-1.0).then_inc(gate_e, 1)

        def dve_gates(f):
            g_split_lo(f, 0)
            g_split_lo(f, 1)
            if at_start(f):
                for k in range(6):
                    V.wait_ge(y_hi_ok, k + 1)
                    V.tensor_tensor(y_lo[:, k, :], y_f[:, k, :], y_hi[:, k, :].bitcast(F32), ALU.subtract).then_inc(y_lo_ok, 1)
            g_split_lo(f, 2)
            for half in range(2):
                g = g_tmp[half]
                V.wait_ge(gate_e, 6 * f + 3 * half + 3)
                V.wait_ge(gate_pe, 8 * f + 4 * half + 4)
                V.tensor_tensor(g[:, :, :], g[:, :, :], bank[:, 4 * half + 2:4 * half + 4, :], ALU.mult).then_inc(gated_ok, 1)
                V.wait_ge(gated_ok, 2 * f + half + 1)
                V.tensor_tensor(merged[:, f, half * HALF:(half + 1) * HALF] if at_start(f) else
                                merged[:, bass.ds(f, 1), half * HALF:(half + 1) * HALF].rearrange("p f n -> p (f n)"),
                                g[:, 0, :], g[:, 1, :], ALU.add).then_inc(merged_ok, 1)

        def pe_gates(f):
            for half in range(2):
                t = slice(half * HALF, (half + 1) * HALF)
                if not at_start(f):
                    nc.tensor.wait_ge(merged_ok, 2 * (f - 1) + half + 1)
                for i in range(2):
                    nc.tensor.wait_ge(g_lo_ok, 3 * f + i + 1)
                    for k in range(KT):
                        mm = three(bank[:, 4 * half + i, :], (g_hi[i][:, k, :], g_lo[i][:, k, :]),
                                   (h_hi[:, k, t], h_lo[:, k, t]), k == 0, k == KT - 1)
                    mm.then_inc(gate_pe, 1)
                nc.tensor.wait_ge(g_lo_ok, 3 * f + 3)
                for i, ks in enumerate((range(0, 4), range(4, 6))):
                    for k in ks:
                        if at_start(f) and half == 0:
                            nc.tensor.wait_ge(y_lo_ok, k + 1)
                        mm = three(bank[:, 4 * half + 2 + i, :], (g_hi[2][:, k, :], g_lo[2][:, k, :]),
                                   (y_hi[:, k, t], y_lo[:, k, t]), k == ks[0], k == ks[-1])
                    mm.then_inc(gate_pe, 1)

        def loads_before(step, at):
            n = 2 * step + at // 6 + 1
            return n if at % 6 < 2 or at_start(step) else n - 1

        def chunk_hi(step, i, place=None, first=False):
            place = i if place is None else place
            A.wait_ge(e_ld[place % 6], 16 * loads_before(step, place))
            if not first:
                A.wait_ge(e_used, CHUNKS * (step - 1) + i + 1)
            A.activation(e_hi[i][:, :, :], e_raw[place % 6][:, :, :], ACT.Copy).then_inc(
                e_hi_ok, 5 if first and i == 7 else 1)

        def chunk_lo(step, i, place=None):
            place = i if place is None else place
            V.wait_ge(e_hi_ok, CHUNKS * step + place + 1)
            V.tensor_tensor(e_lo[i][:, :, :], e_raw[place % 6][:, :, :], e_hi[i][:, :, :].bitcast(F32),
                            ALU.subtract).then_inc(e_lo_ok, 1)

        def chunk_load(sp, step, place, src):
            if not at_start(step) or place >= 6:
                sp.wait_ge(e_lo_ok, CHUNKS * step + place - 5)
            sp.dma_start(e_raw[place % 6][:, :, :], src).then_inc(e_ld[place % 6], 16)

        def three(dst, lhs, rhs, first, last):
            for n, (a, b) in enumerate(((0, 0), (0, 1), (1, 0))):
                mm = nc.tensor.matmul(dst, lhs[a], rhs[b], start=first and n == 0, stop=last and n == 2)
            return mm

        def pe_up(e, which, first=False):
            if which == 0:
                nc.tensor.wait_ge(xT_lo_ok, e + 1)
            if not first:
                nc.tensor.wait_ge(act_ok, e)
            for i in range(4):
                c = 4 * which + i
                nc.tensor.wait_ge(e_lo_ok, CHUNKS * e + c + 1)
                for kk in range(2):
                    k = 2 * i + kk
                    mm = three(bank[:, which, :], (xT_hi[:, k, :], xT_lo[:, k, :]),
                               (e_hi[c][:, kk, :], e_lo[c][:, kk, :]), k == 0, k == KT - 1)
                mm.then_inc(e_used, 5 if first and c == 7 else 1)

        def pe_turn_act(b):
            nc.tensor.wait_ge(act_ok, b + 1)
            if not at_start(b):
                nc.tensor.wait_ge(aT_lo_ok, b)
            for k in range(4):
                mm = nc.tensor.transpose(bank[:, 4, k * P:(k + 1) * P], act_in[:, k * P:(k + 1) * P], ident)
            mm.then_inc(actT_pe, 1)

        def pe_turn_x(b):
            nc.tensor.wait_ge(xg_ld, 16 * (b + 1))
            if not at_start(b):
                nc.tensor.wait_ge(xT_lo_ok, b)
            for k in range(KT):
                mm = nc.tensor.transpose(bank[:, 5 + k // 4, k % 4 * P:(k % 4 + 1) * P], xg[:, k * P:(k + 1) * P], ident)
            mm.then_inc(xgT_pe, 1)

        def pe_down(b, place=8):
            nc.tensor.wait_ge(aT_lo_ok, b + 1)
            if not at_start(b):
                nc.tensor.wait_ge(ye_act, b)
                nc.tensor.wait_ge(ye_dve, b)
            for i in range(4):
                c = 8 + i
                nc.tensor.wait_ge(e_lo_ok, CHUNKS * (b + 1) + place + i + 1)
                for kk in range(2):
                    k = 2 * (i % 2) + kk
                    mm = three(bank[:, 2 + i // 2, :], (aT_hi[:, k, :], aT_lo[:, k, :]),
                               (e_hi[c][:, kk, :], e_lo[c][:, kk, :]), k == 0, k == 3)
                mm.then_inc(e_used, 1)

        turned_x = bank[:, 5:7, :].rearrange("p b (k n) -> p (b k) n", n=P)
        turned_act = bank[:, 4, :].rearrange("p (k n) -> p k n", n=P)

        def act_xT(b, first=False):
            A.wait_ge(xgT_pe, b + 1)
            if not first:
                A.wait_ge(e_used, CHUNKS * (b - 1) + 8)
            A.activation(xT_hi[:, :, :], turned_x, ACT.Copy).then_inc(xT_hi_ok, 1)

        def dve_xT(b):
            V.wait_ge(xT_hi_ok, b + 1)
            V.tensor_tensor(xT_lo[:, :, :], turned_x, xT_hi[:, :, :].bitcast(F32), ALU.subtract).then_inc(xT_lo_ok, 1)

        def act_sig(e, first=False):
            A.wait_ge(e_used, CHUNKS * e + 4)
            if not first:
                A.wait_ge(act_ok, e)
            A.activation(gate_act[:, :], bank[:, 0, :], ACT.Exp, scale=-1.0).then_inc(sig_e, 1)
            A.wait_ge(sig_e, 3 * e + 1)
            A.activation(gate_act[:, :], gate_act[:, :], ACT.Ln, bias=ones[:, 0:1]).then_inc(sig_e, 1)
            A.wait_ge(sig_e, 3 * e + 2)
            A.activation(gate_act[:, :], gate_act[:, :], ACT.Exp, scale=-1.0).then_inc(sig_e, 1)

        def dve_silu(e):
            V.wait_ge(sig_e, 3 * e + 3)
            V.tensor_tensor(gate_act[:, :], gate_act[:, :], bank[:, 0, :], ALU.mult).then_inc(silu_v, 1)

        def dve_act(e, first=False):
            V.wait_ge(silu_v, e + 1)
            V.wait_ge(e_used, CHUNKS * e + 8)
            if not first:
                V.wait_ge(actT_pe, e)
            V.tensor_tensor(act_in[:, :], gate_act[:, :], bank[:, 1, :], ALU.mult).then_inc(act_ok, 1)

        def act_aT(b):
            A.wait_ge(actT_pe, b + 1)
            if not at_start(b):
                A.wait_ge(e_used, CHUNKS * (b + 1))
            A.activation(aT_hi[:, :, :], turned_act, ACT.Copy).then_inc(aT_hi_ok, 1)

        def dve_aT(b):
            V.wait_ge(aT_hi_ok, b + 1)
            V.tensor_tensor(aT_lo[:, :, :], turned_act, aT_hi[:, :, :].bitcast(F32), ALU.subtract).then_inc(aT_lo_ok, 1)

        def act_y(b, place=8):
            if not at_start(b):
                A.wait_ge(ye_st, 16 * b)
            A.wait_ge(e_used, CHUNKS * (b + 1) + place + 2)
            A.activation(y_e[:, 0:HALF], bank[:, 2, :], ACT.Copy).then_inc(ye_act, 1)

        def dve_y(b, place=8):
            if not at_start(b):
                V.wait_ge(ye_st, 16 * b)
            V.wait_ge(e_used, CHUNKS * (b + 1) + place + 4)
            V.tensor_copy(y_e[:, HALF:D], bank[:, 3, :]).then_inc(ye_dve, 1)

        def store_y(b, signal=None):
            row = b * SLOTS
            A.wait_ge(ye_act, b + 1)
            A.wait_ge(ye_dve, b + 1)
            A.dma_start(d_y[bass.ds(row, SLOTS), :], y_e[:, :]).then_inc(signal or ye_st, 16)

        def act_step(e, last=False):
            first = at_start(e)
            if not last:
                chunk_hi(e + 1, 0)
                chunk_hi(e + 1, 1)
            if not first:
                act_aT(e - 1)
            if not last:
                chunk_hi(e + 1, 2)
                chunk_hi(e + 1, 3)
            act_sig(e, first)
            if not last:
                chunk_hi(e + 1, 4)
                chunk_hi(e + 1, 5)
                chunk_hi(e + 1, 6)
                chunk_hi(e + 1, 7)
                act_xT(e + 1)
            for i in range(4):
                chunk_hi(e + 1, 8 + i, i if last else None, first)
                if not first and i == 1:
                    act_y(e - 1)
            if not first:
                store_y(e - 1)

        def dve_step(e, last=False):
            first = at_start(e)
            if not last:
                chunk_lo(e + 1, 0)
                chunk_lo(e + 1, 1)
            if not first:
                dve_aT(e - 1)
            if not last:
                chunk_lo(e + 1, 2)
                chunk_lo(e + 1, 3)
            dve_silu(e)
            if not last:
                chunk_lo(e + 1, 4)
                chunk_lo(e + 1, 5)
            dve_act(e, first)
            if not last:
                chunk_lo(e + 1, 6)
                chunk_lo(e + 1, 7)
                dve_xT(e + 1)
            for i in range(4):
                chunk_lo(e + 1, 8 + i, i if last else None)
            if not first:
                dve_y(e - 1)

        def pe_step(e, last=False):
            first = at_start(e)
            pe_up(e, 0, first)
            if not first:
                pe_turn_act(e - 1)
            if not last:
                pe_turn_x(e + 1)
            pe_up(e, 1, first)
            if not first:
                pe_down(e - 1)

        w1_v = w1.rearrange("e (k p) n -> (e k) p n", p=P)
        w3_v = w3.rearrange("e (k p) n -> (e k) p n", p=P)
        w2_v = w2.rearrange("e (k p) n -> (e k) p n", p=P)

        def sp_up(sp, step, expert):
            for i in range(8):
                src = (w1_v, w3_v)[i // 4][bass.ds(expert * 8 + 2 * (i % 4), 2), :, :]
                chunk_load(sp, step, i, src.rearrange("k p n -> p k n"))

        def sp_down(sp, step, expert, place=8):
            for i in range(4):
                c = slice(i // 2 * HID, (i // 2 + 1) * HID)
                src = w2_v[bass.ds(expert * 4 + 2 * (i % 2), 2), :, c]
                chunk_load(sp, step, place + i, src.rearrange("k p n -> p k n"))

        def pool_index(pool, b, first=False):
            if not first:
                pool.wait_ge(xgT_pe, b)
            pool.tensor_copy(idx_now[:, :], slot_tok[:, bass.ds(b, 1)]).then_inc(idx_ok, 1)
            pool.wait_ge(idx_ok, b + 1)

        def pool_gather(pool):
            pool.indirect_dma_start(xg[:, :], None, d_h2, bass.IndirectOffsetOnAxis(ap=idx_now[:, :], axis=0)).then_inc(xg_ld, 16)

        def bc(ap, axis, shape):
            return ap.unsqueeze(axis).to_broadcast([P] + shape)

        def pick(dst, scores, top, priority, groups):
            link_v(V.tensor_reduce(top[:, :], scores, AX.X, ALU.max))
            link_v(V.tensor_tensor(dst[:, :, :], scores, bc(top[:, :], 2, [NT, groups]), ALU.is_equal))
            link_v(V.tensor_tensor(dst[:, :, :], dst[:, :, :], bc(priority, 1, [NT, groups]), ALU.mult))
            link_v(V.tensor_reduce(e_first[:, :], dst[:, :, :], AX.X, ALU.max))
            link_v(V.tensor_tensor(dst[:, :, :], dst[:, :, :], bc(e_first[:, :], 2, [NT, groups]), ALU.is_equal))

        def dve_route():
            row = lambda at, n: consts[:, K_ROW + at:K_ROW + at + n]
            G, EG = N_GROUPS, PER_GROUP
            V.wait_ge(rt_pe, 1)
            V.wait_ge(h2_st[2], 16 * (NT - 2))
            link_v(V.tensor_tensor(lg[:, :, :], bank[:, 4, 0:NT * N_ROUTE].rearrange("p (t n) -> p t n", t=NT),
                                   bc(brr[:, :], 1, [NT, N_ROUTE]), ALU.add))
            gl = lg[:, :, 0:G]
            el = lg[:, :, G:].rearrange("p t (g e) -> p t g e", g=G)
            pick(g_hot, gl, g_max, row(R_PRI4, G), G)
            V.tensor_tensor(g_ex[:, :, :], gl, bc(g_max[:, :], 2, [NT, G]), ALU.subtract).then_inc(r_d, 1)
            pr = r_prod[:, :, :].rearrange("p t (g e) -> p t g e", g=G)
            link_v(V.tensor_tensor(pr, el, bc(g_hot[:, :, :], 3, [NT, G, EG]), ALU.mult))
            link_v(V.tensor_reduce(e_in[:, :, :], r_prod[:, :, :].rearrange("p t (g e) -> p t e g", g=G), AX.X, ALU.add))
            pick(hot1, e_in[:, :, :], m_one, row(R_PRI8, EG), EG)
            link_v(V.tensor_scalar(e_next[:, :, :], hot1[:, :, :], -3e38, None, ALU.mult))
            link_v(V.tensor_tensor(e_next[:, :, :], e_next[:, :, :], e_in[:, :, :], ALU.add))
            pick(hot2, e_next[:, :, :], m_two, row(R_PRI8, EG), EG)
            V.tensor_tensor(m_ex[:, :], m_two[:, :], m_one[:, :], ALU.subtract).then_inc(r_d, 1)
            link_v(V.tensor_tensor(e_eq[:, :, :], hot1[:, :, :], hot2[:, :, :], ALU.add))
            for g in range(G):
                last = V.tensor_tensor(r_mask[:, :, g * EG:(g + 1) * EG], e_eq[:, :, :],
                                       bc(g_hot[:, :, g], 2, [NT, EG]), ALU.mult)
            last.then_inc(r_d, 1)
            V.wait_ge(r_a, 2)
            link_v(V.tensor_reduce(g_sum[:, :], g_ex[:, :, :], AX.X, ALU.add))
            link_v(V.tensor_scalar(m_r[:, :], m_ex[:, :], 1.0, None, ALU.add))
            link_v(V.tensor_tensor(m_r[:, :], m_r[:, :], g_sum[:, :], ALU.mult))
            link_v(V.reciprocal(wts[:, 0:NT], m_r[:, :]))
            link_v(V.tensor_tensor(wts[:, NT:], wts[:, 0:NT], m_ex[:, :], ALU.mult))
            V.memset(before[:, 0, :], 0.0).then_inc(r_d, 1)
            V.wait_ge(r_d, 4)
            V.wait_ge(rank_pe, 1)
            tot = bank[:, 6, 0:NT * N_EXP].rearrange("p (t e) -> p t e", t=NT)
            for t in range(1, NT):
                link_v(V.tensor_tensor(before[:, t, :], before[:, t - 1, :], tot[:, t - 1, :], ALU.add))
            link_v(V.tensor_tensor(rank[:, :, :], bank[:, 5, 0:NT * N_EXP].rearrange("p (t e) -> p t e", t=NT),
                                   before[:, :, :], ALU.add))
            link_v(V.tensor_tensor(over[0][:, :], before[:, NT - 1, :], tot[:, NT - 1, :], ALU.add))
            link_v(V.tensor_scalar(over[0][:, :], over[0][:, :], 1.0, -1.0, ALU.max, ALU.add))
            link_v(V.tensor_copy(c_int[:, :], over[0][:, :]))
            link_v(V.tensor_scalar(c_int[:, :], c_int[:, :], 7, None, ALU.arith_shift_right))
            link_v(V.tensor_copy(over[0][:, :], c_int[:, :]))
            link_v(V.tensor_copy(over[1][:, :], over[0][:, :]))
            src, dst = 1, 2
            for s in (1, 2, 4, 8, 16):
                V.tensor_copy(over[dst][:, 0:s], over[src][:, 0:s])
                link_v(V.tensor_tensor(over[dst][:, s:], over[src][:, s:], over[src][:, 0:N_EXP - s], ALU.add))
                src, dst = dst, src
            upto, spare = over[src], over[dst]
            link_v(V.tensor_tensor(exp_cmp[:, :, :], upto[0:1, :].unsqueeze(1).to_broadcast([1, N_OVER, N_EXP]),
                                   row(R_IOTA, N_OVER)[0:1, :].unsqueeze(2).to_broadcast([1, N_OVER, N_EXP]), ALU.is_le))
            link_v(V.tensor_reduce(exp_of[:, :], exp_cmp[:, :, :], AX.X, ALU.add))
            link_v(V.tensor_scalar(exp_of[:, :], exp_of[:, :], N_EXP - 1.0, None, ALU.min))
            V.tensor_copy(blk_exp[0:1, 0:N_EXP], row(R_IOTA, N_EXP)[0:1, :])
            V.tensor_copy(blk_exp[0:1, N_EXP:MAX_BLK], exp_of[:, :])
            link_v(V.tensor_scalar(blk_exp[0:1, MAX_BLK:MAX_BLK + 1], upto[0:1, N_EXP - 1:N_EXP], N_EXP - 3.0, None, ALU.add))
            link_v(V.tensor_tensor(spare[:, :], upto[:, :], over[0][:, :], ALU.subtract))
            link_v(V.scalar_tensor_tensor(out=spare[:, :], in0=spare[:, :], scalar=N_EXP - 1.0, in1=row(R_IOTA, N_EXP),
                                          op0=ALU.add, op1=ALU.subtract))
            link_v(V.tensor_copy(r_int[:, :, :], rank[:, :, :]))
            link_v(V.tensor_scalar(r_int[:, :, :], r_int[:, :, :], 7, None, ALU.arith_shift_right))
            link_v(V.tensor_copy(r_prod[:, :, :], r_int[:, :, :]))
            link_v(V.scalar_tensor_tensor(out=rank[:, :, :], in0=r_prod[:, :, :], scalar=-float(SLOTS), in1=rank[:, :, :],
                                          op0=ALU.mult, op1=ALU.add))
            link_v(V.tensor_tensor(r_blk[:, :, :], r_prod[:, :, :], bc(spare[:, :], 1, [NT, N_EXP]), ALU.add))
            link_v(V.scalar_tensor_tensor(out=r_blk[:, :, :], in0=r_prod[:, :, :], scalar=0.0, in1=r_blk[:, :, :],
                                          op0=ALU.is_gt, op1=ALU.mult))
            link_v(V.tensor_tensor(r_blk[:, :, :], r_blk[:, :, :], bc(row(R_IOTA, N_EXP), 1, [NT, N_EXP]), ALU.add))
            for k, hot in enumerate((hot1, hot2)):
                for g in range(G):
                    last = V.tensor_tensor(r_mask[:, :, g * EG:(g + 1) * EG], hot[:, :, :],
                                           bc(g_hot[:, :, g], 2, [NT, EG]), ALU.mult)
                link_v(last)
                for value, to in ((rank, place_f), (r_blk, blk_f)):
                    link_v(V.tensor_tensor(r_prod[:, :, :], r_mask[:, :, :], value[:, :, :], ALU.mult))
                    link_v(V.tensor_reduce(to[:, k * NT:(k + 1) * NT], r_prod[:, :, :], AX.X, ALU.add))
            V.wait_ge(h2_st[0], 16)
            V.wait_ge(h2_st[1], 16)
            n = 2 * NT
            V.tensor_tensor(hot_place[:, :, :], bc(place_f[:, :], 2, [n, SLOTS]), bc(row(R_IOTA, SLOTS), 1, [n, SLOTS]),
                            ALU.is_equal)
            flat_blk = hot_blk[:, :, :, :].rearrange("p k t b -> p (k t) b")
            link_v(V.tensor_tensor(flat_blk, bc(blk_f[:, :], 2, [n, MAX_BLK]), bc(row(R_IOTA, MAX_BLK), 1, [n, MAX_BLK]),
                                   ALU.is_equal))
            for k in range(2):
                last = V.tensor_tensor(hot_blk[:, k, :, :], hot_blk[:, k, :, :], bc(row(R_TOK, NT), 2, [NT, MAX_BLK]), ALU.mult)
            last.then_inc(hot_ok, 1)
            link_v(V.scalar_tensor_tensor(out=dest_f[:, :], in0=blk_f[:, :], scalar=float(SLOTS), in1=place_f[:, :],
                                          op0=ALU.mult, op1=ALU.add))
            V.tensor_copy(dest[:, :], dest_f[:, :])
            V.wait_ge(slot_pe, 1)
            V.tensor_copy(slot_tok[:, :], bank[:, 7, 0:MAX_BLK]).then_inc(dest_ok, 1)

        def dve_norm2(dve, t):
            dve.wait_ge(rs2_ok, t + 1)
            if t == 0:
                dve.wait_ge(mod2_ld, 32)
            if t >= XN:
                dve.wait_ge(h2_st[t - XN], 16)
                dve.wait_ge(h2_pe, KT)
            tile = xn2[t % XN]
            link_v(V.scalar_tensor_tensor(out=tile[:, :], in0=x2[:, t, :], scalar=rstd[:, t:t + 1],
                                          in1=mod2_row[0][:, :], op0=ALU.mult, op1=ALU.mult))
            V.tensor_tensor(tile[:, :], tile[:, :], mod2_row[1][:, :], ALU.add).then_inc(xn2_ok, 1)

        def h2_evac_act(n):
            half, f = n // KT, n % KT
            A.wait_ge(h2_pe, n + 1)
            A.activation(h2T[:, f, half * HALF:(half + 1) * HALF], bank[:, n % 4, :],
                         ACT.Copy).then_inc(h2_act, 1)

        @block.sync
        def _(sp):
            sp.dma_start(consts[:, :], cst).then_inc(rows_ld, 16)
            for r0, src in small_rows[3:6]:
                sp.dma_start(rows[r0:r0 + src.shape[0], :], src).then_inc(rows_ld, 16)
            w_ada_v = w_ada.rearrange("(k p) n -> p k n", p=P)
            for n in range(4):
                sp.dma_start(ada_w[n][:, :, :], w_ada_v[:, :, n * 256:(n + 1) * 256]).then_inc(ada_ld[n], 16)
            for t in range(0, NT, 2):
                sp.dma_start(xt[:, t:t + 2, :], x[t * P:(t + 2) * P, :].rearrange("(t p) n -> p t n", p=P)).then_inc(tile_ld[t // 2], 16)
            for n in range(4, ADA_FIRST):
                sp.wait_ge(ada_pe, n - 3)
                sp.dma_start(ada_w[n % 4][:, :, :], w_ada_v[:, :, n * 256:(n + 1) * 256]).then_inc(ada_ld[n % 4], 16)
            sp.wait_ge(ada_pe, ADA_FIRST)
            for j in range(len(jobs) + 1):
                if j < len(jobs):
                    for i, (raw, src) in enumerate(raw_parts(j)):
                        if j:
                            sp.wait_ge(w_lo_ok, 4 * j)
                        sp.dma_start(raw, src).then_inc(w_ld[i], 16)
                if 1 <= j <= J_FOX and jobs[j - 1][0] == "qk":
                    jp = (j - 1) // 3 * 2 + (j - 1) % 3 - 1
                    g, h0 = jp // 2, 2 * (jp % 2)
                    sp.wait_ge(y_ok, 16 * (jp + 1))
                    sp.wait_ge(exp_ok, 16 * (jp + 1))
                    dst = d_rec[g, :, h0 * UW:(h0 + 2) * UW]
                    for q in range(NT):
                        o = (q * P, q // 2 + 512 * (q % 2), q)[g]
                        n = ORDER_STEP[g]
                        sp.dma_start(dst[o:min(o + n * P, T):n, :], rec[jp % 2][:, q, :]).then_inc(rec_st[jp % 2], 16)
                if j == J_FOX + 1:
                    sp.wait_ge(rec_st[0], 128 * NG)
                    sp.wait_ge(rec_st[1], 128 * NG)
                    for half in range(2):
                        if half:
                            sp.wait_ge(mrg_y, 1)
                        for g in range(NG):
                            src = d_rec[g, half * HALF:(half + 1) * HALF, :].rearrange("(t p) w -> p t w", p=P)
                            sp.dma_start(mrec[:, :, g, :, :].rearrange("p t h w -> p t (h w)"), src).then_inc(mrec_ld, 16)
                if j == J_FOX + 2:
                    sp.wait_ge(cumT_ev, 1)
                    sp.dma_start(d_cum, cumT[:, :]).then_inc(cum_st, 16)
                    sp.wait_ge(cum_st, 16)
                if j >= J_FOX + 2 and j < len(jobs):
                    p = j - J_FOX - 2
                    sp.wait_ge(min_ok, 16 * (6 + p))
                    sp.dma_start(cum_row[:, :, :].rearrange("p h t -> p (h t)"),
                                 d_cum[16 * p:16 * p + 16, :].rearrange("a b -> (a b)").partition_broadcast(P)).then_inc(cum_ld, 16)
            sp.wait_ge(proj_pe, 40)
            g_load(sp, 0)
            rows_stored(sp)
            sp.wait_ge(min_ok, 160)
            for i, r in enumerate((16, 40)):
                sp.dma_start(gate_row[i][:, :], d_mod[r:r + 8, :].rearrange("a b -> (a b)").partition_broadcast(P)).then_inc(gate_ld, 16)
            with sp.Fori(0, KT - 1) as i:
                g_load(sp, i + 1)
            sp.wait_ge(gate_pe, 64)
            for cc in range(3):
                sp.dma_start(o_raw[cc][:, :, :], w_out.rearrange("(k p) n -> p k n", p=P)[:, :, cc * OC:(cc + 1) * OC]).then_inc(o_ld[cc], 16)
            sp.wait_ge(merged_ok, 16)
            sp.dma_start(x2[:, :, :], x.rearrange("(t p) n -> p t n", p=P)).then_inc(x2_ld, 16)
            sp.wait_ge(o_lo_ok, 2)
            sp.dma_start(o_raw[0][:, :, :], w_out.rearrange("(k p) n -> p k n", p=P)[:, :, 3 * OC:4 * OC]).then_inc(o_ld[0], 16)
            sp.wait_ge(o_lo_ok, 4)
            sp.dma_start(w_rt[:, :, 0:N_GROUPS], w_rg.rearrange("(k p) n -> p k n", p=P)).then_inc(rt_ld, 16)
            sp.dma_start(w_rt[:, :, N_GROUPS:], w_re.rearrange("(k p) n -> p k n", p=P)).then_inc(rt_ld, 16)
            sp.wait_ge(o_pe, 24)
            for i, r in enumerate((32, 24)):
                sp.dma_start(mod2_row[i][:, :], d_mod[r:r + 8, :].rearrange("a b -> (a b)").partition_broadcast(P)).then_inc(mod2_ld, 16)
            for t in range(NT):
                sp.wait_ge(xn2_ok, t + 1)
                sp.dma_start(d_h2[t * P:(t + 1) * P, :], xn2[t % XN][:, :]).then_inc(h2_st[min(t, 2)], 16)
            sp.wait_ge(h2_pe, 2 * KT)
            sp.wait_ge(h2_st[2], 16 * (NT - 2))
            sp_up(sp, 0, 0)
            sp_up(sp, 1, 1)
            sp_down(sp, 1, 0)
            sp.wait_ge(dest_ok, 1)
            more = sp.value_load(blk_exp[0:1, MAX_BLK:MAX_BLK + 1], min_val=N_EXP - 3, max_val=MAX_BLK - 4)
            with sp.Fori(0, more + 1) as i:
                up = sp.value_load(blk_exp[0:1, bass.ds(i + 2, 1)], min_val=0, max_val=N_EXP - 1)
                down = sp.value_load(blk_exp[0:1, bass.ds(i + 1, 1)], min_val=0, max_val=N_EXP - 1)
                sp_up(sp, i + 2, up)
                sp_down(sp, i + 2, down)
            final = sp.value_load(blk_exp[0:1, bass.ds(more + 2, 1)], min_val=0, max_val=N_EXP - 1)
            sp_down(sp, more + 3, final, 0)
            for t in range(NT):
                sp.wait_ge(f_pool, t + 1)
                sp.dma_start(out[t * P:(t + 1) * P, :], x2[:, t, :]).then_inc(out_st, 16)
            sp.wait_ge(out_st, 16 * NT)

        @block.gpsimd
        def _(pool):
            pool.memset(ones[:, :], 1.0).then_inc(pool_set, 1)
            pool.memset(eps_col[:, :], EPS).then_inc(pool_set, 1)
            pool.wait_ge(rel_ev, 1)
            for g in range(NG):
                pool.dma_start(d_rel[4 * g:4 * g + 4, :, :], relrow[:, g, :].unsqueeze(1).to_broadcast([4, P, 384])).then_inc(rel_st, 16)
            pool.wait_ge(rel_st, 48)
            row = P * 384
            for h in range(DIL_HEADS):
                if h < 8:
                    src = bass.AP(d_rel.tensor, offset=h * row + 127, ap=[[383, P], [1, 256]])
                    pool.dma_start(bias01[:, h, :], src).then_inc(bias_ld, 16)
                else:
                    src = bass.AP(d_rel.tensor, offset=h * row + 255, ap=[[383, P], [1, P]])
                    pool.dma_start(bias2[:, h - 8, :], src).then_inc(bias_ld, 16)
            for i in range(N_OVER * SLOTS // T):
                row = N_EXP * SLOTS + i * T
                pool.dma_start(d_y[row:row + T, :], x).then_inc(fill_st, 16)
            flat = d_mod.rearrange("a b -> (a b)")
            pool.wait_ge(h_lo_ok, 2 * KT)
            for i in range(2):
                pool.memset(bg_b[i][:, :], 0.0).then_inc(bg_zero, 1)
            pool.wait_ge(bg_zero, 2)
            pool.dma_start(bg_gain[:, :], n2.rearrange("(a b) -> a b", a=1)).then_inc(gain_ld, 16)
            for n in range(ADA_FIRST, ADA_CHUNKS + 3):
                c = slice(n * 256, (n + 1) * 256)
                if n < ADA_CHUNKS:
                    if n - ADA_FIRST >= 2:
                        pool.wait_ge(bg_sum_ok, BG_STEPS * (n - ADA_FIRST - 1))
                    pool.dma_start(bg_w[n % 2][:, :, :], w_ada.rearrange("(k p) n -> p k n", p=P)[:, :, c]).then_inc(bg_ld[n % 2], 16)
                    pool.dma_start(bg_b[n % 2][0:1, :], b_ada[c].rearrange("(a b) -> a b", a=1)).then_inc(bg_ld[n % 2], 16)
                if ADA_FIRST < n <= ADA_CHUNKS:
                    pool_ada_bg(pool, n - 1)
                if n - ADA_FIRST >= 3:
                    m = n - 3
                    pool.wait_ge(bg_row_ok, m - ADA_FIRST + 1)
                    pool.dma_start(flat[m * 256:(m + 1) * 256].rearrange("(a b) -> a b", a=1), bg_row[m % 2][:, :]).then_inc(mod_st[m % 2], 16)
            for i in range(8):
                pool.wait_ge(e_hi_ok, i + 1)
                pool.tensor_tensor(e_lo[i][:, :, :], e_raw[i % 6][:, :, :], e_hi[i][:, :, :].bitcast(F32),
                                   ALU.subtract).then_inc(e_lo_ok, 5 if i == 7 else 1)
            pool.wait_ge(fill_st, 16 * (N_OVER * SLOTS // T))
            pool.wait_ge(dest_ok, 1)
            for i in range(3):
                pool.wait_ge(h2_st[i], 16 * (1 if i < 2 else NT - 2))
            pool_index(pool, 0, first=True)
            pool_gather(pool)
            pool_index(pool, 1)
            pool_gather(pool)
            pool_index(pool, 2)
            more = pool.value_load(blk_exp[0:1, MAX_BLK:MAX_BLK + 1], min_val=N_EXP - 3, max_val=MAX_BLK - 4)
            with pool.Fori(0, more + 1) as i:
                pool_gather(pool)
                pool_index(pool, i + 3)
            pool.wait_ge(ye_end, 16)
            for t in range(NT):
                for k in range(2):
                    pool.indirect_dma_start(y_slot[2 * t + k][:, :], None, d_y,
                                            bass.IndirectOffsetOnAxis(ap=dest[:, k * NT + t:k * NT + t + 1], axis=0)).then_inc(slot_y[t // 2], 16)
            for t in range(NT):
                pool.wait_ge(f_dve, 2 * t + 2)
                pool.tensor_tensor(x2[:, t, :], x2[:, t, :], y_sum[t % 4][:, :], ALU.add).then_inc(f_pool, 1)

        @block.scalar
        def _(act):
            act.add_instruction(mybir.InstLoadActFuncSet(name=nc.get_next_instruction_name(),
                                                         act_func_set_id=EXP_AND_LN, engine=act.engine))
            for r0, src in small_rows[0:3]:
                A.dma_start(rows[r0:r0 + src.shape[0], :], src).then_inc(rows_ld, 16)
            A.dma_start(ohs[0:33, :], oh).then_inc(small_ld, 16)
            A.dma_start(tab[0:32, :], rel).then_inc(small_ld, 16)
            A.dma_start(bfr[:, :], b_f.partition_broadcast(P)).then_inc(small_ld, 16)
            A.dma_start(brr[:, 0:N_GROUPS], b_rg.partition_broadcast(P)).then_inc(small_ld, 16)
            A.dma_start(brr[:, N_GROUPS:], b_re.partition_broadcast(P)).then_inc(small_ld, 16)
            act.wait_ge(rowsT_pe, 1)
            A.activation(col[:, :], bank[:, 0, 0:N_ROWS], ACT.Copy).then_inc(col_ok, 1)
            act.wait_ge(col_ok, 1)
            A.activation(silu_t[:, :], col[:, C_C:C_C + KT], ACT.Exp, scale=-1.0).then_inc(silu_e, 1)
            act.wait_ge(pool_set, 2)
            for t in range(NT):
                act.wait_ge(tile_ld[t // 2], 16)
                link_a(A.activation(junk[:, :], xt[:, t, :], ACT.Square, accum_out=ssq[:, t:t + 1]))
            link_a(A.activation(rstd[:, :], ssq[:, :], ACT.Ln, scale=1.0 / D, bias=eps_col[:, :]))
            A.activation(rstd[:, :], rstd[:, :], ACT.Exp, scale=-0.5).then_inc(rstd_ok, 1)
            for n in range(ADA_FIRST):
                act.wait_ge(ada_pe, n + 1)
                A.activation(ada_row[:, n * 256:(n + 1) * 256], bank[0:1, 4 + n % 4, 0:256], ACT.Copy).then_inc(ada_ev, 1)
            act.wait_ge(scl_ok, 1)
            for n in range(2 * KT):
                f, half = n // 2, n % 2
                if n == 10:
                    act_split(act, 0)
                act.wait_ge(xT_pe, n + 1)
                if n >= 2:
                    act.wait_ge(h_lo_ok, n - 1)
                A.activation(h_tmp[n % 2][:, :], bank[:, n % 4, :], ACT.Identity, scale=scale1[:, f:f + 1],
                             bias=mod[:, f:f + 1]).then_inc(xT_act, 1)
            vj = 0
            for j, (kind, _, _) in enumerate(jobs):
                if kind == "v":
                    ev_values(act, act_copy, j, vj, 0, v_ev_act)
                    vj += 1
                    act_split(act, j + 1)
                    if j == J_FOX:
                        merge_act(0)
                    if j == J_FOX + 1:
                        merge_out(0)
                        act.wait_ge(fg_ok, 1)
                        link_a(A.activation(fg[3][:, :, :], fg[2][:, :, :], ACT.Exp, scale=-1.0))
                        A.activation(fg[4][:, :, :], fg[3][:, :, :], ACT.Ln, bias=ones[:, 0:1]).then_inc(fg_act, 1)
                        act.wait_ge(cumT_pe, 1)
                        A.activation(cumT[:, :], bank[0:64, 4, P:2 * P], ACT.Copy).then_inc(cumT_ev, 1)
                        merge_act(1)
                else:
                    jp = (j // 3 * 2 + j % 3 - 1) if j < J_FOX else j - J_FOX - 2 + 6
                    act_pair(act, jp, j)
            act_gates(0)
            with act.Fori(0, KT - 1) as i:
                act_gates(i + 1)
            act.wait_ge(gate_pe, 64)
            act.wait_ge(merged_ok, 16)
            for k in range(KT):
                if k in (3, 5):
                    act.wait_ge(o_ld[0], 16)
                    ks = slice(0, 4) if k == 3 else slice(4, KT)
                    A.activation(o_hi[0][:, ks, :], o_raw[0][:, ks, :], ACT.Copy).then_inc(o_hi_ok, 1)
                A.activation(m_hi[:, k, :], merged[:, k, :], ACT.Copy).then_inc(m_hi_ok, 1)
            for cc in range(1, 4):
                act.wait_ge(o_ld[cc % 3], 32 if cc == 3 else 16)
                if cc >= 2:
                    act.wait_ge(o_pe, 8 * (cc - 1))
                A.activation(o_hi[cc % 2][:, :, :], o_raw[cc % 3][:, :, :], ACT.Copy).then_inc(o_hi_ok, 1)
            for t in range(NT):
                act.wait_ge(o_done, 24 + t + 1)
                link_a(A.activation(o_junk[:, :], x2[:, t, :], ACT.Square, accum_out=ssq[:, t:t + 1]))
                link_a(A.activation(rstd[:, t:t + 1], ssq[:, t:t + 1], ACT.Ln, scale=1.0 / D, bias=eps_col[:, :]))
                A.activation(rstd[:, t:t + 1], rstd[:, t:t + 1], ACT.Exp, scale=-0.5).then_inc(rs2_ok, 1)
            for n in range(2 * KT):
                h2_evac_act(n)
            act.wait_ge(r_d, 1)
            A.activation(g_ex[:, :, :], g_ex[:, :, :], ACT.Exp).then_inc(r_a, 1)
            act.wait_ge(r_d, 2)
            A.activation(m_ex[:, :], m_ex[:, :], ACT.Exp).then_inc(r_a, 1)
            act.wait_ge(o_pe, 32)
            for i in range(8):
                chunk_hi(0, i, first=True)
            act_xT(0, first=True)
            act_step(0)
            act_step(1)
            more = act.value_load(blk_exp[0:1, MAX_BLK:MAX_BLK + 1], min_val=N_EXP - 3, max_val=MAX_BLK - 4)
            with act.Fori(0, more) as i:
                act_step(i + 2)
            act_step(more + 2, last=True)
            act_aT(more + 2)
            act_y(more + 2, 0)
            store_y(more + 2, ye_end)
            for t in range(NT):
                act.wait_ge(slot_y[t // 2], 64)
                A.activation(y_slot[2 * t][:, :], y_slot[2 * t][:, :], ACT.Copy, scale=wts[:, t:t + 1]).then_inc(f_act, 1)

        @block.vector
        def _(dve):
            dve.wait_ge(silu_e, 1)
            link_v(V.tensor_scalar(silu_t[:, :], silu_t[:, :], 1.0, None, ALU.add))
            link_v(V.reciprocal(silu_t[:, :], silu_t[:, :]))
            V.tensor_tensor(silu_c[:, :], col[:, C_C:C_C + KT], silu_t[:, :], ALU.mult).then_inc(col_ok, 1)
            V.tensor_scalar(qgain[:, :], col[:, C_QG:C_QG + 10], -(E ** -0.5), None, ALU.mult).then_inc(col_ok, 1)
            dve.wait_ge(small_ld, 16 * N_SMALL)
            V.memset(tab[32:33, :], 1.0).then_inc(bf_set, 1)
            V.tensor_copy(id_bf[:, :], ident).then_inc(bf_set, 1)
            V.tensor_copy(cm_bf[:, :], consts[:, K_CM:K_CM + P]).then_inc(bf_set, 1)
            dve.wait_ge(rel_pe, 1)
            V.tensor_copy(relrow[:, :, :], bank[0:4, 1:4, 0:384]).then_inc(rel_ev, 1)
            dve.wait_ge(rstd_ok, 1)
            for t in range(NT):
                V.tensor_scalar(xt[:, t, :], xt[:, t, :], rstd[:, t:t + 1], None, ALU.mult).then_inc(xn_ok, 1)
            dve.wait_ge(adaT_pe, 1)
            link_v(V.tensor_tensor(mod[:, :], bank[:, 3, 0:16], col[:, C_BADA:C_BADA + 16], ALU.add))
            V.scalar_tensor_tensor(out=scale1[:, :], in0=mod[:, 8:16], scalar=1.0, in1=col[:, C_N1:C_N1 + KT],
                                   op0=ALU.add, op1=ALU.mult).then_inc(scl_ok, 1)
            for n in range(2 * KT):
                f, half = n // 2, n % 2
                t = slice(half * HALF, (half + 1) * HALF)
                if n == 10:
                    dve_split(dve, 0)
                dve.wait_ge(xT_act, n + 1)
                V.tensor_copy(h_hi[:, f, t], h_tmp[n % 2][:, :]).then_inc(h_hi_ok, 1)
                dve.wait_ge(h_hi_ok, n + 1)
                V.tensor_tensor(h_lo[:, f, t], h_tmp[n % 2][:, :], h_hi[:, f, t].bitcast(F32),
                                ALU.subtract).then_inc(h_lo_ok, 1)
            dve.wait_ge(bias_ld, 16 * DIL_HEADS)
            vj = 0
            for j, (kind, _, _) in enumerate(jobs):
                if kind == "v":
                    dve_ada_bg(dve, j)
                    ev_values(dve, V.tensor_copy, j, vj, 1, v_ev_dve)
                    vj += 1
                    dve_split(dve, j + 1)
                    if j == J_FOX:
                        merge_dve(0)
                    if j == J_FOX + 1:
                        dve.wait_ge(v_ev_act, 20)
                        dve.wait_ge(v_ev_dve, 20)
                        link_v(V.tensor_tensor(fg[1][:, :, :], fg[0][:, :, :],
                                               bfr[:, :].unsqueeze(2).to_broadcast([P, FOX_HEADS, NT]), ALU.add))
                        V.scalar_tensor_tensor(out=fg[2][:, :, :], in0=fg[1][:, :, :], scalar=-1.0,
                                               in1=fg[1][:, :, :], op0=ALU.mult, op1=ALU.max).then_inc(fg_ok, 1)
                        dve.wait_ge(fg_act, 1)
                        V.scalar_tensor_tensor(out=fg[5][:, :, :], in0=fg[1][:, :, :], scalar=0.0, in1=fg[4][:, :, :],
                                               op0=ALU.min, op1=ALU.subtract).then_inc(fg_ok, 1)
                        dve.wait_ge(fg_ok, 2)
                        link_v(V.memset(fg[1][:, :, 0:1], 0.0))
                        dve.wait_ge(cum_pe, 1)
                        tot = bank[:, 4, 64:128].rearrange("p (h t) -> p h t", t=NT)
                        for t in range(1, NT):
                            link_v(V.tensor_tensor(fg[1][:, :, t:t + 1], fg[1][:, :, t - 1:t], tot[:, :, t - 1:t], ALU.add))
                        V.tensor_tensor(fg[2][:, :, :], bank[:, 4, 0:64].rearrange("p (h t) -> p h t", t=NT),
                                        fg[1][:, :, :], ALU.add).then_inc(cum_dve, 1)
                        merge_dve(1)
                else:
                    jp = (j // 3 * 2 + j % 3 - 1) if j < J_FOX else j - J_FOX - 2 + 6
                    dve_pair(dve, jp, j)
            dve_gates(0)
            with dve.Fori(0, KT - 1) as i:
                dve_gates(i + 1)
            for k in range(KT):
                if k in (3, 5):
                    ks = slice(0, 4) if k == 3 else slice(4, KT)
                    dve.wait_ge(o_hi_ok, 1 if k == 3 else 2)
                    V.tensor_tensor(o_lo[0][:, ks, :], o_raw[0][:, ks, :], o_hi[0][:, ks, :].bitcast(F32),
                                    ALU.subtract).then_inc(o_lo_ok, 1)
                dve.wait_ge(m_hi_ok, k + 1)
                V.tensor_tensor(m_lo[:, k, :], merged[:, k, :], m_hi[:, k, :].bitcast(F32), ALU.subtract).then_inc(m_lo_ok, 1)
            dve.wait_ge(m_lo_ok, KT)
            for cc in range(4):
                if cc < 3:
                    dve.wait_ge(o_hi_ok, cc + 3)
                    V.tensor_tensor(o_lo[(cc + 1) % 2][:, :, :], o_raw[(cc + 1) % 3][:, :, :],
                                    o_hi[(cc + 1) % 2][:, :, :].bitcast(F32), ALU.subtract).then_inc(o_lo_ok, 1)
                if cc == 0:
                    dve.wait_ge(gate_ld, 32)
                    dve.wait_ge(x2_ld, 16)
                c = slice(cc * OC, (cc + 1) * OC)
                for t in range(NT):
                    dve.wait_ge(o_pe, 8 * cc + t + 1)
                    link_v(V.tensor_tensor(o_tmp[:, t % 2, :], bank[:, t, (cc % 2) * OC:(cc % 2 + 1) * OC], gate_row[0][:, c], ALU.mult))
                    V.tensor_tensor(x2[:, t, c], x2[:, t, c], o_tmp[:, t % 2, :], ALU.add).then_inc(o_done, 1)
                    if cc == 3 and t:
                        dve_norm2(dve, t - 1)
            dve_norm2(dve, NT - 1)
            dve_route()
            dve.wait_ge(e_lo_ok, CHUNKS)
            dve_xT(0)
            dve_step(0)
            dve_step(1)
            more = dve.value_load(blk_exp[0:1, MAX_BLK:MAX_BLK + 1], min_val=N_EXP - 3, max_val=MAX_BLK - 4)
            with dve.Fori(0, more) as i:
                dve_step(i + 2)
            dve_step(more + 2, last=True)
            dve_aT(more + 2)
            dve_y(more + 2, 0)
            for t in range(NT):
                dve.wait_ge(f_act, t + 1)
                dve.wait_ge(slot_y[t // 2], 64)
                if t >= 4:
                    dve.wait_ge(f_pool, t - 3)
                V.scalar_tensor_tensor(out=y_sum[t % 4][:, :], in0=y_slot[2 * t + 1][:, :], scalar=wts[:, NT + t:NT + t + 1],
                                       in1=y_slot[2 * t][:, :], op0=ALU.mult, op1=ALU.add).then_inc(f_dve, 1)
                dve.wait_ge(f_dve, 2 * t + 1)
                V.tensor_tensor(y_sum[t % 4][:, :], y_sum[t % 4][:, :], gate_row[1][:, :], ALU.mult).then_inc(f_dve, 1)

        @block.tensor
        def _(pe):
            pe.wait_ge(rows_ld, 16 * N_ROWS_LD)
            nc.tensor.transpose(bank[:, 0, 0:N_ROWS], rows[0:N_ROWS, :], ident[0:N_ROWS, 0:N_ROWS]).then_inc(rowsT_pe, 1)
            pe.wait_ge(col_ok, 2)
            for n in range(ADA_FIRST):
                if n == 4:
                    pe.wait_ge(pool_set, 2)
                    pe.wait_ge(bf_set, 1)
                    pe.wait_ge(small_ld, 16 * N_SMALL)
                    for g in range(NG):
                        mm = nc.tensor.matmul(bank[0:4, 1 + g, 0:384], tab[0:33, 4 * g:4 * g + 4],
                                              ohs[0:33, g * 384:(g + 1) * 384], start=True, stop=True)
                    mm.then_inc(rel_pe, 1)
                pe.wait_ge(ada_ld[n % 4], 16 * (n // 4 + 1))
                if n >= 4:
                    pe.wait_ge(ada_ev, n - 3)
                for k in range(KT):
                    mm = nc.tensor.matmul(bank[0:1, 4 + n % 4, 0:256], silu_c[:, k:k + 1], ada_w[n % 4][:, k, :],
                                          start=(k == 0), stop=(k == KT - 1))
                mm.then_inc(ada_pe, 1)
            pe.wait_ge(ada_ev, ADA_FIRST)
            pe.wait_ge(rel_ev, 1)
            for i in range(2 * KT):
                mm = nc.tensor.matmul(bank[:, 3, i:i + 1], ada_row[:, i * P:(i + 1) * P], ones[0:1, 0:1],
                                      start=True, stop=True)
            mm.then_inc(adaT_pe, 1)
            pe.wait_ge(xn_ok, NT)
            pe.wait_ge(scl_ok, 1)
            for n in range(2 * KT):
                f, half = n // 2, n % 2
                if n >= 4:
                    pe.wait_ge(xT_act, n - 3)
                for t in range(4):
                    mm = nc.tensor.transpose(bank[:, n % 4, t * P:(t + 1) * P], xt[:, 4 * half + t, f * P:(f + 1) * P], ident)
                mm.then_inc(xT_pe, 1)
            pe.wait_ge(h_lo_ok, 2 * KT)
            pe.wait_ge(bf_set, 3)
            vj = 0
            for j, (kind, _, _) in enumerate(jobs):
                if kind == "v":
                    pe_values(pe, j, vj, j // 3 if j < J_FOX else -1)
                    vj += 1
                    if j == J_FOX + 1:
                        merge_turn(0)
                        pe.wait_ge(fg_ok, 2)
                        nc.tensor.matmul(bank[:, 4, 0:64], tri_incl, fg[5][:, :, :].rearrange("p h t -> p (h t)"),
                                         start=True, stop=True)
                        nc.tensor.matmul(bank[:, 4, 64:128], ones[:, :], fg[5][:, :, :].rearrange("p h t -> p (h t)"),
                                         start=True, stop=True).then_inc(cum_pe, 1)
                        pe.wait_ge(cum_dve, 1)
                        nc.tensor.transpose(bank[0:64, 4, P:2 * P], fg[2][:, :, :].rearrange("p h t -> p (h t)"),
                                            ident).then_inc(cumT_pe, 1)
                else:
                    jp = (j // 3 * 2 + j % 3 - 1) if j < J_FOX else j - J_FOX - 2 + 6
                    pe_pair(pe, jp, j)
            pe.wait_ge(min_ok, 160)
            pe.wait_ge(y_ok, 160)
            pe.wait_ge(yT_ok, 8)
            pe_gates(0)
            with pe.Fori(0, KT - 1) as i:
                pe_gates(i + 1)
            pe.wait_ge(merged_ok, 16)
            for k in range(KT):
                pe.wait_ge(o_lo_ok, 1 if k < 4 else 2)
                pe.wait_ge(m_lo_ok, k + 1)
                for t in range(NT):
                    mm = three(bank[:, t, 0:OC], (m_hi[:, k, t * P:(t + 1) * P], m_lo[:, k, t * P:(t + 1) * P]),
                               (o_hi[0][:, k, :], o_lo[0][:, k, :]), k == 0, k == KT - 1)
                    if k == KT - 1:
                        mm.then_inc(o_pe, 1)
            for cc in range(1, 4):
                pe.wait_ge(o_lo_ok, cc + 2)
                for t in range(NT):
                    pe.wait_ge(o_done, 8 * (cc - 1) + t + 1)
                    for k in range(KT):
                        mm = three(bank[:, t, (cc % 2) * OC:(cc % 2 + 1) * OC],
                                   (m_hi[:, k, t * P:(t + 1) * P], m_lo[:, k, t * P:(t + 1) * P]),
                                   (o_hi[cc % 2][:, k, :], o_lo[cc % 2][:, k, :]), k == 0, k == KT - 1)
                    mm.then_inc(o_pe, 1)
            for half in range(2):
                pe.wait_ge(xn2_ok, 4 * half + 4)
                for f in range(KT):
                    n = half * KT + f
                    if n < 4:
                        pe.wait_ge(o_done, 24 + n + 1)
                    else:
                        pe.wait_ge(h2_act, n - 3)
                    for t in range(4):
                        mm = nc.tensor.transpose(bank[:, n % 4, t * P:(t + 1) * P],
                                                 xn2[(4 * half + t) % XN][:, f * P:(f + 1) * P], ident)
                    mm.then_inc(h2_pe, 1)
                pe.wait_ge(h2_act, KT * (half + 1))
                pe.wait_ge(o_done, 32)
                pe.wait_ge(rt_ld, 32)
                for t in range(4 * half, 4 * half + 4):
                    for k in range(KT):
                        mm = nc.tensor.matmul(bank[:, 4, t * N_ROUTE:(t + 1) * N_ROUTE], h2T[:, k, t * P:(t + 1) * P],
                                              w_rt[:, k, :], start=(k == 0), stop=(k == KT - 1))
            mm.then_inc(rt_pe, 1)
            pe.wait_ge(r_d, 3)
            mask = r_mask[:, :, :].rearrange("p t e -> p (t e)")
            nc.tensor.matmul(bank[:, 5, 0:NT * N_EXP], tri_strict, mask, start=True, stop=True)
            nc.tensor.matmul(bank[:, 6, 0:NT * N_EXP], ones[:, :], mask, start=True, stop=True).then_inc(rank_pe, 1)
            pe.wait_ge(hot_ok, 1)
            for i in range(2 * NT):
                mm = nc.tensor.matmul(bank[:, 7, 0:MAX_BLK], hot_place[:, i, :], hot_blk[:, i // NT, i % NT, :],
                                      start=(i == 0), stop=(i == 2 * NT - 1))
            mm.then_inc(slot_pe, 1)
            pe_turn_x(0)
            pe_step(0)
            pe_step(1)
            more = pe.value_load(blk_exp[0:1, MAX_BLK:MAX_BLK + 1], min_val=N_EXP - 3, max_val=MAX_BLK - 4)
            with pe.Fori(0, more) as i:
                pe_step(i + 2)
            pe_step(more + 2, last=True)
            pe_turn_act(more + 2)
            pe_down(more + 2, 0)


def bucket_rows():
    import numpy as np

    half, far = 16, 2048
    hot = np.zeros((33, NG, 384), np.float32)
    for g, dil in enumerate(DILATION):
        for n in range(384):
            m = 255 - n
            if g == 2:
                m = m / 2 if m % 2 == 0 else -1
            if m < 0 or m > P:
                hot[32, g, n] = BIG
                continue
            dist = int(m * dil)
            if dist < half:
                b = dist
            else:
                big = np.log(np.float32(dist) / half) / np.log(far / half) * half
                b = min(half + int(np.float32(big)), 2 * half - 1)
            hot[b, g, n] = -1.0
    return hot.reshape(33, NG * 384)


def shape_constants():
    import numpy as np

    k = np.zeros((P, K_COLS), np.float32)
    i = np.arange(P)
    k[:, K_ID:K_ID + P] = np.eye(P)
    k[:, K_CM:K_CM + P] = np.where(i[None, :] > i[:, None], BIG, 0.0)
    k[:, K_BO:K_BO + P] = (i[None, :] // E == i[:, None] // E)
    k[:, K_TI:K_TI + P] = (i[:, None] <= i[None, :])
    k[:, K_TS:K_TS + P] = (i[:, None] < i[None, :])
    r = k[:, K_ROW:]
    r[:, R_PRI4:R_PRI4 + 4] = np.arange(4, 0, -1)
    r[:, R_PRI8:R_PRI8 + 8] = np.arange(8, 0, -1)
    r[:, R_IOTA:R_IOTA + P] = i
    r[:, R_TOK:R_TOK + NT] = i[:, None] + P * np.arange(NT)
    return k


NAMES = ["x", "c", "rel_bias_table", "w_ada", "b_ada", "norm1_g", "w_in", "b_forget", "q_gain", "k_gain",
         "w_branch_a", "w_branch_b", "w_out", "norm2_g", "w_router_group", "b_router_group",
         "w_router_expert", "b_router_expert", "w1", "w3", "w2"]


def kernel(**inputs):
    import numpy as np
    import concourse.bacc as bacc
    from concourse.bass_utils import run_bass_kernel_spmd

    nc = bacc.Bacc("TRN2", target_bir_lowering=False, num_devices=1)
    arrays, args = {}, []
    for name in NAMES:
        a = np.ascontiguousarray(inputs[name])
        arrays[f"in_{name}"] = a.reshape(a.shape[1:]) if name != "rel_bias_table" else a
    arrays["shape_constants"] = shape_constants()
    arrays["bucket_rows"] = bucket_rows()
    for name, a in arrays.items():
        args.append(nc.dram_tensor(name, a.shape, mybir.dt.from_np(a.dtype), kind="ExternalInput").ap())
    args.append(nc.dram_tensor("out", (T, D), F32, kind="ExternalOutput").ap())
    build(nc, *args)
    r = run_bass_kernel_spmd(nc, [arrays], core_ids=[0])
    return np.asarray(r.results[0]["out"]).reshape(1, T, D)
```
